# Optimizing a Trainium2 kernel written in Bass

```python
import jax, jax.numpy as jnp
from jax import lax
import numpy as np

D_MODEL = 1024
BATCH = 1
SEQ = 256
DEPTH = 2

N_A = DEPTH // 2
N_B = DEPTH - N_A
N_DENSE = (DEPTH + 1) // 2
N_MOE = DEPTH // 2

HEAD_DIM = 128
N_HEADS_A = D_MODEL // HEAD_DIM
N_KV_HEADS_A = 2
GROUP_A = N_HEADS_A // N_KV_HEADS_A
N_IDX_HEADS = 8
IDX_DIM = 64
MAX_TOPK = 256
N_HEADS_B = D_MODEL // HEAD_DIM

ROPE_THETA = 500000.0
ROT_FRAC = 4
Q_BLOCK = 128
NORM_EPS = 1e-6

D_FF = 2816
N_EXPERTS = 8
TOP_K_EXPERTS = 2

A_Q = N_HEADS_A * HEAD_DIM
A_K = N_KV_HEADS_A * HEAD_DIM
A_V = N_KV_HEADS_A * HEAD_DIM
A_QI = N_IDX_HEADS * IDX_DIM
A_KI = IDX_DIM
A_WI = N_IDX_HEADS
A_IN = A_Q + A_K + A_V + A_QI + A_KI + A_WI
A_SPLITS = (A_Q, A_Q + A_K, A_Q + A_K + A_V, A_Q + A_K + A_V + A_QI, A_Q + A_K + A_V + A_QI + A_KI)
KV_B = 2 * N_HEADS_B * HEAD_DIM

kernel_name = "yoco_dsa_stickbreaking_moe_block"

def rms_norm(x, w):
    xf = x.astype(jnp.float32)
    y = xf * lax.rsqrt(jnp.mean(xf * xf, axis=-1, keepdims=True) + NORM_EPS)
    return (y * w.astype(jnp.float32)).astype(x.dtype)

def partial_rope(x, pos):
    d = x.shape[-1]
    r = d // ROT_FRAC
    half = r // 2
    inv = ROPE_THETA ** (-jnp.arange(half, dtype=jnp.float32) * 2.0 / r)
    ang = pos.astype(jnp.float32)[:, None] * inv[None, :]
    shape = (1, pos.shape[0]) + (1,) * (x.ndim - 3) + (half,)
    cos = jnp.cos(ang).reshape(shape).astype(x.dtype)
    sin = jnp.sin(ang).reshape(shape).astype(x.dtype)
    x1, x2, rest = x[..., :half], x[..., half:r], x[..., r:]
    return jnp.concatenate([x1 * cos - x2 * sin, x2 * cos + x1 * sin, rest], axis=-1)

def swiglu(u, w_gate_up, w_down):
    g, up = jnp.split(u @ w_gate_up, 2, axis=-1)
    return (jax.nn.silu(g) * up) @ w_down

def dsa_attention(h, norm_w, w_in, q_norm_w, k_norm_w, w_out):
    B, S, _ = h.shape
    topk = min(MAX_TOPK, S // 4)
    pos = jnp.arange(S)
    u = rms_norm(h, norm_w)
    q, k, v, qi, ki, wi = jnp.split(u @ w_in, A_SPLITS, axis=-1)
    q = q.reshape(B, S, N_KV_HEADS_A, GROUP_A, HEAD_DIM)
    k = k.reshape(B, S, N_KV_HEADS_A, HEAD_DIM)
    v = v.reshape(B, S, N_KV_HEADS_A, HEAD_DIM)
    q = partial_rope(rms_norm(q, q_norm_w), pos)
    k = partial_rope(rms_norm(k, k_norm_w), pos)
    qi = partial_rope(qi.reshape(B, S, N_IDX_HEADS, IDX_DIM), pos)
    ki = partial_rope(ki[:, :, None, :], pos)[:, :, 0, :]
    wi = wi * (N_IDX_HEADS ** -0.5)
    s_idx = jnp.arange(S)
    scale = HEAD_DIM ** -0.5
    gather = jax.vmap(lambda kb, ib: kb[ib])

    def block(i):
        start = i * Q_BLOCK
        t = start + jnp.arange(Q_BLOCK)
        qb = lax.dynamic_slice_in_dim(q, start, Q_BLOCK, axis=1)
        qib = lax.dynamic_slice_in_dim(qi, start, Q_BLOCK, axis=1)
        wib = lax.dynamic_slice_in_dim(wi, start, Q_BLOCK, axis=1)
        causal = s_idx[None, :] <= t[:, None]
        rel = jax.nn.relu(jnp.einsum('bqhd,bsd->bqhs', qib, ki).astype(jnp.float32) * (IDX_DIM ** -0.5))
        score = jnp.einsum('bqhs,bqh->bqs', rel, wib.astype(jnp.float32))
        score = jnp.where(causal[None], score, -jnp.inf)
        _, sel = lax.top_k(score, topk)
        sel_valid = sel <= t[None, :, None]
        k_sel = gather(k, sel)
        v_sel = gather(v, sel)
        logits = jnp.einsum('bqhgd,bqkhd->bqhgk', qb, k_sel).astype(jnp.float32) * scale
        logits = jnp.where(sel_valid[:, :, None, None, :], logits, -jnp.inf)
        p = jax.nn.softmax(logits, axis=-1).astype(v.dtype)
        o = jnp.einsum('bqhgk,bqkhd->bqhgd', p, v_sel)
        return o.reshape(B, Q_BLOCK, A_Q)

    o = lax.map(block, jnp.arange(S // Q_BLOCK))
    o = jnp.transpose(o, (1, 0, 2, 3)).reshape(B, S, A_Q)
    return o @ w_out

def stick_breaking_attention(h, norm_w, w_q, w_out, k_sb, v_sb):
    B, S, _ = h.shape
    u = rms_norm(h, norm_w)
    q = (u @ w_q).reshape(B, S, N_HEADS_B, HEAD_DIM)
    s_idx = jnp.arange(S)
    scale = HEAD_DIM ** -0.5

    def block(i):
        start = i * Q_BLOCK
        t = start + jnp.arange(Q_BLOCK)
        qb = lax.dynamic_slice_in_dim(q, start, Q_BLOCK, axis=1)
        strict = (s_idx[None, :] < t[:, None])[None, None]
        z = jnp.einsum('bqhd,bshd->bhqs', qb, k_sb).astype(jnp.float32) * scale
        log_beta = jax.nn.log_sigmoid(z)
        log_keep = jnp.where(strict, jax.nn.log_sigmoid(-z), 0.0)
        after = lax.cumsum(log_keep, axis=3, reverse=True) - log_keep
        a = jnp.where(strict, jnp.exp(log_beta + after), 0.0)
        o = jnp.einsum('bhqs,bshd->bqhd', a.astype(v_sb.dtype), v_sb)
        return o.reshape(B, Q_BLOCK, N_HEADS_B * HEAD_DIM)

    o = lax.map(block, jnp.arange(S // Q_BLOCK))
    o = jnp.transpose(o, (1, 0, 2, 3)).reshape(B, S, N_HEADS_B * HEAD_DIM)
    return o @ w_out

def moe_ffn(u, router_w, w_gate_up, w_down):
    B, S, D = u.shape
    tok = u.reshape(B * S, D)
    logits = (tok @ router_w).astype(jnp.float32)
    top_vals, top_idx = lax.top_k(logits, TOP_K_EXPERTS)
    gates = jax.nn.softmax(top_vals, axis=-1)
    dense_gates = jnp.sum(jax.nn.one_hot(top_idx, N_EXPERTS, dtype=jnp.float32) * gates[..., None], axis=1)
    y = jnp.zeros_like(tok)
    for e in range(N_EXPERTS):
        y = y + dense_gates[:, e:e + 1].astype(tok.dtype) * swiglu(tok, w_gate_up[e], w_down[e])
    return y.reshape(B, S, D)

def setup_inputs(seed: int = 0) -> dict:
    key = jax.random.key(seed)
    ks = iter(jax.random.split(key, 32))

    def w(shape, fan_in):
        return jax.random.normal(next(ks), shape, jnp.float32) * (fan_in ** -0.5)

    def gain(shape):
        return 1.0 + 0.02 * jax.random.normal(next(ks), shape, jnp.float32)

    return {
        "x": jax.random.normal(next(ks), (BATCH, SEQ, D_MODEL), jnp.float32),
        "a_norm_w": gain((N_A, D_MODEL)),
        "a_w_in": w((N_A, D_MODEL, A_IN), D_MODEL),
        "a_q_norm_w": gain((N_A, HEAD_DIM)),
        "a_k_norm_w": gain((N_A, HEAD_DIM)),
        "a_w_out": w((N_A, A_Q, D_MODEL), A_Q),
        "kv_norm_w": gain((D_MODEL,)),
        "kv_w": w((D_MODEL, KV_B), D_MODEL),
        "b_norm_w": gain((N_B, D_MODEL)),
        "b_w_q": w((N_B, D_MODEL, N_HEADS_B * HEAD_DIM), D_MODEL),
        "b_w_out": w((N_B, N_HEADS_B * HEAD_DIM, D_MODEL), N_HEADS_B * HEAD_DIM),
        "ffn_norm_w": gain((DEPTH, D_MODEL)),
        "dense_w_gate_up": w((N_DENSE, D_MODEL, 2 * D_FF), D_MODEL),
        "dense_w_down": w((N_DENSE, D_FF, D_MODEL), D_FF),
        "moe_router_w": w((N_MOE, D_MODEL, N_EXPERTS), D_MODEL),
        "moe_w_gate_up": w((N_MOE, N_EXPERTS, D_MODEL, 2 * D_FF), D_MODEL),
        "moe_w_down": w((N_MOE, N_EXPERTS, D_FF, D_MODEL), D_FF),
    }

def reference(x, a_norm_w, a_w_in, a_q_norm_w, a_k_norm_w, a_w_out, kv_norm_w, kv_w,
              b_norm_w, b_w_q, b_w_out, ffn_norm_w, dense_w_gate_up, dense_w_down,
              moe_router_w, moe_w_gate_up, moe_w_down):
    B, S, _ = x.shape
    h = x
    k_sb = v_sb = None
    for l in range(DEPTH):
        if l < N_A:
            h = h + dsa_attention(h, a_norm_w[l], a_w_in[l], a_q_norm_w[l], a_k_norm_w[l], a_w_out[l])
        else:
            j = l - N_A
            h = h + stick_breaking_attention(h, b_norm_w[j], b_w_q[j], b_w_out[j], k_sb, v_sb)
        u = rms_norm(h, ffn_norm_w[l])
        if l % 2 == 0:
            h = h + swiglu(u, dense_w_gate_up[l // 2], dense_w_down[l // 2])
        else:
            m = l // 2
            h = h + moe_ffn(u, moe_router_w[m], moe_w_gate_up[m], moe_w_down[m])
        if l == N_A - 1:
            kv = rms_norm(h, kv_norm_w) @ kv_w
            k_sb, v_sb = jnp.split(kv, 2, axis=-1)
            k_sb = k_sb.reshape(B, S, N_HEADS_B, HEAD_DIM)
            v_sb = v_sb.reshape(B, S, N_HEADS_B, HEAD_DIM)
    return h


_drawn_inputs = setup_inputs


def setup_inputs(seed=0):
    import zlib

    import numpy as np

    out = dict(_drawn_inputs(seed))
    spreads = {}
    factors = {'a_q_norm_w': 3.475, 'a_k_norm_w': 3.697, 'kv_norm_w': 2.736, 'b_norm_w': 3.362}
    for name, (base, spread) in spreads.items():
        noise = np.random.default_rng([zlib.crc32(name.encode()), seed]).standard_normal(out[name].shape)
        drawn = base * np.exp(spread * noise) if base else spread * noise
        out[name] = __import__('jax').numpy.asarray(drawn.astype(out[name].dtype))
    for name, factor in factors.items():
        out[name] = (out[name] * factor).astype(out[name].dtype)
    return out
```

```python
import concourse.bass as bass
from concourse import mybir
from concourse.alu_op_type import AluOpType as ALU
from contextlib import ExitStack

P = 128
TOK = 256
NT = TOK // P
DM = 1024
KD = DM // P
HD = 128
NH = 8
NKV = 2
GROUP = NH // NKV
IH, ID = 8, 64
A_IN = 2120
C_K, C_V, C_QI, C_KI, C_WI = 1024, 1280, 1536, 2048, 2112
TOPK = 64
F = 2816
FSTEP = 256
STEPS = F // FSTEP
NEXP = 8
SLOTS = 96
CHUNKS = -(-TOK // SLOTS)
JOBS = NEXP * CHUNKS
RING = 6
EPS = 1e-6
SCALE = HD ** -0.5
NOT_CAUSAL = -1.0e38
TAKEN = -2.0e38
MASKED = -1.0e30
NO_SLOT = -1.0e4

K_ID, K_BEFORE, K_AFTER, K_ONES, K_IMASK, K_SLOT, K_COS, K_SIN = 0, 128, 256, 384, 512, 768, 864, 896
K_END = 928

NORM_A, NORM_F0, NORM_KV, NORM_B, NORM_F1 = range(5)

T_IN, T_OUT, T_DENSE = 0, 5, 7
T_BK, T_BQ, T_BV, T_BO = T_DENSE + STEPS, T_DENSE + STEPS + 2, T_DENSE + STEPS + 4, T_DENSE + STEPS + 6
T_MOE = T_BO + 2
IN_COLS = [(C_QI, 512), (C_KI, 72), (C_K, 512), (0, 512), (512, 512)]


def program(nc, x, a_norm_w, a_w_in, a_q_norm_w, a_k_norm_w, a_w_out, kv_norm_w, kv_w, b_norm_w,
            b_w_q, b_w_out, ffn_norm_w, dense_w_gate_up, dense_w_down, moe_router_w,
            moe_w_gate_up, moe_w_down, consts, out):
    f32, i32 = mybir.dt.float32, mybir.dt.int32
    ACT = mybir.ActivationFunctionType
    AX = mybir.AxisListType
    ctx = ExitStack()
    with ctx:
        def sb(name, shape, dt=f32):
            return ctx.enter_context(nc.sbuf_tensor(name, shape, dt))

        def sem(name):
            return ctx.enter_context(nc.semaphore(name))

        up_ring = sb("up_ring", [P, RING, 4096])
        dn_ring = sb("dn_ring", [P, RING, 2048])
        cst = sb("cst", [P, K_END])
        h = sb("h", [P, NT, DM])
        u = sb("u", [P, NT, DM])
        uT = sb("uT", [P, KD, TOK])
        uT_b = sb("uT_b", [P, KD, TOK])
        work = sb("work", [P, NT * A_IN])
        kT_a = sb("kT_a", [P, NKV, TOK])
        norm_rows = sb("norm_rows", [5 * KD, P])
        nw = sb("nw", [P, 5 * KD])
        qk_w = sb("qk_w", [P, 2, HD])
        router = sb("router", [P, KD, NEXP])
        stat = sb("stat", [P, 16])
        qk_ss = sb("qk_ss", [P, 3, NT, GROUP])
        qk_rs = sb("qk_rs", [P, 3, NT, GROUP])
        w_idx = sb("w_idx", [P, NT, IH])
        top8 = sb("top8", [P, NT, 8])
        soft = sb("soft", [P, 3, NT * NH])
        rt = sb("rt", [P, 10, NT, NEXP])
        slot_of = sb("slot_of", [P, NT, JOBS + 1])
        gate_of = sb("gate_of", [P, NT, JOBS + 1])
        n_jobs = sb("n_jobs", [P, 1], i32)

        ident, before, after = cst[:, K_ID:K_ID + P], cst[:, K_BEFORE:K_BEFORE + P], cst[:, K_AFTER:K_AFTER + P]
        ones, imask = cst[:, K_ONES:K_ONES + P], cst[:, K_IMASK:K_IMASK + 2 * P]
        slot_no = cst[:, K_SLOT:K_SLOT + SLOTS]
        cos = cst[:, K_COS:K_COS + 32].rearrange("p (t f) -> p t f", t=NT)
        sin = cst[:, K_SIN:K_SIN + 32].rearrange("p (t f) -> p t f", t=NT)

        proj = work[:, :].rearrange("p (t c) -> p t c", t=NT)
        qT_a = uT_b
        scratch = dn_ring[:, :, :].rearrange("p s c -> p (s c)")
        at = [0]

        def take(n):
            at[0] += n
            assert at[0] <= RING * 2048
            return scratch[:, at[0] - n:at[0]]

        rel0 = take(1024).rearrange("p (h s) -> p h s", h=IH)
        rel1 = take(2048).rearrange("p (h s) -> p h s", h=IH)
        prob0 = take(1024).rearrange("p (h s) -> p h s", h=NH)
        prob1 = take(2048).rearrange("p (h s) -> p h s", h=NH)
        probT = take(3072).rearrange("p (h c) -> p h c", h=NH)
        sq = probT.rearrange("p h c -> p (h c)")[:, 0:1024].rearrange("p (t c) -> p t c", t=NT)
        qiT = take(1024).rearrange("p (j t) -> p j t", j=IH // 2)
        kiT = take(256)
        ki2 = take(256).rearrange("p (t c) -> p t c", t=NT)
        score = [take(128), take(256)]
        bias = [take(128), take(256)]
        at[0] = 0
        qT_b = take(2048).rearrange("p (h t) -> p h t", h=NH)
        kT_b = take(2048).rearrange("p (h t) -> p h t", h=NH)
        v_b = take(2048).rearrange("p (t c) -> p t c", t=NT)
        att = take(3072).rearrange("p (h c) -> p h c", h=NH)
        absz = [take(384), take(384)]
        lb = [take(384), take(384)]
        lk = [work[:, 384 * j:384 * j + 384] for j in range(2)]
        neg = [work[:, 768 + 384 * j:1152 + 384 * j] for j in range(2)]
        d_silu = work[:, 0:1024].rearrange("p (b f c) -> p b f c", b=2, f=2)
        d_h = work[:, 1024:2048].rearrange("p (b f c) -> p b f c", b=2, f=2)
        m_u = work[:, 0:768].rearrange("p (k c) -> p k c", k=KD)
        m_silu = work[:, 768:1152].rearrange("p (b f c) -> p b f c", b=2, f=2)
        m_h = work[:, 1152:1536].rearrange("p (b f c) -> p b f c", b=2, f=2)
        m_yT = work[:, 1536:2304].rearrange("p (k c) -> p k c", k=KD)
        m_y = work[0:SLOTS, 2304:3328]
        m_pick = work[:, 3328:3520].rearrange("p (t c) -> p t c", t=NT)
        m_pickT = work[0:SLOTS, 3520:3776]

        pair = [ctx.enter_context(nc.psum_tensor(f"pair{i}", [P, 1024], f32)) for i in range(4)]
        bank = [pair[i // 2][:, 512 * (i % 2):512 * (i % 2) + 512] for i in range(8)]

        consts_in, x_in, rows_in, qkw_in, router_in = (sem(n) for n in
            ("consts_in", "x_in", "rows_in", "qkw_in", "router_in"))
        up_in = [sem(f"up_in{s}") for s in range(RING)]
        dn_in = [sem(f"dn_in{s}") for s in range(RING)]
        up_used, dn_used = sem("up_used"), sem("dn_used")
        nw_ps, nw_done = sem("nw_ps"), sem("nw_done")
        h_done = sem("h_done")
        sumsq, ms_done, root_done, u_done = sem("sumsq"), sem("ms_done"), sem("root_done"), sem("u_done")
        uT_ps, uT_act, uT_dve = sem("uT_ps"), sem("uT_act"), sem("uT_dve")
        proj_ps, proj_sb = sem("proj_ps"), sem("proj_sb")
        idx_roped, idx_T, idx_T_sb = sem("idx_roped"), sem("idx_T"), sem("idx_T_sb")
        idx_qk, rel_done = sem("idx_qk"), sem("rel_done")
        qk_sq, qk_ms, qk_root, qk_roped = sem("qk_sq"), sem("qk_ms"), sem("qk_root"), sem("qk_roped")
        qk_T, qk_T_sb = sem("qk_T"), sem("qk_T_sb")
        logits_ps, rowmax_done, exp_done, prob_done = sem("logits_ps"), sem("rowmax_done"), sem("exp_done"), sem("prob_done")
        probT_ps, probT_sb = sem("probT_ps"), sem("probT_sb")
        o_ps, o_sb = sem("o_ps"), sem("o_sb")
        res_ps = sem("res_ps")
        dve_chain = sem("dve_chain")
        silu_done, hid_done = sem("silu_done"), sem("hid_done")
        bk_sb, bq_sb = sem("bk_sb"), sem("bq_sb")
        z_ps, z_log, keep_raw, keep_done = sem("z_ps"), sem("z_log"), sem("keep_raw"), sem("keep_done")
        after_ps, expo_done, stick_raw, stick_done = sem("after_ps"), sem("expo_done"), sem("stick_raw"), sem("stick_done")
        v_ps, v_sb = sem("v_ps"), sem("v_sb")
        route_ps, route_top, route_exp, sel_done = sem("route_ps"), sem("route_top"), sem("route_exp"), sem("sel_done")
        rank_ps, jobs_known = sem("rank_ps"), sem("jobs_known")
        e_silu, e_hid = sem("e_silu"), sem("e_hid")
        e_yT_act, e_yT_dve = sem("e_yT_act"), sem("e_yT_dve")
        e_y, e_y_act, e_y_dve = sem("e_y"), sem("e_y_act"), sem("e_y_dve")
        e_pick, e_pickT, e_pickT_sb = sem("e_pick"), sem("e_pickT"), sem("e_pickT_sb")
        e_gather, e_u_act, e_u_dve = sem("e_gather"), sem("e_u_act"), sem("e_u_dve")
        e_scatter, e_added, out_done = sem("e_scatter"), sem("e_added"), sem("out_done")

        block = ctx.enter_context(nc.Block())

        def up_tile(n, cols=512):
            return up_ring[:, n % RING, 0:KD * cols].rearrange("p (k c) -> p k c", k=KD)

        def ffn_up(s):
            return up_ring[:, s, :].rearrange("p (k g c) -> p k g c", k=KD, g=2)

        def ffn_dn(s):
            return dn_ring[:, s, :].rearrange("p (b n) -> p b n", b=2)

        def up_arrived(n):
            return 16 * sum(2 if T_DENSE <= m < T_DENSE + STEPS else 1 for m in range(n % RING, n + 1, RING))

        def dn_arrived(n):
            return 16 * (n // RING + 1)

        def job_arrived(first, i, k, before_jobs, transfers):
            slot = [(first + j) % RING for j in range(STEPS)]
            return k * (16 * transfers * slot.count(slot[i])) + (before_jobs + 16 * transfers * slot[:i + 1].count(slot[i]))

        def job_up_arrived(i, k):
            last = max(n for n in range(T_MOE) if n % RING == (T_MOE + i) % RING)
            return job_arrived(T_MOE, i, k, up_arrived(last), 2)

        def job_dn_arrived(i, k):
            last = max(n for n in range(STEPS) if n % RING == (STEPS + i) % RING)
            return job_arrived(STEPS, i, k, dn_arrived(last), 1)

        def job_free(first, i, k):
            last_user = i - RING if i >= RING else max(range(i, STEPS, RING)) - STEPS
            return k * STEPS + (first + last_user + 1)

        AHEAD = 4

        @block.sync
        def _(sp):
            sp.dma_start(h[:, :, :], x[0].rearrange("(t p) d -> p t d", p=P)).then_inc(x_in, 16)

            def columns(n, w, c0, cols=512):
                if n >= RING:
                    sp.wait_ge(up_used, n - RING + 1)
                sp.dma_start(up_tile(n, cols), w.rearrange("(k p) c -> p k c", p=P)[:, :, c0:c0 + cols])\
                  .then_inc(up_in[n % RING], 16)

            for j, (c, cols) in enumerate(IN_COLS):
                columns(T_IN + j, a_w_in[0], c, cols)
            for j in range(2):
                columns(T_OUT + j, a_w_out[0], 512 * j)

            dup = dense_w_gate_up[0].rearrange("(k p) (g c) -> p k g c", p=P, g=2)
            ddn = dense_w_down[0].rearrange("(b p) n -> p b n", p=P)
            for i in range(STEPS + AHEAD):
                if i < STEPS:
                    n = T_DENSE + i
                    sp.wait_ge(up_used, n - RING + 1)
                    for g in range(2):
                        sp.dma_start(ffn_up(n % RING)[:, :, g, :], dup[:, :, g, FSTEP * i:FSTEP * (i + 1)])\
                          .then_inc(up_in[n % RING], 16)
                m = i - AHEAD
                if m == 0:
                    sp.wait_ge(o_ps, 2)
                if m >= RING:
                    sp.wait_ge(dn_used, m - RING + 1)
                if m >= 0:
                    sp.dma_start(ffn_dn(m % RING), ddn[:, 2 * m:2 * m + 2, :]).then_inc(dn_in[m % RING], 16)

            for first, w, c0 in ((T_BK, kv_w, 0), (T_BQ, b_w_q[0], 0), (T_BV, kv_w, DM), (T_BO, b_w_out[0], 0)):
                for j in range(2):
                    columns(first + j, w, c0 + 512 * j)

            eup = moe_w_gate_up[0].rearrange("e (k p) (g c) -> e p k g c", p=P, g=2)
            edn = moe_w_down[0].rearrange("e (b p) n -> e p b n", p=P)

            def expert_up(i, e):
                s = (T_MOE + i) % RING
                for g in range(2):
                    src = eup[bass.ds(e, 1), :, :, g, FSTEP * i:FSTEP * (i + 1)]
                    sp.dma_start(ffn_up(s)[:, :, g, :], src.rearrange("e p k c -> (e p) k c")).then_inc(up_in[s], 16)

            def expert_dn(i, e):
                s = (STEPS + i) % RING
                sp.dma_start(ffn_dn(s), edn[bass.ds(e, 1), :, 2 * i:2 * i + 2, :].rearrange("e p b n -> (e p) b n")).then_inc(dn_in[s], 16)

            for i in range(STEPS + AHEAD):
                if i < STEPS:
                    sp.wait_ge(up_used, T_MOE + i - RING + 1)
                    expert_up(i, 0)
                m = i - AHEAD
                if m == 0:
                    sp.wait_ge(dn_used, STEPS)
                    sp.wait_ge(o_ps, 4)
                if m >= RING:
                    sp.wait_ge(dn_used, STEPS + m - RING + 1)
                if m >= 0:
                    expert_dn(m, 0)

            def job_weights(k, e):
                for i in range(STEPS):
                    sp.wait_ge(up_used, job_free(T_MOE, i, k))
                    expert_up(i, e)
                    sp.wait_ge(dn_used, job_free(STEPS, i, k))
                    expert_dn(i, e)

            with sp.Fori(1, NEXP) as k:
                job_weights(k, k)
            sp.wait_ge(jobs_known, 1)
            jobs = sp.value_load(n_jobs[0:1, 0:1], min_val=NEXP, max_val=JOBS)
            with sp.If(jobs > NEXP):
                for c in range(1, CHUNKS):
                    with sp.Fori(0, NEXP) as e:
                        job_weights(e + c * NEXP, e)
            for t in range(NT):
                sp.wait_ge(e_added, jobs * NT + (t + 2))
                sp.dma_start(out[0, P * t:P * t + P, :], h[:, t, :]).then_inc(out_done, 16)
            sp.wait_ge(out_done, 16 * NT)

        @block.tensor
        def _(pe):
            def uT_blocks(n):
                for t in range(NT):
                    pe.wait_ge(u_done, NT * n + t + 1)
                    for k in range(KD):
                        c = 256 * (k % 2) + P * t
                        mm = pe.transpose(bank[4 + k // 2][:, c:c + P], u[:, t, P * k:P * k + P], ident)
                        if t == NT - 1 and k % 2 == 1:
                            mm.then_inc(uT_ps, 1)

            def token_columns(n, t, ps, lhs, cols=512):
                for k in range(KD):
                    mm = pe.matmul(ps[:, 0:cols], lhs[:, k, P * t:P * t + P], up_tile(n, cols)[:, k, :],
                                   start=(k == 0), stop=(k == KD - 1))
                return mm

            def residual_product(n0, lhs, first_bank):
                for half in range(2):
                    n = n0 + half
                    pe.wait_ge(up_in[n % RING], up_arrived(n))
                    for t in range(NT):
                        mm = token_columns(n, t, bank[first_bank + 2 * t + half], lhs)
                        mm.then_inc(res_ps if t == 0 else up_used, 1)

            pe.wait_ge(consts_in, 16)
            pe.wait_ge(rows_in, 16 * 5)
            pe.transpose(bank[0][:, 0:5 * KD], norm_rows[:, :], ident[0:5 * KD, 0:5 * KD]).then_inc(nw_ps, 1)

            uT_blocks(0)

            def project(j):
                n, cols = T_IN + j, IN_COLS[j][1]
                pe.wait_ge(up_in[n % RING], up_arrived(n))
                for t in range(NT):
                    use = NT * j + t
                    if j == 0 and t == 0:
                        pe.wait_ge(nw_done, 1)
                        pe.wait_ge(uT_act, 2)
                        pe.wait_ge(uT_dve, 2)
                    if use >= 4:
                        pe.wait_ge(proj_sb, use - 3)
                    token_columns(n, t, bank[use % 4], uT, cols).then_inc(proj_ps if t == 0 else up_used, 1)

            project(0)
            project(1)
            project(2)
            pe.wait_ge(idx_roped, 1)
            for j in range(IH // 2):
                for t in range(NT):
                    c = 256 * (j % 2) + P * t
                    pe.transpose(bank[4 + j // 2][:, c:c + P], proj[:, t, C_QI + P * j:C_QI + P * j + P], ident)
            for t in range(NT):
                mm = pe.transpose(bank[6][:, P * t:P * t + P], ki2[:, t, :], ident)
            mm.then_inc(idx_T, 1)
            project(3)

            def index_scores(t, heads, first_bank):
                keys = P * (t + 1)
                for n, i in enumerate(heads):
                    part = slice(ID * (i % 2), ID * (i % 2) + ID)
                    c = (n // 2) * keys
                    mm = pe.matmul(bank[first_bank + i % 2][:, c:c + keys], qiT[part, i // 2, P * t:P * t + P],
                                   kiT[part, 0:keys], start=True, stop=True)
                mm.then_inc(idx_qk, 1)

            pe.wait_ge(idx_T_sb, 3)
            index_scores(0, range(8), 4)
            index_scores(1, range(4), 6)
            pe.wait_ge(rel_done, 2)
            index_scores(1, range(4, 8), 4)
            project(4)

            for n, ps in enumerate((bank[4], bank[5], bank[6], bank[7], bank[0])):
                if n == 0:
                    pe.wait_ge(rel_done, 6)
                if n == 4:
                    pe.wait_ge(proj_sb, 9)
                pe.wait_ge(qk_roped, (1, 2, 2, 3, 3)[n])
                c0 = C_K if n == 0 else 2 * HD * (n - 1)
                for i in range(2):
                    for t in range(NT):
                        mm = pe.transpose(ps[:, 256 * i + P * t:256 * i + P * t + P],
                                          proj[:, t, c0 + HD * i:c0 + HD * i + HD], ident)
                mm.then_inc(qk_T, 1)

            pe.wait_ge(qk_T_sb, 5)
            pe.wait_ge(proj_sb, 10)
            for i in range(NH):
                mm = pe.matmul(pair[1][:, P * i:P * i + P], qT_a[:, i, 0:P], kT_a[:, i // GROUP, 0:P],
                               start=True, stop=True)
            mm.then_inc(logits_ps, 1)
            for i in range(NH):
                mm = pe.matmul(pair[2 + i // 4][:, TOK * (i % 4):TOK * (i % 4) + TOK], qT_a[:, i, P:TOK],
                               kT_a[:, i // GROUP, :], start=True, stop=True)
                if i % 4 == 3:
                    mm.then_inc(logits_ps, 1)
            for g in range(3):
                pe.wait_ge(prob_done, g + 1)
                for i in range(8):
                    src = prob0[:, i, :] if g == 0 else prob1[:, 4 * (g - 1) + i // 2, P * (i % 2):P * (i % 2) + P]
                    mm = pe.transpose(pair[g][:, P * i:P * i + P], src, ident)
                mm.then_inc(probT_ps, 1)

            def weighted_values(weightsT, value, pairs):
                for i in range(NH):
                    ps = pair[pairs[i // 4]][:, TOK * (i % 4):TOK * (i % 4) + TOK]
                    pe.matmul(ps, value(0, i), weightsT[:, i, 0:TOK], start=True, stop=False)
                    mm = pe.matmul(ps[:, P:TOK], value(1, i), weightsT[:, i, TOK:TOK + P], start=False, stop=True)
                    if i % 4 == 3:
                        mm.then_inc(o_ps, 1)

            pe.wait_ge(probT_sb, 3)
            weighted_values(probT, lambda t, i: proj[:, t, C_V + HD * (i // GROUP):C_V + HD * (i // GROUP) + HD], (3, 0))
            pe.wait_ge(o_sb, 2)
            residual_product(T_OUT, uT, 2)

            uT_blocks(1)
            pe.wait_ge(uT_act, 4)
            pe.wait_ge(uT_dve, 4)

            def dense_up(i):
                n = T_DENSE + i
                pe.wait_ge(up_in[n % RING], up_arrived(n))
                if i >= 2:
                    pe.wait_ge(hid_done, i - 1)
                for f in range(2):
                    for g in range(2):
                        for k in range(KD):
                            mm = pe.matmul(bank[2 * (i % 2) + f][:, TOK * g:TOK * g + TOK],
                                           ffn_up(n % RING)[:, k, g, P * f:P * f + P], uT[:, k, :],
                                           start=(k == 0), stop=(k == KD - 1))
                mm.then_inc(up_used, 1)

            def dense_dn(i):
                pe.wait_ge(dn_in[i % RING], dn_arrived(i))
                pe.wait_ge(hid_done, i + 1)
                for f in range(2):
                    for t in range(NT):
                        for half in range(2):
                            mm = pe.matmul(bank[4 + 2 * t + half], d_h[:, i % 2, f, P * t:P * t + P],
                                           ffn_dn(i % RING)[:, f, 512 * half:512 * half + 512],
                                           start=(i == 0 and f == 0), stop=(i == STEPS - 1 and f == 1))
                mm.then_inc(dn_used, 1)

            for i in range(STEPS):
                dense_up(i)
                if i > 0:
                    dense_dn(i - 1)
            dense_dn(STEPS - 1)

            uT_blocks(2)
            pe.wait_ge(uT_act, 8)
            pe.wait_ge(uT_dve, 8)
            for n0, src, p0 in ((T_BK, uT, 0), (T_BQ, uT_b, 2)):
                for j in range(2):
                    n = n0 + j
                    pe.wait_ge(up_in[n % RING], up_arrived(n))
                    for i in range(4):
                        for k in range(KD):
                            mm = pe.matmul(pair[p0 + j][:, TOK * i:TOK * i + TOK], up_tile(n)[:, k, HD * i:HD * i + HD],
                                           src[:, k, :], start=(k == 0), stop=(k == KD - 1))
                    mm.then_inc(up_used, 1)

            def sticks_z(i):
                if i >= 2:
                    pe.wait_ge(keep_raw, i - 1)
                ps = bank[i % 2]
                pe.matmul(ps[:, 0:TOK], kT_b[:, i, 0:P], qT_b[:, i, :], start=True, stop=True)
                pe.matmul(ps[:, TOK:TOK + P], kT_b[:, i, P:TOK], qT_b[:, i, P:TOK], start=True, stop=True)\
                  .then_inc(z_ps, 1)

            def sticks_after(i):
                pe.wait_ge(keep_done, i + 1)
                if i >= 2:
                    pe.wait_ge(expo_done, i - 1)
                ps, src = bank[2 + i % 2], lk[i % 2]
                pe.matmul(ps[:, 0:TOK], after, src[:, 0:TOK], start=True, stop=False)
                pe.matmul(ps[:, P:TOK], ones, src[:, TOK:TOK + P], start=False, stop=True)
                pe.matmul(ps[:, TOK:TOK + P], after, src[:, TOK:TOK + P], start=True, stop=True).then_inc(after_ps, 1)

            def values(j):
                n, t = T_BV + j // 2, j % 2
                if t == 0:
                    pe.wait_ge(up_in[n % RING], up_arrived(n))
                token_columns(n, t, bank[4 + 2 * t + j // 2], uT).then_inc(v_ps if t == 0 else up_used, 1)

            pe.wait_ge(bk_sb, 2)
            pe.wait_ge(bq_sb, 2)
            sticks_z(0)
            sticks_z(1)
            for j in range(4):
                values(j)
                for i in (2 * j, 2 * j + 1):
                    sticks_after(i)
                    if i + 2 < NH:
                        sticks_z(i + 2)
            pe.wait_ge(stick_done, NH)
            pe.wait_ge(v_sb, 4)
            weighted_values(att, lambda t, i: v_b[:, t, HD * i:HD * i + HD], (0, 1))
            pe.wait_ge(o_sb, 4)
            residual_product(T_BO, uT, 4)

            uT_blocks(3)
            pe.wait_ge(uT_act, 10)
            pe.wait_ge(uT_dve, 10)
            pe.wait_ge(router_in, 16)
            for t in range(NT):
                for k in range(KD):
                    mm = pe.matmul(bank[0][:, NEXP * t:NEXP * t + NEXP], uT[:, k, P * t:P * t + P], router[:, k, :],
                                   start=(k == 0), stop=(k == KD - 1))
            mm.then_inc(route_ps, 1)
            pe.wait_ge(sel_done, 1)
            routed = rt[:, 5]
            pe.matmul(bank[1][:, 0:8], before, routed[:, 0, :], start=True, stop=True)
            pe.matmul(bank[1][:, 8:16], ones, routed[:, 0, :], start=True, stop=False)
            pe.matmul(bank[1][:, 8:16], before, routed[:, 1, :], start=False, stop=True)
            pe.matmul(bank[1][:, 16:24], ones, routed[:, 0, :], start=True, stop=False)
            pe.matmul(bank[1][:, 16:24], ones, routed[:, 1, :], start=False, stop=True).then_inc(rank_ps, 1)

            def block_of(p, b):
                return bank[2 * p + b // 4][:, SLOTS * (b % 4):SLOTS * (b % 4) + SLOTS]

            def gather():
                for b in range(KD):
                    for t in range(NT):
                        mm = pe.matmul(block_of(2, b), u[:, t, P * b:P * b + P], m_pick[:, t, :],
                                       start=(t == 0), stop=(t == NT - 1))
                mm.then_inc(e_gather, 1)

            def result_to_rows(k):
                for b in range(KD):
                    mm = pe.transpose(pair[2][0:SLOTS, P * b:P * b + P], m_yT[:, b, :], ident)
                mm.then_inc(e_y, 1)

            def scatter(k, t):
                if t == 0:
                    pe.wait_ge(e_y_act, k + 1)
                    pe.wait_ge(e_y_dve, k + 1)
                    pe.wait_ge(e_pickT_sb, k + 1)
                for half in range(2):
                    mm = pe.matmul(pair[3 - t][:, 512 * half:512 * half + 512], m_pickT[:, P * t:P * t + P],
                                   m_y[:, 512 * half:512 * half + 512], start=True, stop=True)
                mm.then_inc(e_scatter, 1)

            def expert_up(k, i):
                s = (T_MOE + i) % RING
                pe.wait_ge(up_in[s], job_up_arrived(i, k))
                if i == 0:
                    pe.wait_ge(e_u_act, k + 1)
                    pe.wait_ge(e_u_dve, k + 1)
                if i >= 2:
                    pe.wait_ge(e_hid, k * STEPS + (i - 1))
                for g in range(2):
                    for f in range(2):
                        for b in range(KD):
                            mm = pe.matmul(bank[i % 2][:, SLOTS * (2 * g + f):SLOTS * (2 * g + f + 1)],
                                           ffn_up(s)[:, b, g, P * f:P * f + P], m_u[:, b, :],
                                           start=(b == 0), stop=(b == KD - 1))
                mm.then_inc(up_used, 1)

            def expert_dn(k, i):
                s = (STEPS + i) % RING
                pe.wait_ge(dn_in[s], job_dn_arrived(i, k))
                pe.wait_ge(e_hid, k * STEPS + (i + 1))
                for f in range(2):
                    for b in range(KD):
                        mm = pe.matmul(block_of(1, b), ffn_dn(s)[:, f, P * b:P * b + P], m_h[:, i % 2, f, :],
                                       start=(i == 0 and f == 0 and b % 4 == 0),
                                       stop=(i == STEPS - 1 and f == 1), skip_group_check=True)
                mm.then_inc(dn_used, 1)

            def job(k):
                for i in range(STEPS):
                    expert_up(k, i)
                    if i == 1:
                        pe.wait_ge(e_yT_act, k + 1)
                        pe.wait_ge(e_yT_dve, k + 1)
                    if i == 2:
                        result_to_rows(k)
                    if i == 4:
                        scatter(k, 0)
                    if i == 5:
                        scatter(k, 1)
                    if i == 7:
                        pe.wait_ge(e_pick, k * 2 + 2)
                        pe.wait_ge(e_added, k * NT + 2)
                        for t in range(NT):
                            mm = pe.transpose(bank[6][0:SLOTS, P * t:P * t + P], m_pick[:, t, :], ident)
                        mm.then_inc(e_pickT, 1)
                    if i == 9:
                        pe.wait_ge(e_pick, k * 2 + 3)
                        pe.wait_ge(e_added, k * NT + 3)
                        gather()
                    if i > 0:
                        expert_dn(k, i - 1)
                expert_dn(k, STEPS - 1)

            pe.wait_ge(e_pick, 1)
            gather()
            with pe.Fori(0, NEXP) as k:
                job(k)
            pe.wait_ge(jobs_known, 1)
            jobs = pe.value_load(n_jobs[0:1, 0:1], min_val=NEXP, max_val=JOBS)
            with pe.If(jobs > NEXP):
                with pe.Fori(NEXP, JOBS) as k:
                    job(k)
            pe.wait_ge(e_yT_act, jobs + 1)
            pe.wait_ge(e_yT_dve, jobs + 1)
            pe.wait_ge(e_u_act, jobs + 1)
            pe.wait_ge(e_u_dve, jobs + 1)
            result_to_rows(jobs)
            scatter(jobs, 0)
            scatter(jobs, 1)

        @block.scalar
        def _(act):
            act.dma_start(cst[:, :], consts).then_inc(consts_in, 16)
            for r, w in enumerate((a_norm_w[0], ffn_norm_w[0], kv_norm_w, b_norm_w[0], ffn_norm_w[1])):
                act.dma_start(norm_rows[KD * r:KD * r + KD, :], w.rearrange("(k c) -> k c", c=P)).then_inc(rows_in, 16)
            act.dma_start(qk_w[:, 0, :], a_q_norm_w[0].partition_broadcast(P)).then_inc(qkw_in, 16)
            act.dma_start(qk_w[:, 1, :], a_k_norm_w[0].partition_broadcast(P)).then_inc(qkw_in, 16)
            act.dma_start(router[:, :, :], moe_router_w[0].rearrange("(k p) e -> p k e", p=P)).then_inc(router_in, 16)

            def copy(out_, in_, scale=1.0):
                return act.activation(out_, in_, ACT.Copy, scale=scale)

            def sums_of_squares(n):
                for t in range(NT):
                    if n == 0:
                        if t == 0:
                            act.wait_ge(x_in, 16)
                    else:
                        act.wait_ge(h_done, (4, 8, 12)[n - 1] - 1 + t)
                    act.activation(u[:, t, :], h[:, t, :], ACT.Square, accum_out=stat[:, 2 * n + t:2 * n + t + 1])\
                       .then_inc(sumsq, 1)
                act.wait_ge(ms_done, n + 1)
                act.activation(stat[:, 8 + 2 * n:10 + 2 * n], stat[:, 8 + 2 * n:10 + 2 * n], ACT.Sqrt).then_inc(root_done, 1)

            def uT_part(n, norm, banks, dst):
                for b in banks:
                    act.wait_ge(uT_ps, 4 * n + b + 1)
                    for k in (2 * b, 2 * b + 1):
                        c = 256 * (k % 2)
                        e = copy(dst[:, k, :], bank[4 + b][:, c:c + TOK], nw[:, KD * norm + k:KD * norm + k + 1])
                    e.then_inc(uT_act, 1)

            sums_of_squares(0)
            act.wait_ge(nw_done, 1)
            uT_part(0, NORM_A, (0, 2), uT)

            def proj_copy(j):
                c, cols = IN_COLS[j]
                for t in range(NT):
                    if t == 0:
                        act.wait_ge(proj_ps, j + 1)
                    else:
                        act.wait_ge(up_used, j + 1)
                    copy(proj[:, t, c:c + cols], bank[(NT * j + t) % 4][:, 0:cols]).then_inc(proj_sb, 1)

            def qk_squares(g):
                c, n = ((C_K, 2), (0, 4), (512, 4))[g]
                act.wait_ge(proj_sb, (6, 8, 10)[g])
                if g > 0:
                    act.wait_ge(qk_ms, g)
                act.activation(sq[:, :, 0:HD * n], proj[:, :, c:c + HD * n], ACT.Square).then_inc(qk_sq, 1)
                act.wait_ge(qk_ms, g + 1)
                act.activation(qk_rs[:, g, :, 0:n], qk_rs[:, g, :, 0:n], ACT.Sqrt).then_inc(qk_root, 1)

            def relu_scores(n):
                act.wait_ge(idx_qk, n + 1)
                for odd in range(2):
                    ps = bank[(4, 6, 4)[n] + odd]
                    if n == 0:
                        dst, src = rel0[:, odd:8:2, :], ps.rearrange("p (i s) -> p i s", i=4)
                    else:
                        dst, src = rel1[:, 4 * (n - 1) + odd:4 * n:2, :], ps.rearrange("p (i s) -> p i s", i=2)
                    act.activation(dst, src, ACT.Relu, scale=ID ** -0.5).then_inc(rel_done, 1)

            proj_copy(0)
            proj_copy(1)
            proj_copy(2)
            qk_squares(0)
            act.wait_ge(idx_T, 1)
            for n in range(2):
                copy(qiT[:, 2 * n:2 * n + 2, :], bank[4 + n].rearrange("p (j t) -> p j t", j=2)).then_inc(idx_T_sb, 1)
            copy(kiT, bank[6][:, 0:TOK]).then_inc(idx_T_sb, 1)
            proj_copy(3)
            relu_scores(0)
            relu_scores(1)
            relu_scores(2)
            proj_copy(4)
            qk_squares(1)
            qk_squares(2)
            for n, ps in enumerate((bank[4], bank[5], bank[6], bank[7], bank[0])):
                act.wait_ge(qk_T, n + 1)
                dst = kT_a[:, :, :] if n == 0 else qT_a[:, 2 * (n - 1):2 * n, :]
                copy(dst, ps.rearrange("p (i t) -> p i t", i=2)).then_inc(qk_T_sb, 1)
            for g in range(3):
                act.wait_ge(rowmax_done, g + 1)
                for i in range(8 if g == 0 else 4):
                    r = i if g == 0 else 8 + 4 * (g - 1) + i
                    row = prob0[:, i, :] if g == 0 else prob1[:, 4 * (g - 1) + i, :]
                    e = act.activation(row, row, ACT.Exp, bias=soft[:, 0, r:r + 1], accum_out=soft[:, 1, r:r + 1])
                e.then_inc(exp_done, 1)
            for g in range(3):
                act.wait_ge(probT_ps, g + 1)
                if g == 0:
                    copy(probT[:, :, 0:P], pair[0][:, :].rearrange("p (i s) -> p i s", i=8)).then_inc(probT_sb, 1)
                else:
                    copy(probT[:, 4 * (g - 1):4 * g, P:], pair[g][:, :].rearrange("p (i s) -> p i s", i=4)).then_inc(probT_sb, 1)
            act.wait_ge(o_ps, 1)
            copy(uT[:, 0:4, :], pair[3][:, :].rearrange("p (i t) -> p i t", i=4)).then_inc(o_sb, 1)

            sums_of_squares(1)
            uT_part(1, NORM_F0, (0, 2), uT)
            for i in range(STEPS):
                act.wait_ge(up_used, T_DENSE + i + 1)
                if i >= 2:
                    act.wait_ge(hid_done, i - 1)
                gate = pair[i % 2][:, :].rearrange("p (f c) -> p f c", f=2)[:, :, 0:TOK]
                act.activation(d_silu[:, i % 2], gate, ACT.Silu).then_inc(silu_done, 1)

            sums_of_squares(2)
            uT_part(2, NORM_KV, (0, 1), uT)
            act.wait_ge(uT_dve, 6)
            uT_part(2, NORM_KV, (2, 3), uT)
            for j in range(2):
                act.wait_ge(up_used, T_BK + j + 1)
                copy(kT_b[:, 4 * j:4 * j + 4, :], pair[j][:, :].rearrange("p (i t) -> p i t", i=4)).then_inc(bk_sb, 1)

            def log1p_exp(i):
                act.wait_ge(z_ps, i + 1)
                if i >= 2:
                    act.wait_ge(keep_raw, i - 1)
                b = absz[i % 2]
                act.activation(b, bank[i % 2][:, 0:384], ACT.Abs, scale=SCALE).then_inc(z_log, 1)
                act.wait_ge(z_log, 3 * i + 1)
                act.activation(b, b, ACT.Exp, scale=-1.0).then_inc(z_log, 1)
                act.wait_ge(z_log, 3 * i + 2)
                act.activation(b, b, ACT.Ln, bias=1.0).then_inc(z_log, 1)

            def stick_weights(i):
                act.wait_ge(expo_done, i + 1)
                act.activation(att[:, i, :], neg[i % 2], ACT.Exp).then_inc(stick_raw, 1)

            for i in range(NH):
                log1p_exp(i)
                if i >= 1:
                    stick_weights(i - 1)
                if i % 2 == 1:
                    j = i // 2
                    if j % 2 == 0:
                        act.wait_ge(v_ps, j // 2 + 1)
                    else:
                        act.wait_ge(up_used, T_BV + j // 2 + 1)
                    copy(v_b[:, j % 2, 512 * (j // 2):512 * (j // 2) + 512], bank[4 + 2 * (j % 2) + j // 2]).then_inc(v_sb, 1)
            stick_weights(NH - 1)
            act.wait_ge(o_ps, 3)
            copy(uT[:, 0:4, :], pair[0][:, :].rearrange("p (i t) -> p i t", i=4)).then_inc(o_sb, 1)

            sums_of_squares(3)
            uT_part(3, NORM_F1, (0, 2), uT)
            act.wait_ge(route_top, 1)
            for t in range(NT):
                e = act.activation(rt[:, 6, t, :], rt[:, 0, t, :], ACT.Exp, bias=rt[:, 9, t, 2:3])
            e.then_inc(route_exp, 1)

            def gathered(k):
                act.wait_ge(e_gather, k + 1)
                for b in range(4):
                    e = copy(m_u[:, b, :], bank[4][:, SLOTS * b:SLOTS * b + SLOTS], nw[:, KD * NORM_F1 + b:KD * NORM_F1 + b + 1])
                e.then_inc(e_u_act, 1)

            def rows(k):
                act.wait_ge(e_y, k + 1)
                act.wait_ge(e_scatter, k * NT + 1)
                copy(m_y[:, 0:512], bank[4][0:SLOTS, :]).then_inc(e_y_act, 1)

            def job(k):
                for i in range(STEPS):
                    act.wait_ge(up_used, k * STEPS + (T_MOE + i + 1))
                    if i >= 2:
                        act.wait_ge(e_hid, k * STEPS + (i - 1))
                    act.activation(m_silu[:, i % 2], bank[i % 2][:, 0:2 * SLOTS].rearrange("p (f c) -> p f c", f=2),
                                   ACT.Silu).then_inc(e_silu, 1)
                    if i == 2:
                        rows(k)
                    if i == 7:
                        act.wait_ge(e_pickT, k + 1)
                        act.wait_ge(e_scatter, k * NT + 3)
                        copy(m_pickT, bank[6][0:SLOTS, 0:TOK]).then_inc(e_pickT_sb, 1)
                gathered(k + 1)
                act.wait_ge(dn_used, k * STEPS + 2 * STEPS)
                act.wait_ge(e_y, k + 1)
                copy(m_yT[:, 0:4, :], bank[2][:, 0:4 * SLOTS].rearrange("p (b c) -> p b c", b=4)).then_inc(e_yT_act, 1)

            gathered(0)
            with act.Fori(0, NEXP) as k:
                job(k)
            act.wait_ge(jobs_known, 1)
            jobs = act.value_load(n_jobs[0:1, 0:1], min_val=NEXP, max_val=JOBS)
            with act.If(jobs > NEXP):
                with act.Fori(NEXP, JOBS) as k:
                    job(k)
            rows(jobs)

        @block.gpsimd
        def _(pool):
            mask = before.unsqueeze(1).to_broadcast([P, 2, P])

            def diagonal(v):
                return v.rearrange("p (b c) -> p b c", b=3)[:, 0:3:2, :]

            pool.wait_ge(consts_in, 16)
            for i in range(NH + 1):
                if i < NH:
                    pool.wait_ge(keep_raw, i + 1)
                    pool.tensor_tensor(diagonal(lk[i % 2]), diagonal(lk[i % 2]), mask, ALU.mult).then_inc(keep_done, 1)
                if i >= 1:
                    pool.wait_ge(stick_raw, i)
                    pool.tensor_tensor(diagonal(att[:, i - 1, :]), diagonal(att[:, i - 1, :]), mask, ALU.mult)\
                        .then_inc(stick_done, 1)

        @block.vector
        def _(dve):
            marks = [0]

            def mark(ins):
                marks[0] += 1
                ins.then_inc(dve_chain, 1)
                return marks[0]

            def reads(n):
                dve.wait_ge(dve_chain, n)

            def normalise(n):
                dve.wait_ge(sumsq, NT * (n + 1))
                rs = stat[:, 8 + 2 * n:10 + 2 * n]
                dve.tensor_scalar(rs, stat[:, 2 * n:2 * n + 2], 1.0 / DM, EPS, ALU.mult, ALU.add).then_inc(ms_done, 1)
                dve.wait_ge(root_done, n + 1)
                reads(mark(dve.reciprocal(rs, rs)))
                for t in range(NT):
                    dve.tensor_scalar(u[:, t, :], h[:, t, :], rs[:, t:t + 1], None, ALU.mult).then_inc(u_done, 1)

            def uT_part(n, norm, banks, dst):
                for b in banks:
                    dve.wait_ge(uT_ps, 4 * n + b + 1)
                    for k in (2 * b, 2 * b + 1):
                        c = 256 * (k % 2)
                        last = dve.tensor_scalar(dst[:, k, :], bank[4 + b][:, c:c + TOK],
                                                 nw[:, KD * norm + k:KD * norm + k + 1], None, ALU.mult)
                    last.then_inc(uT_dve, 1)

            def add_residual(first_bank, tile0, res0):
                for half in range(2):
                    for t in range(NT):
                        if t == 0:
                            dve.wait_ge(res_ps, res0 + half + 1)
                        else:
                            dve.wait_ge(up_used, tile0 + half + 1)
                        c = slice(512 * half, 512 * half + 512)
                        dve.tensor_tensor(h[:, t, c], h[:, t, c], bank[first_bank + 2 * t + half], ALU.add).then_inc(h_done, 1)

            def rope(v, half, step):
                n = v.shape[2]
                shape = [P, NT, n, half]
                c = cos[:, :, 0:16:step].unsqueeze(2).to_broadcast(shape)
                s = sin[:, :, 0:16:step].unsqueeze(2).to_broadcast(shape)
                tmp = prob0.rearrange("p h s -> p (h s)")
                t1, t2, t3, t4 = (tmp[:, 256 * j:256 * j + NT * n * half].rearrange("p (t n f) -> p t n f", t=NT, n=n)
                                  for j in range(4))
                x1, x2 = v[:, :, :, 0:half], v[:, :, :, half:2 * half]
                dve.tensor_tensor(t1, x1, c, ALU.mult)
                dve.tensor_tensor(t2, x2, s, ALU.mult)
                dve.tensor_tensor(t3, x2, c, ALU.mult)
                reads(mark(dve.tensor_tensor(t4, x1, s, ALU.mult)))
                dve.tensor_tensor(x1, t1, t2, ALU.subtract)
                return dve.tensor_tensor(x2, t3, t4, ALU.add)

            dve.wait_ge(nw_ps, 1)
            dve.tensor_copy(nw[:, :], bank[0][:, 0:5 * KD]).then_inc(nw_done, 1)
            normalise(0)
            dve.wait_ge(nw_done, 1)
            uT_part(0, NORM_A, (1, 3), uT)

            dve.wait_ge(proj_sb, 4)
            reads(mark(rope(proj[:, :, C_QI:C_WI].rearrange("p t (n d) -> p t n d", d=ID), ID // 8, 2)))
            for t in range(NT):
                dve.tensor_copy(ki2[:, t, :].rearrange("p (r d) -> p r d", r=2),
                                proj[:, t, C_KI:C_WI].unsqueeze(1).to_broadcast([P, 2, ID]))
            dve.tensor_scalar(w_idx[:, :, :], proj[:, :, C_WI:A_IN], IH ** -0.5, None, ALU.mult).then_inc(idx_roped, 1)

            def qk_norm(g):
                c, n = ((C_K, 2), (0, 4), (512, 4))[g]
                v = proj[:, :, c:c + HD * n].rearrange("p t (n d) -> p t n d", d=HD)
                dve.wait_ge(qk_sq, g + 1)
                reads(mark(dve.tensor_reduce(qk_ss[:, g, :, 0:n], sq[:, :, 0:HD * n].rearrange("p t (n d) -> p t n d", d=HD),
                                             AX.X, ALU.add)))
                rs = qk_rs[:, g, :, 0:n]
                dve.tensor_scalar(rs, qk_ss[:, g, :, 0:n], 1.0 / HD, EPS, ALU.mult, ALU.add).then_inc(qk_ms, 1)
                dve.wait_ge(qk_root, g + 1)
                reads(mark(dve.reciprocal(rs, rs)))
                for t in range(NT):
                    for i in range(n):
                        last = dve.scalar_tensor_tensor(v[:, t, i, :], v[:, t, i, :], qk_rs[:, g, t, i:i + 1],
                                                        qk_w[:, int(g == 0), :], ALU.mult, ALU.mult)
                reads(mark(last))
                rope(v, HD // 8, 1).then_inc(qk_roped, 1)

            dve.wait_ge(qkw_in, 32)
            qk_norm(0)

            dve.wait_ge(idx_roped, 1)
            dve.wait_ge(rel_done, 6)
            rel = (rel0, rel1)
            masks = (imask[:, P:2 * P], imask)
            done = [0, 0]
            for i in range(IH):
                for t in range(NT):
                    if i:
                        reads(done[t])
                    done[t] = mark(dve.scalar_tensor_tensor(score[t], rel[t][:, i, :], w_idx[:, t, i:i + 1],
                                                            masks[t] if i == 0 else score[t], ALU.mult, ALU.add))
            for _ in range(TOPK // 8):
                for t in range(NT):
                    reads(done[t])
                    done[t] = mark(dve.max(top8[:, t, :], score[t]))
                for t in range(NT):
                    reads(done[t])
                    done[t] = mark(dve.match_replace(score[t], top8[:, t, :], score[t], TAKEN))
            for t in range(NT):
                reads(done[t])
                done[t] = mark(dve.tensor_scalar(bias[t], score[t], 0.5 * (TAKEN + NOT_CAUSAL), MASKED, ALU.is_ge, ALU.mult))
            for t in range(NT):
                reads(done[t])
                own = bias[t][:, P * t:P * t + P]
                done[t] = mark(dve.tensor_tensor(own, own, imask[:, P:2 * P], ALU.add))
            qk_norm(1)
            qk_norm(2)

            def group(g):
                return (prob0, 0, 8, 0) if g == 0 else (prob1[:, 4 * (g - 1):4 * g, :], 4 + 4 * g, 4, 1)

            dve.wait_ge(qk_roped, 3)
            for g in range(3):
                prob, r, n, t = group(g)
                dve.wait_ge(logits_ps, g + 1)
                reads(done[t])
                for b in range(2):
                    part = prob[:, b * n // 2:(b + 1) * n // 2, :]
                    last = dve.scalar_tensor_tensor(part, bank[2 * (g + 1) + b].rearrange("p (i s) -> p i s", i=n // 2), SCALE,
                                                    bias[t].unsqueeze(1).to_broadcast([P, n // 2, P * (t + 1)]),
                                                    ALU.mult, ALU.add)
                reads(mark(last))
                dve.tensor_reduce(soft[:, 0, r:r + n], prob, AX.X, ALU.max, negate=True).then_inc(rowmax_done, 1)
            for g in range(3):
                prob, r, n, t = group(g)
                dve.wait_ge(exp_done, g + 1)
                reads(mark(dve.reciprocal(soft[:, 2, r:r + n], soft[:, 1, r:r + n])))
                dve.tensor_tensor(prob, prob, soft[:, 2, r:r + n].unsqueeze(2).to_broadcast([P, n, P * (t + 1)]),
                                  ALU.mult).then_inc(prob_done, 1)
            dve.wait_ge(o_ps, 2)
            dve.tensor_copy(uT[:, 4:8, :], pair[0][:, :].rearrange("p (i t) -> p i t", i=4)).then_inc(o_sb, 1)
            add_residual(2, T_OUT, 0)

            dve.wait_ge(h_done, 4)
            normalise(1)
            uT_part(1, NORM_F0, (1, 3), uT)
            for i in range(STEPS):
                dve.wait_ge(silu_done, i + 1)
                if i >= 2:
                    dve.wait_ge(dn_used, i - 1)
                up = pair[i % 2][:, :].rearrange("p (f c) -> p f c", f=2)[:, :, TOK:2 * TOK]
                dve.tensor_tensor(d_h[:, i % 2], d_silu[:, i % 2], up, ALU.mult).then_inc(hid_done, 1)
            dve.wait_ge(dn_used, STEPS)
            for half in range(2):
                for t in range(NT):
                    c = slice(512 * half, 512 * half + 512)
                    dve.tensor_tensor(h[:, t, c], h[:, t, c], bank[4 + 2 * t + half], ALU.add).then_inc(h_done, 1)

            dve.wait_ge(h_done, 8)
            normalise(2)
            uT_part(2, NORM_B, (2, 3), uT_b)
            dve.wait_ge(uT_act, 6)
            uT_part(2, NORM_B, (0, 1), uT_b)
            for j in range(2):
                dve.wait_ge(up_used, T_BQ + j + 1)
                dve.tensor_copy(qT_b[:, 4 * j:4 * j + 4, :], pair[2 + j][:, :].rearrange("p (i t) -> p i t", i=4)).then_inc(bq_sb, 1)

            def log_keep(i):
                z, b = bank[i % 2][:, 0:384], i % 2
                dve.wait_ge(z_ps, i + 1)
                dve.wait_ge(z_log, 3 * i + 3)
                reads(mark(dve.tensor_scalar(lb[b], z, SCALE, 0.0, ALU.mult, ALU.min)))
                reads(mark(dve.tensor_tensor(lb[b], lb[b], absz[b], ALU.subtract)))
                if i >= 2:
                    dve.wait_ge(after_ps, i - 1)
                dve.scalar_tensor_tensor(lk[b], z, -SCALE, lb[b], ALU.mult, ALU.add).then_inc(keep_raw, 1)

            def exponent(i):
                dve.wait_ge(after_ps, i + 1)
                if i >= 2:
                    dve.wait_ge(stick_raw, i - 1)
                dve.tensor_tensor(neg[i % 2], bank[2 + i % 2][:, 0:384], lb[i % 2], ALU.add).then_inc(expo_done, 1)

            log_keep(0)
            for i in range(NH):
                if i + 1 < NH:
                    log_keep(i + 1)
                exponent(i)
            dve.wait_ge(o_ps, 4)
            dve.tensor_copy(uT[:, 4:8, :], pair[1][:, :].rearrange("p (i t) -> p i t", i=4)).then_inc(o_sb, 1)
            add_residual(4, T_BO, 2)

            dve.wait_ge(h_done, 12)
            normalise(3)
            uT_part(3, NORM_F1, (1, 3), uT)
            lg, gt, eq, rank, fits, routed, ex, gate, need = (rt[:, j] for j in range(9))
            misc = rt[:, 9]
            wide = [P, NT, NEXP]
            dve.memset(m_yT[:, 0:4, :], 0.0).then_inc(e_yT_act, 1)
            dve.memset(m_yT[:, 4:8, :], 0.0).then_inc(e_yT_dve, 1)
            dve.memset(m_pickT, 0.0).then_inc(e_pickT_sb, 1)
            dve.memset(m_y, 0.0).then_inc(e_scatter, 1)
            dve.memset(gate_of[:, :, 0:1], 0.0).then_inc(e_added, 1)
            dve.memset(slot_of[:, :, JOBS:JOBS + 1], NO_SLOT)
            dve.wait_ge(route_ps, 1)
            reads(mark(dve.tensor_copy(lg, bank[0][:, 0:NT * NEXP].rearrange("p (t e) -> p t e", t=NT))))
            for t in range(NT):
                last = dve.max(top8[:, t, :], lg[:, t, :])
            reads(mark(last))
            first, second = top8[:, :, 0:1], top8[:, :, 1:2]
            dve.tensor_scalar(misc[:, :, 2:3], first, -1.0, None, ALU.mult).then_inc(route_top, 1)
            dve.tensor_tensor(misc[:, :, 0:1], first, second, ALU.is_gt)
            dve.tensor_tensor(gt, lg, second.to_broadcast(wide), ALU.is_gt)
            reads(mark(dve.tensor_tensor(eq, lg, second.to_broadcast(wide), ALU.is_equal)))
            for t in range(NT):
                dve.tensor_tensor_scan(rank[:, t, :], ones[:, 0:NEXP], eq[:, t, :], 0.0, ALU.mult, ALU.add)
            reads(mark(dve.tensor_scalar(misc[:, :, 1:2], misc[:, :, 0:1], -1.0, 2.0, ALU.mult, ALU.add)))
            reads(mark(dve.tensor_tensor(fits, rank, misc[:, :, 1:2].to_broadcast(wide), ALU.is_le)))
            reads(mark(dve.tensor_tensor(fits, fits, eq, ALU.mult)))
            dve.tensor_tensor(routed, fits, gt, ALU.add).then_inc(sel_done, 1)
            dve.wait_ge(sel_done, 1)
            dve.wait_ge(route_exp, 1)
            reads(mark(dve.tensor_tensor(ex, ex, routed, ALU.mult)))
            reads(mark(dve.tensor_reduce(misc[:, :, 3:4], ex, AX.X, ALU.add)))
            reads(mark(dve.reciprocal(misc[:, :, 4:5], misc[:, :, 3:4])))
            reads(mark(dve.tensor_tensor(gate, ex, misc[:, :, 4:5].to_broadcast(wide), ALU.mult)))
            dve.wait_ge(rank_ps, 1)
            ranks = bank[1][:, 0:NT * NEXP].rearrange("p (t e) -> p t e", t=NT)
            reads(mark(dve.tensor_scalar(rank, ranks, -NO_SLOT, None, ALU.add)))
            reads(mark(dve.tensor_tensor(rank, rank, routed, ALU.mult)))
            for c in range(CHUNKS):
                dve.tensor_copy(gate_of[:, :, 1 + NEXP * c:1 + NEXP * (c + 1)], gate)
                last = dve.tensor_scalar(slot_of[:, :, NEXP * c:NEXP * (c + 1)], rank, NO_SLOT - SLOTS * c, None, ALU.add)
            reads(mark(dve.tensor_reduce(misc[:, 0, 5:6], bank[1][:, 2 * NEXP:3 * NEXP], AX.X, ALU.max)))
            reads(mark(dve.tensor_scalar(misc[:, 0, 6:7], misc[:, 0, 5:6], float(SLOTS), float(JOBS - NEXP), ALU.is_gt, ALU.mult)))
            dve.tensor_scalar(n_jobs[:, :], misc[:, 0, 6:7], float(NEXP), None, ALU.add).then_inc(jobs_known, 1)

            def pick(j):
                for t in range(NT):
                    last = dve.tensor_scalar(m_pick[:, t, :], slot_no, slot_of[:, t, bass.ds(j, 1)], None, ALU.is_equal)
                last.then_inc(e_pick, 1)

            def gathered(k):
                dve.wait_ge(e_gather, k + 1)
                w = nw[:, KD * NORM_F1 + 4:KD * NORM_F1 + 8].unsqueeze(2).to_broadcast([P, 4, SLOTS])
                dve.tensor_tensor(m_u[:, 4:8, :], bank[5][:, 0:4 * SLOTS].rearrange("p (b c) -> p b c", b=4), w, ALU.mult)\
                   .then_inc(e_u_dve, 1)

            def rows(k):
                dve.wait_ge(e_y, k + 1)
                dve.wait_ge(e_scatter, k * NT + 1)
                dve.tensor_copy(m_y[:, 512:1024], bank[5][0:SLOTS, :]).then_inc(e_y_dve, 1)

            def add_scattered(k, t):
                dve.wait_ge(e_scatter, k * NT + (t + 2))
                dve.wait_ge(e_added, k * NT + (t + 1))
                dve.scalar_tensor_tensor(h[:, t, :], pair[3 - t][:, :], gate_of[:, t, bass.ds(k, 1)], h[:, t, :],
                                         ALU.mult, ALU.add).then_inc(e_added, 1)

            def job(k):
                for i in range(STEPS):
                    dve.wait_ge(e_silu, k * STEPS + (i + 1))
                    dve.wait_ge(dn_used, k * STEPS + (STEPS + (i - 1 if i >= 2 else 0)))
                    dve.tensor_tensor(m_h[:, i % 2], m_silu[:, i % 2],
                                      bank[i % 2][:, 2 * SLOTS:4 * SLOTS].rearrange("p (f c) -> p f c", f=2),
                                      ALU.mult).then_inc(e_hid, 1)
                    if i == 2:
                        rows(k)
                    if i == 4:
                        add_scattered(k, 0)
                    if i == 5:
                        add_scattered(k, 1)
                    if i == 6:
                        dve.wait_ge(e_gather, k + 1)
                        pick(k)
                    if i == 8:
                        dve.wait_ge(e_pickT, k + 1)
                        pick(k + 1)
                gathered(k + 1)
                dve.wait_ge(dn_used, k * STEPS + 2 * STEPS)
                dve.wait_ge(e_y, k + 1)
                dve.tensor_copy(m_yT[:, 4:8, :], bank[3][:, 0:4 * SLOTS].rearrange("p (b c) -> p b c", b=4)).then_inc(e_yT_dve, 1)

            dve.wait_ge(jobs_known, 1)
            pick(0)
            gathered(0)
            with dve.Fori(0, NEXP) as k:
                job(k)
            jobs = dve.value_load(n_jobs[0:1, 0:1], min_val=NEXP, max_val=JOBS)
            with dve.If(jobs > NEXP):
                with dve.Fori(NEXP, JOBS) as k:
                    job(k)
            rows(jobs)
            add_scattered(jobs, 0)
            add_scattered(jobs, 1)


def shape_constants():
    import numpy as np
    c = np.zeros((P, K_END), np.float32)
    r = np.arange(P)
    c[:, K_ID:K_ID + P] = np.eye(P)
    c[:, K_BEFORE:K_BEFORE + P] = r[:, None] < r[None, :]
    c[:, K_AFTER:K_AFTER + P] = r[:, None] > r[None, :]
    c[:, K_ONES:K_ONES + P] = 1.0
    c[:, K_IMASK + P:K_IMASK + 2 * P] = np.where(r[None, :] > r[:, None], np.float32(NOT_CAUSAL), np.float32(0))
    c[:, K_SLOT:K_SLOT + SLOTS] = np.arange(SLOTS)
    inv = np.float32(500000.0) ** (-np.arange(16, dtype=np.float32) * np.float32(2.0) / np.float32(32))
    angle = np.arange(TOK, dtype=np.float32)[:, None] * inv.astype(np.float32)[None, :]
    for k, fn in ((K_COS, np.cos), (K_SIN, np.sin)):
        c[:, k:k + 32] = fn(angle).reshape(NT, P, 16).transpose(1, 0, 2).reshape(P, 32)
    return c


_INS = ["x", "a_norm_w", "a_w_in", "a_q_norm_w", "a_k_norm_w", "a_w_out", "kv_norm_w", "kv_w", "b_norm_w",
        "b_w_q", "b_w_out", "ffn_norm_w", "dense_w_gate_up", "dense_w_down", "moe_router_w",
        "moe_w_gate_up", "moe_w_down"]


def kernel(**inputs):
    import numpy as np
    import concourse.bacc as bacc
    from concourse.bass_utils import run_bass_kernel_spmd

    nc = bacc.Bacc("TRN2", target_bir_lowering=False, num_devices=1)
    arrays = {f"in_{name}": np.ascontiguousarray(inputs[name]) for name in _INS}
    arrays["in_consts"] = shape_constants()
    args = [nc.dram_tensor(name, a.shape, mybir.dt.from_np(a.dtype), kind="ExternalInput").ap()
            for name, a in arrays.items()]
    args.append(nc.dram_tensor("out_0", (1, TOK, DM), mybir.dt.float32, kind="ExternalOutput").ap())
    program(nc, *args)
    return run_bass_kernel_spmd(nc, [arrays], core_ids=[0]).results[0]["out_0"]
```

```python
import concourse.bass as bass
from concourse import mybir
from concourse.alu_op_type import AluOpType as ALU
from contextlib import ExitStack

P = 128
TOK = 256
NT = TOK // P
DM = 1024
KD = DM // P
HD = 128
NH = 8
NKV = 2
GROUP = NH // NKV
IH, ID = 8, 64
A_IN = 2120
C_K, C_V, C_QI, C_KI, C_WI = 1024, 1280, 1536, 2048, 2112
TOPK = 64
F = 2816
FSTEP = 256
STEPS = F // FSTEP
NEXP = 8
SLOTS = 96
CHUNKS = -(-TOK // SLOTS)
JOBS = NEXP * CHUNKS
RING = 4
EPS = 1e-6
SCALE = HD ** -0.5
NOT_CAUSAL = -1.0e38
TAKEN = -2.0e38
MASKED = -1.0e30
NO_SLOT = -1.0e4

K_ID, K_BEFORE, K_AFTER, K_ONES, K_IMASK, K_SLOT, K_COS, K_SIN = 0, 128, 256, 384, 512, 768, 864, 896
K_END = 928

NORM_A, NORM_F0, NORM_KV, NORM_B, NORM_F1 = range(5)

T_IN, T_OUT, T_DENSE = 0, 5, 7
T_BQ, T_BK, T_BV, T_BO = T_DENSE + STEPS, T_DENSE + STEPS + 2, T_DENSE + STEPS + 4, T_DENSE + STEPS + 6
T_MOE = T_BO + 2
IN_COLS = [(C_QI, 512), (C_KI, 72), (C_K, 512), (0, 512), (512, 512)]


def program(nc, x, a_norm_w, a_w_in, a_q_norm_w, a_k_norm_w, a_w_out, kv_norm_w, kv_w, b_norm_w,
            b_w_q, b_w_out, ffn_norm_w, dense_w_gate_up, dense_w_down, moe_router_w,
            moe_w_gate_up, moe_w_down, consts, out):
    f32, f32r, i32 = mybir.dt.float32, mybir.dt.float32r, mybir.dt.int32
    ACT = mybir.ActivationFunctionType
    AX = mybir.AxisListType
    ctx = ExitStack()
    with ctx:
        def sb(name, shape, dt=f32):
            return ctx.enter_context(nc.sbuf_tensor(name, shape, dt))

        def sem(name):
            return ctx.enter_context(nc.semaphore(name))

        up_ring = sb("up_ring", [P, RING, 4096])
        dn_ring = sb("dn_ring", [P, RING, 2048])
        up_hi = sb("up_hi", [P, 2, 2048], f32r)
        up_lo = sb("up_lo", [P, 2, 2048], f32r)
        dn_hi = sb("dn_hi", [P, 2, DM], f32r)
        dn_lo = sb("dn_lo", [P, 2, DM], f32r)
        cst = sb("cst", [P, K_END])
        h = sb("h", [P, NT, DM])
        u = sb("u", [P, NT, DM])
        uT_hi = sb("uT_hi", [P, KD, TOK], f32r)
        uT_lo = sb("uT_lo", [P, KD, TOK], f32r)
        q_T = sb("q_T", [P, NH, TOK])
        hid_hi = sb("hid_hi", [P, 512], f32r)
        hid_lo = sb("hid_lo", [P, 512], f32r)
        router_hi = sb("router_hi", [P, KD * NEXP], f32r)
        router_lo = sb("router_lo", [P, KD * NEXP], f32r)
        work = sb("work", [P, NT * (A_IN - DM)])
        kT_a = sb("kT_a", [P, NKV, TOK])
        norm_rows = sb("norm_rows", [5 * KD, P])
        nw = sb("nw", [P, 5 * KD])
        qk_w = sb("qk_w", [P, 2, HD])
        router = sb("router", [P, KD, NEXP])
        stat = sb("stat", [P, 16])
        silu_of_one = sb("silu_of_one", [1, 1])
        qk_ss = sb("qk_ss", [P, 3, NT, GROUP])
        qk_rs = sb("qk_rs", [P, 3, NT, GROUP])
        w_idx = sb("w_idx", [P, NT, IH])
        top8 = sb("top8", [P, NT, 8])
        soft = sb("soft", [P, 3, NT * NH])
        rt = sb("rt", [P, 10, NT, NEXP])
        slot_of = sb("slot_of", [P, NT, JOBS + 1])
        gate_of = sb("gate_of", [P, NT, JOBS + 1])
        n_last_job = sb("n_last_job", [P, 1], i32)

        ident, before, after = cst[:, K_ID:K_ID + P], cst[:, K_BEFORE:K_BEFORE + P], cst[:, K_AFTER:K_AFTER + P]
        ones, imask = cst[:, K_ONES:K_ONES + P], cst[:, K_IMASK:K_IMASK + 2 * P]
        slot_no = cst[:, K_SLOT:K_SLOT + SLOTS]
        cos = cst[:, K_COS:K_COS + 32].rearrange("p (t f) -> p t f", t=NT)
        sin = cst[:, K_SIN:K_SIN + 32].rearrange("p (t f) -> p t f", t=NT)

        pj_rest = work[:, :].rearrange("p (t c) -> p t c", t=NT)

        def proj(c, cols):
            return u[:, :, c:c + cols] if c < DM else pj_rest[:, :, c - DM:c - DM + cols]

        scratch = dn_ring[:, :, :].rearrange("p s c -> p (s c)")
        at = [0]

        def take(n):
            at[0] += n
            assert at[0] <= RING * 2048
            return scratch[:, at[0] - n:at[0]]

        space0, space1, spaceT = take(1024), take(2048), take(3072)
        rel0 = space0.rearrange("p (h s) -> p h s", h=IH)
        rel1 = space1.rearrange("p (h s) -> p h s", h=IH)
        prob0 = space0.rearrange("p (h s) -> p h s", h=NH)
        prob1 = space1.rearrange("p (h s) -> p h s", h=NH)
        probT = spaceT.rearrange("p (h c) -> p h c", h=NH)
        sq = spaceT[:, 0:1024].rearrange("p (t c) -> p t c", t=NT)
        rope_tmp = spaceT[:, 1024:2048]
        qiT = spaceT[:, 2048:3072].rearrange("p (j t) -> p j t", j=IH // 2)
        kiT = take(256)
        ki2 = take(256).rearrange("p (t c) -> p t c", t=NT)
        score = [take(128), take(256)]
        bias = [take(128), take(256)]
        at[0] = 0
        kT_b = take(2048).rearrange("p (h t) -> p h t", h=NH)
        v_b = take(2048).rearrange("p (t c) -> p t c", t=NT)
        att = take(3072).rearrange("p (h c) -> p h c", h=NH)
        absz = [work[:, 384 * j:384 * j + 384] for j in range(2)]
        lb = [work[:, 768 + 384 * j:1152 + 384 * j] for j in range(2)]
        u_flat = u[:, :, :].rearrange("p t c -> p (t c)")
        lk = [u_flat[:, 384 * j:384 * j + 384] for j in range(2)]
        neg = [u_flat[:, 768 + 384 * j:1152 + 384 * j] for j in range(2)]
        d_silu = work[:, 0:1024].rearrange("p (b f c) -> p b f c", b=2, f=2)
        d_raw = work[:, 1024:2048].rearrange("p (b f c) -> p b f c", b=2, f=2)
        d_hi = hid_hi[:, :].rearrange("p (f c) -> p f c", f=2)
        d_lo = hid_lo[:, :].rearrange("p (f c) -> p f c", f=2)
        m_silu = work[0:SLOTS, 0:768].rearrange("p (b c) -> p b c", b=3)
        m_raw = work[0:SLOTS, 768:1536].rearrange("p (b c) -> p b c", b=3)
        m_pick = work[:, 1536:1536 + NT * SLOTS].rearrange("p (t c) -> p t c", t=NT)
        m_pickT = work[0:SLOTS, 1792:1792 + TOK]
        q_flat = q_T[:, :, :].rearrange("p h t -> p (h t)")
        m_y = q_flat[0:SLOTS, 0:DM]
        m_u = q_flat[:, DM:DM + KD * SLOTS]
        m_u_hi = uT_hi[:, :, :].rearrange("p k t -> p (k t)")[:, 0:KD * SLOTS]
        m_u_lo = uT_lo[:, :, :].rearrange("p k t -> p (k t)")[:, 0:KD * SLOTS]
        m_hT_hi = hid_hi[:, 0:4 * SLOTS].rearrange("p (b f c) -> p b f c", b=2, f=2)
        m_hT_lo = hid_lo[:, 0:4 * SLOTS].rearrange("p (b f c) -> p b f c", b=2, f=2)

        pair = [ctx.enter_context(nc.psum_tensor(f"pair{i}", [P, 1024], f32)) for i in range(4)]
        step_bank = (0, 1, 7)
        bank = [pair[i // 2][:, 512 * (i % 2):512 * (i % 2) + 512] for i in range(8)]

        consts_in, x_in, rows_in, qkw_in, router_in = (sem(n) for n in
            ("consts_in", "x_in", "rows_in", "qkw_in", "router_in"))
        up_in = [sem(f"up_in{s}") for s in range(RING)]
        dn_in = [sem(f"dn_in{s}") for s in range(RING)]
        up_h, up_l, up_used = sem("up_h"), sem("up_l"), sem("up_used")
        dn_h, dn_l, dn_used = sem("dn_h"), sem("dn_l"), sem("dn_used")
        router_h, router_l = sem("router_h"), sem("router_l")
        nw_ps, nw_done = sem("nw_ps"), sem("nw_done")
        h_done = sem("h_done")
        sumsq, ms_done, root_done, u_done = sem("sumsq"), sem("ms_done"), sem("root_done"), sem("u_done")
        uT_ps, uT_h, uT_l = sem("uT_ps"), sem("uT_h"), sem("uT_l")
        proj_ps, proj_sb = sem("proj_ps"), sem("proj_sb")
        idx_roped, idx_T, idx_T_sb = sem("idx_roped"), sem("idx_T"), sem("idx_T_sb")
        idx_qk, rel_done = sem("idx_qk"), sem("rel_done")
        qk_sq, qk_ms, qk_root, qk_roped = sem("qk_sq"), sem("qk_ms"), sem("qk_root"), sem("qk_roped")
        qk_T, qk_T_sb = sem("qk_T"), sem("qk_T_sb")
        logits_ps, rowmax_done, exp_done, prob_done = sem("logits_ps"), sem("rowmax_done"), sem("exp_done"), sem("prob_done")
        probT_ps, probT_sb = sem("probT_ps"), sem("probT_sb")
        o_ps, o_h, o_l = sem("o_ps"), sem("o_h"), sem("o_l")
        res_ps = sem("res_ps")
        dve_chain = sem("dve_chain")
        silu_done, hid_raw, hid_h, hid_l = sem("silu_done"), sem("hid_raw"), sem("hid_h"), sem("hid_l")
        bk_sb, bq_sb = sem("bk_sb"), sem("bq_sb")
        z_ps, z_log, keep_raw, keep_done = sem("z_ps"), sem("z_log"), sem("keep_raw"), sem("keep_done")
        after_ps, expo_done, stick_raw, stick_done = sem("after_ps"), sem("expo_done"), sem("stick_raw"), sem("stick_done")
        v_ps, v_sb = sem("v_ps"), sem("v_sb")
        route_ps, route_top, route_exp, sel_done = sem("route_ps"), sem("route_top"), sem("route_exp"), sem("sel_done")
        rank_ps, jobs_known = sem("rank_ps"), sem("jobs_known")
        e_silu, e_raw, e_hT, e_hT_h, e_hT_l = sem("e_silu"), sem("e_raw"), sem("e_hT"), sem("e_hT_h"), sem("e_hT_l")
        e_y_act, e_y_dve = sem("e_y_act"), sem("e_y_dve")
        e_pick, e_pickT, e_pickT_sb = sem("e_pick"), sem("e_pickT"), sem("e_pickT_sb")
        e_gather, e_u, e_u_h, e_u_l = sem("e_gather"), sem("e_u"), sem("e_u_h"), sem("e_u_l")
        e_scatter, e_added, out_done = sem("e_scatter"), sem("e_added"), sem("out_done")

        block = ctx.enter_context(nc.Block())

        def up_tile(n, cols=512):
            return up_ring[:, n % RING, 0:KD * cols].rearrange("p (k c) -> p k c", k=KD)

        def ffn_up(s):
            return up_ring[:, s, :].rearrange("p (k g c) -> p k g c", k=KD, g=2)

        def ffn_dn(s):
            return dn_ring[:, s, :].rearrange("p (b n) -> p b n", b=2)

        def up_arrived(n):
            return 16 * sum(2 if T_DENSE <= m < T_DENSE + STEPS else 1 for m in range(n % RING, n + 1, RING))

        def dn_arrived(n):
            return 16 * (n // RING + 1)

        def job_arrived(first, i, k, before_jobs, transfers):
            slot = [(first + j) % RING for j in range(STEPS)]
            return k * (16 * transfers * slot.count(slot[i])) + (before_jobs + 16 * transfers * slot[:i + 1].count(slot[i]))

        def job_up_arrived(i, k):
            last = max(n for n in range(T_MOE) if n % RING == (T_MOE + i) % RING)
            return job_arrived(T_MOE, i, k, up_arrived(last), 2)

        def job_dn_arrived(i, k):
            last = max(n for n in range(STEPS) if n % RING == (STEPS + i) % RING)
            return job_arrived(STEPS, i, k, dn_arrived(last), 1)

        def job_free(first, i, k):
            last_user = i - RING if i >= RING else max(range(i, STEPS, RING)) - STEPS
            return k * (2 * STEPS) + 2 * (first + last_user + 1)

        FIRST = 3
        DN_LATE = 2

        def step_buffer(i):
            return 2 if i % STEPS == STEPS - 1 else i % STEPS % 2

        def last_step_in_buffer(i):
            return max(j for j in range(-STEPS, i) if step_buffer(j) == step_buffer(i))

        def job_piece(first, i, p, k):
            return k * (2 * STEPS) + (2 * (first + i) + p)

        def buffer(ring, n, cols):
            return ring[:, n % 2, 0:cols]

        def raw_piece(n, cols=512):
            return up_ring[:, (n // 2) % RING, 4 * cols * (n % 2):4 * cols * (n % 2 + 1)]

        def piece_cols(n):
            return IN_COLS[n // 2][1] if n < 2 * T_OUT else 512

        AHEAD = 2

        @block.sync
        def _(sp):
            sp.dma_start(h[:, :, :], x[0].rearrange("(t p) d -> p t d", p=P)).then_inc(x_in, 16)

            def columns(n, w, c0, cols=512):
                if n >= RING:
                    sp.wait_ge(up_l, 2 * (n - RING + 1))
                sp.dma_start(up_tile(n, cols), w.rearrange("(k p) c -> p k c", p=P)[:, :, c0:c0 + cols])\
                  .then_inc(up_in[n % RING], 16)

            for j, (c, cols) in enumerate(IN_COLS):
                columns(T_IN + j, a_w_in[0], c, cols)
            for j in range(2):
                columns(T_OUT + j, a_w_out[0], 512 * j)

            dup = dense_w_gate_up[0].rearrange("(k p) (g c) -> p k g c", p=P, g=2)
            ddn = dense_w_down[0].rearrange("(b p) n -> p b n", p=P)
            for i in range(STEPS + AHEAD):
                if i < STEPS:
                    n = T_DENSE + i
                    sp.wait_ge(up_l, 2 * (n - RING + 1))
                    for g in range(2):
                        sp.dma_start(ffn_up(n % RING)[:, :, g, :], dup[:, :, g, FSTEP * i:FSTEP * (i + 1)])\
                          .then_inc(up_in[n % RING], 16)
                m = i - AHEAD
                if m == 0:
                    sp.wait_ge(o_ps, 2)
                if m >= RING:
                    sp.wait_ge(dn_l, 2 * (m - RING + 1))
                if m >= 0:
                    sp.dma_start(ffn_dn(m % RING), ddn[:, 2 * m:2 * m + 2, :]).then_inc(dn_in[m % RING], 16)

            for first, w, c0 in ((T_BQ, b_w_q[0], 0), (T_BK, kv_w, 0), (T_BV, kv_w, DM), (T_BO, b_w_out[0], 0)):
                for j in range(2):
                    columns(first + j, w, c0 + 512 * j)

            eup = moe_w_gate_up[0].rearrange("e (k p) (g c) -> e p k g c", p=P, g=2)
            edn = moe_w_down[0].rearrange("e (b p) n -> e p b n", p=P)

            def expert_up(i, e):
                s = (T_MOE + i) % RING
                for g in range(2):
                    src = eup[bass.ds(e, 1), :, :, g, FSTEP * i:FSTEP * (i + 1)]
                    sp.dma_start(ffn_up(s)[:, :, g, :], src.rearrange("e p k c -> (e p) k c")).then_inc(up_in[s], 16)

            def expert_dn(i, e):
                s = (STEPS + i) % RING
                sp.dma_start(ffn_dn(s), edn[bass.ds(e, 1), :, 2 * i:2 * i + 2, :].rearrange("e p b n -> (e p) b n")).then_inc(dn_in[s], 16)

            for i in range(RING):
                sp.wait_ge(up_l, 2 * (T_MOE + i - RING + 1))
                expert_up(i, 0)
                m = i - DN_LATE
                if m == 0:
                    sp.wait_ge(o_ps, 4)
                if m >= 0:
                    sp.wait_ge(dn_l, 2 * (STEPS + m - RING + 1))
                    expert_dn(m, 0)

            def job(k, e, next_e, last=False):
                for i in range(RING, STEPS + RING):
                    if i < STEPS or not last:
                        sp.wait_ge(up_l, job_free(T_MOE, i % STEPS, k + i // STEPS))
                        expert_up(i % STEPS, e if i < STEPS else next_e)
                    m = i - DN_LATE
                    if m < STEPS or not last:
                        sp.wait_ge(dn_l, job_free(STEPS, m % STEPS, k + m // STEPS))
                        expert_dn(m % STEPS, e if m < STEPS else next_e)

            with sp.Fori(0, NEXP - 1) as k:
                job(k, k, k + 1)
            sp.wait_ge(jobs_known, 1)
            last_job = sp.value_load(n_last_job[0:1, 0:1], min_val=NEXP - 1, max_val=JOBS - 1)
            with sp.If(last_job > NEXP - 1):
                for c in range(1, CHUNKS):
                    job(c * NEXP - 1, NEXP - 1, 0)
                    with sp.Fori(0, NEXP - 1) as e:
                        job(e + c * NEXP, e, e + 1)
            job(last_job, NEXP - 1, None, last=True)
            for t in range(NT):
                sp.wait_ge(e_added, last_job * NT + (NT + t + 2))
                sp.dma_start(out[0, P * t:P * t + P, :], h[:, t, :]).then_inc(out_done, 16)
            sp.wait_ge(out_done, 16 * NT)

        @block.tensor
        def _(pe):
            def uT_blocks(n):
                for t in range(NT):
                    pe.wait_ge(u_done, NT * n + t + 1)
                    for k in range(KD):
                        c = 256 * (k % 2) + P * t
                        mm = pe.transpose(bank[4 + k // 2][:, c:c + P], u[:, t, P * k:P * k + P], ident)
                        if t == NT - 1 and k % 2 == 1:
                            mm.then_inc(uT_ps, 1)

            def product(ps, a_hi, a_lo, b_hi, b_lo, start, stop, shared=False):
                pe.matmul(ps, a_hi, b_hi, start=start, stop=False, skip_group_check=shared)
                pe.matmul(ps, a_hi, b_lo, start=False, stop=False, skip_group_check=shared)
                return pe.matmul(ps, a_lo, b_hi, start=False, stop=stop, skip_group_check=shared)

            def token_columns(n, t, ps, cols=512):
                hi, lo = (buffer(b, n, 4 * cols).rearrange("p (k c) -> p k c", k=4) for b in (up_hi, up_lo))
                for j in range(4):
                    k = 4 * (n % 2) + j
                    mm = product(ps[:, 0:cols], uT_hi[:, k, P * t:P * t + P], uT_lo[:, k, P * t:P * t + P],
                                 hi[:, j, :], lo[:, j, :], k == 0, k == KD - 1)
                return mm

            def residual_product(n0, first_bank):
                for n in range(2 * n0, 2 * n0 + 4):
                    half = n // 2 - n0
                    pe.wait_ge(up_l, n + 1)
                    for t in range(NT):
                        mm = token_columns(n, t, bank[first_bank + 2 * t + half])
                        if t == 0 and n % 2 == 1:
                            mm.then_inc(res_ps, 1)
                    mm.then_inc(up_used, 1)

            pe.wait_ge(consts_in, 16)
            pe.wait_ge(rows_in, 16 * 5)
            pe.transpose(bank[0][:, 0:5 * KD], norm_rows[:, :], ident[0:5 * KD, 0:5 * KD]).then_inc(nw_ps, 1)

            uT_blocks(0)

            def project(j):
                cols = IN_COLS[j][1]
                for n in (2 * j, 2 * j + 1):
                    pe.wait_ge(up_l, n + 1)
                    if n < 2:
                        pe.wait_ge(uT_l, 2 * n + 2)
                    if n == 0:
                        pe.wait_ge(nw_done, 1)
                    for t in range(NT):
                        use = NT * j + t
                        if use >= 4 and n % 2 == 0:
                            pe.wait_ge(proj_sb, use - 3)
                        mm = token_columns(n, t, bank[use % 4], cols)
                        if t == 0 and n % 2 == 1:
                            mm.then_inc(proj_ps, 1)
                    mm.then_inc(up_used, 1)

            project(0)
            project(1)
            project(2)
            pe.wait_ge(idx_roped, 1)
            for j in range(IH // 2):
                for t in range(NT):
                    c = 256 * (j % 2) + P * t
                    pe.transpose(bank[4 + j // 2][:, c:c + P], proj(C_QI + P * j, P)[:, t, :], ident)
            for t in range(NT):
                mm = pe.transpose(bank[6][:, P * t:P * t + P], ki2[:, t, :], ident)
            mm.then_inc(idx_T, 1)
            project(3)

            def index_scores(t, heads, first_bank):
                keys = P * (t + 1)
                for n, i in enumerate(heads):
                    part = slice(ID * (i % 2), ID * (i % 2) + ID)
                    c = (n // 2) * keys
                    mm = pe.matmul(bank[first_bank + i % 2][:, c:c + keys], qiT[part, i // 2, P * t:P * t + P],
                                   kiT[part, 0:keys], start=True, stop=True)
                mm.then_inc(idx_qk, 1)

            pe.wait_ge(idx_T_sb, 3)
            index_scores(0, range(8), 4)
            index_scores(1, range(4), 6)
            pe.wait_ge(rel_done, 2)
            index_scores(1, range(4, 8), 4)
            project(4)

            for n, ps in enumerate((bank[4], bank[5], bank[6], bank[7], bank[0])):
                if n == 0:
                    pe.wait_ge(rel_done, 6)
                if n == 4:
                    pe.wait_ge(proj_sb, 9)
                pe.wait_ge(qk_roped, (1, 2, 2, 3, 3)[n])
                c0 = C_K if n == 0 else 2 * HD * (n - 1)
                for i in range(2):
                    for t in range(NT):
                        mm = pe.transpose(ps[:, 256 * i + P * t:256 * i + P * t + P],
                                          proj(c0 + HD * i, HD)[:, t, :], ident)
                mm.then_inc(qk_T, 1)

            pe.wait_ge(qk_T_sb, 5)
            pe.wait_ge(proj_sb, 10)
            for i in range(NH):
                mm = pe.matmul(pair[1][:, P * i:P * i + P], q_T[:, i, 0:P], kT_a[:, i // GROUP, 0:P],
                               start=True, stop=True)
            mm.then_inc(logits_ps, 1)
            for i in range(NH):
                mm = pe.matmul(pair[2 + i // 4][:, TOK * (i % 4):TOK * (i % 4) + TOK], q_T[:, i, P:TOK],
                               kT_a[:, i // GROUP, :], start=True, stop=True)
                if i % 4 == 3:
                    mm.then_inc(logits_ps, 1)
            for g in range(3):
                pe.wait_ge(prob_done, g + 1)
                for i in range(8):
                    src = prob0[:, i, :] if g == 0 else prob1[:, 4 * (g - 1) + i // 2, P * (i % 2):P * (i % 2) + P]
                    mm = pe.transpose(pair[g][:, P * i:P * i + P], src, ident)
                mm.then_inc(probT_ps, 1)

            def weighted_values(weightsT, value, pairs):
                for i in range(NH):
                    ps = pair[pairs[i // 4]][:, TOK * (i % 4):TOK * (i % 4) + TOK]
                    pe.matmul(ps, value(0, i), weightsT[:, i, 0:TOK], start=True, stop=False)
                    mm = pe.matmul(ps[:, P:TOK], value(1, i), weightsT[:, i, TOK:TOK + P], start=False, stop=True)
                    if i % 4 == 3:
                        mm.then_inc(o_ps, 1)

            pe.wait_ge(probT_sb, 3)
            weighted_values(probT, lambda t, i: proj(C_V + HD * (i // GROUP), HD)[:, t, :], (3, 0))
            pe.wait_ge(o_l, 2)
            residual_product(T_OUT, 2)

            uT_blocks(1)

            def columns_tokens(n, p0, c0s):
                hi, lo = (buffer(b, n, 2048).rearrange("p (k c) -> p k c", k=4) for b in (up_hi, up_lo))
                for b, c0 in enumerate(c0s):
                    for j in range(4):
                        k = 4 * (n % 2) + j
                        mm = product(pair[p0][:, TOK * b:TOK * b + TOK], hi[:, j, c0:c0 + P], lo[:, j, c0:c0 + P],
                                     uT_hi[:, k, :], uT_lo[:, k, :], k == 0 and b % 2 == 0, k == KD - 1, shared=True)
                mm.then_inc(up_used, 1)

            def dense_up(i):
                for n in (2 * (T_DENSE + i), 2 * (T_DENSE + i) + 1):
                    pe.wait_ge(up_l, n + 1)
                    if i == 0:
                        pe.wait_ge(uT_l, 4 + 2 * (n % 2) + 2)
                    if i >= 2 and n % 2 == 0:
                        pe.wait_ge(hid_raw, i - 1)
                    columns_tokens(n, i % 2, (0, FSTEP, P, FSTEP + P))

            def dense_dn(i):
                for f in range(2):
                    n = 2 * i + f
                    pe.wait_ge(dn_l, n + 1)
                    if f == 0:
                        pe.wait_ge(hid_l, i + 1)
                    for t in range(NT):
                        for half in range(2):
                            c = slice(512 * half, 512 * half + 512)
                            mm = product(bank[4 + 2 * t + half], d_hi[:, f, P * t:P * t + P], d_lo[:, f, P * t:P * t + P],
                                         buffer(dn_hi, n, DM)[:, c], buffer(dn_lo, n, DM)[:, c], n == 0, n == 2 * STEPS - 1)
                    mm.then_inc(dn_used, 1)

            for i in range(STEPS):
                dense_up(i)
                if i > 0:
                    dense_dn(i - 1)
            dense_dn(STEPS - 1)

            uT_blocks(2)
            for j in range(4):
                for n in (2 * (T_BQ + j), 2 * (T_BQ + j) + 1):
                    pe.wait_ge(up_l, n + 1)
                    if j == 0:
                        pe.wait_ge(uT_l, 8 + 2 * (n % 2) + 2)
                    if j == 2 and n % 2 == 0:
                        pe.wait_ge(uT_l, 16)
                    columns_tokens(n, j, (0, HD, 2 * HD, 3 * HD))

            def sticks_z(i):
                if i >= 2:
                    pe.wait_ge(keep_raw, i - 1)
                ps = bank[i % 2]
                pe.matmul(ps[:, 0:TOK], kT_b[:, i, 0:P], q_T[:, i, :], start=True, stop=True)
                pe.matmul(ps[:, TOK:TOK + P], kT_b[:, i, P:TOK], q_T[:, i, P:TOK], start=True, stop=True)\
                  .then_inc(z_ps, 1)

            def sticks_after(i):
                pe.wait_ge(keep_done, i + 1)
                if i >= 2:
                    pe.wait_ge(expo_done, i - 1)
                ps, src = bank[2 + i % 2], lk[i % 2]
                pe.matmul(ps[:, 0:TOK], after, src[:, 0:TOK], start=True, stop=False)
                pe.matmul(ps[:, P:TOK], ones, src[:, TOK:TOK + P], start=False, stop=True)
                pe.matmul(ps[:, TOK:TOK + P], after, src[:, TOK:TOK + P], start=True, stop=True).then_inc(after_ps, 1)

            def values(j):
                n = 2 * T_BV + j
                pe.wait_ge(up_l, n + 1)
                for t in range(NT):
                    mm = token_columns(n, t, bank[4 + 2 * t + j // 2])
                    if t == 0 and n % 2 == 1:
                        mm.then_inc(v_ps, 1)
                mm.then_inc(up_used, 1)

            pe.wait_ge(bk_sb, 2)
            pe.wait_ge(bq_sb, 2)
            sticks_z(0)
            sticks_z(1)
            for j in range(4):
                values(j)
                for i in (2 * j, 2 * j + 1):
                    sticks_after(i)
                    if i + 2 < NH:
                        sticks_z(i + 2)
            pe.wait_ge(stick_done, NH)
            pe.wait_ge(v_sb, 4)
            weighted_values(att, lambda t, i: v_b[:, t, HD * i:HD * i + HD], (0, 1))
            pe.wait_ge(o_l, 4)
            residual_product(T_BO, 4)

            uT_blocks(3)
            pe.wait_ge(uT_l, 20)
            pe.wait_ge(router_l, 1)
            for t in range(NT):
                for k in range(KD):
                    c = slice(NEXP * k, NEXP * k + NEXP)
                    mm = product(bank[0][:, NEXP * t:NEXP * t + NEXP], uT_hi[:, k, P * t:P * t + P], uT_lo[:, k, P * t:P * t + P],
                                 router_hi[:, c], router_lo[:, c], k == 0, k == KD - 1)
            mm.then_inc(route_ps, 1)
            pe.wait_ge(sel_done, 1)
            routed = rt[:, 5]
            pe.matmul(bank[1][:, 0:8], before, routed[:, 0, :], start=True, stop=True)
            pe.matmul(bank[1][:, 8:16], ones, routed[:, 0, :], start=True, stop=False)
            pe.matmul(bank[1][:, 8:16], before, routed[:, 1, :], start=False, stop=True)
            pe.matmul(bank[1][:, 16:24], ones, routed[:, 0, :], start=True, stop=False)
            pe.matmul(bank[1][:, 16:24], ones, routed[:, 1, :], start=False, stop=True).then_inc(rank_ps, 1)

            def gather(j):
                pe.wait_ge(e_pick, j * 2 + 1)
                for b in range(KD):
                    for t in range(NT):
                        c = SLOTS * (b % 4)
                        mm = pe.matmul(bank[4 + b // 4][:, c:c + SLOTS], u[:, t, P * b:P * b + P], m_pick[:, t, :],
                                       start=(t == 0), stop=(t == NT - 1))
                mm.then_inc(e_gather, 1)

            def scatter(k, t):
                if t == 0:
                    pe.wait_ge(e_y_act, k + 1)
                    pe.wait_ge(e_y_dve, k + 1)
                    pe.wait_ge(e_pickT_sb, k + 1)
                else:
                    pe.wait_ge(e_added, k * NT + 2)
                for half in range(2):
                    c = slice(512 * half, 512 * half + 512)
                    mm = pe.matmul(pair[2][:, c], m_pickT[:, P * t:P * t + P], m_y[:, c], start=True, stop=True)
                mm.then_inc(e_scatter, 1)

            def expert_up(k, i):
                for p in range(2):
                    pe.wait_ge(up_l, job_piece(T_MOE, i, p + 1, k))
                    if i % STEPS == 0 and p == 0:
                        pe.wait_ge(e_u_l, k + (i // STEPS + 1))
                    if i >= 2 and p == 0:
                        if i == STEPS - 1:
                            pe.wait_ge(e_pickT_sb, k + 2)
                        else:
                            pe.wait_ge(e_raw, k * STEPS + (last_step_in_buffer(i) + 1))
                    hi, lo = (buffer(b, p, 2048).rearrange("p (k c) -> p k c", k=4) for b in (up_hi, up_lo))
                    for j in range(4):
                        c = slice(SLOTS * (4 * p + j), SLOTS * (4 * p + j + 1))
                        mm = product(bank[step_bank[step_buffer(i)]][0:SLOTS, :], m_u_hi[:, c], m_u_lo[:, c],
                                     hi[:, j, :], lo[:, j, :], p == 0 and j == 0, p == 1 and j == 3)
                    mm.then_inc(up_used, 1)

            def hidden_T(k, i):
                pe.wait_ge(e_raw, k * STEPS + (i + 1))
                if i > 0:
                    pe.wait_ge(e_hT_l, k * STEPS + i)
                for f in range(2):
                    mm = pe.transpose(bank[6][:, SLOTS * f:SLOTS * f + SLOTS], m_raw[:, step_buffer(i), P * f:P * f + P],
                                      ident[0:SLOTS, 0:SLOTS])
                mm.then_inc(e_hT, 1)

            def expert_dn(k, i):
                for f in range(2):
                    pe.wait_ge(dn_l, job_piece(STEPS, i, f + 1, k))
                    if f == 0:
                        pe.wait_ge(e_hT_l, k * STEPS + (i + 1))
                    if i % STEPS == 0 and f == 0:
                        pe.wait_ge(e_y_act, k + (i // STEPS + 1))
                        pe.wait_ge(e_y_dve, k + (i // STEPS + 1))
                    for half in range(2):
                        c = slice(512 * half, 512 * half + 512)
                        mm = product(pair[1][0:SLOTS, c], m_hT_hi[:, i % STEPS % 2, f, :], m_hT_lo[:, i % STEPS % 2, f, :],
                                     buffer(dn_hi, f, DM)[:, c], buffer(dn_lo, f, DM)[:, c],
                                     i % STEPS == 0 and f == 0, i % STEPS == STEPS - 1 and f == 1)
                    mm.then_inc(dn_used, 1)

            def iteration(k, i, last=False):
                if i < STEPS or not last:
                    expert_up(k, i)
                if i == 3:
                    scatter(k, 0)
                if i == 5:
                    scatter(k, 1)
                if i == 6:
                    pe.wait_ge(e_pick, k * 2 + 2)
                    for t in range(NT):
                        mm = pe.transpose(bank[7][0:SLOTS, P * t:P * t + P], m_pick[:, t, :], ident)
                    mm.then_inc(e_pickT, 1)
                if i == 8 and not last:
                    pe.wait_ge(e_added, k * NT + 3)
                    gather(k + 1)
                if i >= 1 and (i - 1 < STEPS or not last):
                    hidden_T(k, i - 1)
                if i >= DN_LATE and (i - DN_LATE < STEPS or not last):
                    expert_dn(k, i - DN_LATE)

            def job(k, last=False):
                for i in range(FIRST, STEPS + FIRST):
                    iteration(k, i, last)

            gather(0)
            for i in range(FIRST):
                iteration(0, i)
            with pe.Fori(0, NEXP - 1) as k:
                job(k)
            pe.wait_ge(jobs_known, 1)
            last_job = pe.value_load(n_last_job[0:1, 0:1], min_val=NEXP - 1, max_val=JOBS - 1)
            with pe.If(last_job > NEXP - 1):
                with pe.Fori(NEXP - 1, JOBS - 1) as k:
                    job(k)
            job(last_job, last=True)
            pe.wait_ge(e_added, last_job * NT + (NT + 1))
            scatter(last_job + 1, 0)
            scatter(last_job + 1, 1)

        @block.scalar
        def _(act):
            act.dma_start(cst[:, :], consts).then_inc(consts_in, 16)
            for r, w in enumerate((a_norm_w[0], ffn_norm_w[0], kv_norm_w, b_norm_w[0], ffn_norm_w[1])):
                act.dma_start(norm_rows[KD * r:KD * r + KD, :], w.rearrange("(k c) -> k c", c=P)).then_inc(rows_in, 16)
            act.dma_start(qk_w[:, 0, :], a_q_norm_w[0].partition_broadcast(P)).then_inc(qkw_in, 16)
            act.dma_start(qk_w[:, 1, :], a_k_norm_w[0].partition_broadcast(P)).then_inc(qkw_in, 16)
            act.dma_start(router[:, :, :], moe_router_w[0].rearrange("(k p) e -> p k e", p=P)).then_inc(router_in, 16)

            def copy(out_, in_, scale=1.0):
                return act.activation(out_, in_, ACT.Copy, scale=scale)

            def up_piece(n):
                if n % 2 == 0:
                    act.wait_ge(up_in[(n // 2) % RING], up_arrived(n // 2))
                if n >= 2:
                    act.wait_ge(up_used, n - 1)
                cols = piece_cols(n)
                copy(buffer(up_hi, n, 4 * cols), raw_piece(n, cols)).then_inc(up_h, 1)

            def dn_piece(n):
                if n % 2 == 0:
                    act.wait_ge(dn_in[(n // 2) % RING], dn_arrived(n // 2))
                if n >= 2:
                    act.wait_ge(dn_used, n - 1)
                copy(buffer(dn_hi, n, DM), ffn_dn((n // 2) % RING)[:, n % 2, :]).then_inc(dn_h, 1)

            def squares(n):
                for t in range(NT):
                    if n == 0:
                        if t == 0:
                            act.wait_ge(x_in, 16)
                    else:
                        act.wait_ge(h_done, 4 * n - 1 + t)
                    act.activation(u[:, t, :], h[:, t, :], ACT.Square, accum_out=stat[:, 2 * n + t:2 * n + t + 1])\
                       .then_inc(sumsq, 1)
                act.wait_ge(ms_done, n + 1)
                act.activation(stat[:, 8 + 2 * n:10 + 2 * n], stat[:, 8 + 2 * n:10 + 2 * n], ACT.Sqrt).then_inc(root_done, 1)

            def uT_part(ready, norm):
                for b in range(4):
                    act.wait_ge(uT_ps, ready + b + 1)
                    for k in (2 * b, 2 * b + 1):
                        c = 256 * (k % 2)
                        e = copy(uT_hi[:, k, :], bank[4 + b][:, c:c + TOK], nw[:, KD * norm + k:KD * norm + k + 1])
                    e.then_inc(uT_h, 1)

            def output_part(n, ps):
                act.wait_ge(o_ps, n + 1)
                copy(uT_hi[:, 4 * (n % 2):4 * (n % 2) + 4, :], pair[ps][:, :].rearrange("p (i t) -> p i t", i=4)).then_inc(o_h, 1)

            squares(0)
            up_piece(0)
            act.wait_ge(nw_done, 1)
            uT_part(0, NORM_A)
            up_piece(1)

            def proj_copy(j):
                c, cols = IN_COLS[j]
                for t in range(NT):
                    if t == 0:
                        act.wait_ge(proj_ps, j + 1)
                    else:
                        act.wait_ge(up_used, 2 * j + 2)
                    copy(proj(c, cols)[:, t, :], bank[(NT * j + t) % 4][:, 0:cols]).then_inc(proj_sb, 1)

            def qk_squares(g):
                c, n = ((C_K, 2), (0, 4), (512, 4))[g]
                act.wait_ge(proj_sb, (6, 8, 10)[g])
                if g > 0:
                    act.wait_ge(qk_ms, g)
                act.activation(sq[:, :, 0:HD * n], proj(c, HD * n), ACT.Square).then_inc(qk_sq, 1)
                act.wait_ge(qk_ms, g + 1)
                act.activation(qk_rs[:, g, :, 0:n], qk_rs[:, g, :, 0:n], ACT.Sqrt).then_inc(qk_root, 1)

            def relu_scores(n):
                act.wait_ge(idx_qk, n + 1)
                for odd in range(2):
                    ps = bank[(4, 6, 4)[n] + odd]
                    if n == 0:
                        dst, src = rel0[:, odd:8:2, :], ps.rearrange("p (i s) -> p i s", i=4)
                    else:
                        dst, src = rel1[:, 4 * (n - 1) + odd:4 * n:2, :], ps.rearrange("p (i s) -> p i s", i=2)
                    act.activation(dst, src, ACT.Relu, scale=ID ** -0.5).then_inc(rel_done, 1)

            up_piece(2)
            up_piece(3)
            proj_copy(0)
            up_piece(4)
            up_piece(5)
            proj_copy(1)
            up_piece(6)
            up_piece(7)
            proj_copy(2)
            act.wait_ge(idx_T, 1)
            for n in range(2):
                copy(qiT[:, 2 * n:2 * n + 2, :], bank[4 + n].rearrange("p (j t) -> p j t", j=2)).then_inc(idx_T_sb, 1)
            copy(kiT, bank[6][:, 0:TOK]).then_inc(idx_T_sb, 1)
            qk_squares(0)
            up_piece(8)
            up_piece(9)
            proj_copy(3)
            relu_scores(0)
            relu_scores(1)
            relu_scores(2)
            up_piece(10)
            up_piece(11)
            proj_copy(4)
            qk_squares(1)
            qk_squares(2)
            act.wait_ge(router_in, 16)
            copy(router_hi[:, :], router[:, :, :].rearrange("p k e -> p (k e)")).then_inc(router_h, 1)
            for n, ps in enumerate((bank[4], bank[5], bank[6], bank[7], bank[0])):
                act.wait_ge(qk_T, n + 1)
                dst = kT_a[:, :, :] if n == 0 else q_T[:, 2 * (n - 1):2 * n, :]
                copy(dst, ps.rearrange("p (i t) -> p i t", i=2)).then_inc(qk_T_sb, 1)
            for g in range(3):
                act.wait_ge(rowmax_done, g + 1)
                for i in range(8 if g == 0 else 4):
                    r = i if g == 0 else 8 + 4 * (g - 1) + i
                    row = prob0[:, i, :] if g == 0 else prob1[:, 4 * (g - 1) + i, :]
                    e = act.activation(row, row, ACT.Exp, bias=soft[:, 0, r:r + 1], accum_out=soft[:, 1, r:r + 1])
                e.then_inc(exp_done, 1)
            for g in range(3):
                act.wait_ge(probT_ps, g + 1)
                if g == 0:
                    copy(probT[:, :, 0:P], pair[0][:, :].rearrange("p (i s) -> p i s", i=8)).then_inc(probT_sb, 1)
                else:
                    copy(probT[:, 4 * (g - 1):4 * g, P:], pair[g][:, :].rearrange("p (i s) -> p i s", i=4)).then_inc(probT_sb, 1)
            output_part(0, 3)
            output_part(1, 0)
            up_piece(12)
            up_piece(13)

            squares(1)
            up_piece(14)
            uT_part(4, NORM_F0)
            up_piece(15)
            for i in range(STEPS):
                if i + 1 < STEPS:
                    for p in range(2):
                        up_piece(2 * (T_DENSE + i + 1) + p)
                act.wait_ge(up_used, 2 * (T_DENSE + i + 1))
                if i >= 2:
                    act.wait_ge(hid_raw, i - 1)
                gate = pair[i % 2][:, :].rearrange("p (f c) -> p f c", f=2)[:, :, 0:TOK]
                act.activation(d_silu[:, i % 2], gate, ACT.Silu).then_inc(silu_done, 1)
                dn_piece(2 * i)
                act.wait_ge(hid_raw, i + 1)
                if i >= 1:
                    act.wait_ge(dn_used, 2 * i)
                copy(d_hi[:, :, :], d_raw[:, i % 2]).then_inc(hid_h, 1)
                dn_piece(2 * i + 1)

            squares(2)
            n = 2 * T_BQ
            up_piece(n)
            uT_part(8, NORM_B)
            for m in range(1, 6):
                up_piece(n + m)
            act.wait_ge(up_used, 2 * T_BK)
            act.wait_ge(uT_l, 12)
            uT_part(8, NORM_KV)
            up_piece(n + 6)
            up_piece(n + 7)
            for j in range(2):
                act.wait_ge(up_used, 2 * (T_BK + j + 1))
                copy(kT_b[:, 4 * j:4 * j + 4, :], pair[2 + j][:, :].rearrange("p (i t) -> p i t", i=4)).then_inc(bk_sb, 1)
                up_piece(n + 8 + j)

            def log1p_exp(i):
                act.wait_ge(z_ps, i + 1)
                if i >= 2:
                    act.wait_ge(keep_raw, i - 1)
                b = absz[i % 2]
                act.activation(b, bank[i % 2][:, 0:384], ACT.Abs, scale=SCALE).then_inc(z_log, 1)
                act.wait_ge(z_log, 3 * i + 1)
                act.activation(b, b, ACT.Exp, scale=-1.0).then_inc(z_log, 1)
                act.wait_ge(z_log, 3 * i + 2)
                act.activation(b, b, ACT.Ln, bias=1.0).then_inc(z_log, 1)

            def stick_weights(i):
                act.wait_ge(expo_done, i + 1)
                act.activation(att[:, i, :], neg[i % 2], ACT.Exp).then_inc(stick_raw, 1)

            def values_copy(half):
                for t in range(NT):
                    if t == 0:
                        act.wait_ge(v_ps, half + 1)
                    else:
                        act.wait_ge(up_used, 2 * (T_BV + half + 1))
                    copy(v_b[:, t, 512 * half:512 * half + 512], bank[4 + 2 * t + half]).then_inc(v_sb, 1)

            for i in range(NH):
                log1p_exp(i)
                if i >= 1:
                    stick_weights(i - 1)
                if i % 2 == 1:
                    up_piece(n + 10 + i // 2)
                if i == 3:
                    values_copy(0)
            values_copy(1)
            stick_weights(NH - 1)
            output_part(2, 0)
            output_part(3, 1)
            up_piece(2 * T_BO + 2)
            up_piece(2 * T_BO + 3)

            squares(3)
            uT_part(12, NORM_F1)
            act.wait_ge(route_top, 1)
            for t in range(NT):
                e = act.activation(rt[:, 6, t, :], rt[:, 0, t, :], ACT.Exp, bias=rt[:, 9, t, 2:3])
            e.then_inc(route_exp, 1)

            def gathered(k):
                act.wait_ge(e_u, k + 1)
                act.wait_ge(up_used, job_piece(T_MOE, 0, 0, k))
                copy(m_u_hi, m_u).then_inc(e_u_h, 1)

            def up_half(k, i, p):
                if p == 0:
                    act.wait_ge(up_in[(T_MOE + i % STEPS) % RING], job_up_arrived(i % STEPS, k + i // STEPS))
                act.wait_ge(up_used, job_piece(T_MOE, i, p - 1, k))
                copy(buffer(up_hi, p, 2048), raw_piece(2 * (T_MOE + i % STEPS) + p)).then_inc(up_h, 1)

            def dn_step(k, i):
                for p in range(2):
                    if p == 0:
                        act.wait_ge(dn_in[(STEPS + i % STEPS) % RING], job_dn_arrived(i % STEPS, k + i // STEPS))
                    act.wait_ge(dn_used, job_piece(STEPS, i, p - 1, k))
                    copy(buffer(dn_hi, p, DM), ffn_dn((STEPS + i % STEPS) % RING)[:, p, :]).then_inc(dn_h, 1)

            def silu_step(k, i):
                b = step_buffer(i)
                act.wait_ge(up_used, job_piece(T_MOE, i, 2, k))
                if i >= 2 and b < 2:
                    act.wait_ge(e_raw, k * STEPS + (last_step_in_buffer(i) + 1))
                act.activation(m_silu[:, b], bank[step_bank[b]][0:SLOTS, 0:FSTEP], ACT.Silu).then_inc(e_silu, 1)

            def hidden_step(k, i):
                act.wait_ge(e_hT, k * STEPS + (i + 1))
                if i >= 2:
                    act.wait_ge(dn_used, job_piece(STEPS, i - (1 if i == STEPS else 2), 2, k))
                copy(m_hT_hi[:, i % STEPS % 2], bank[6][:, 0:2 * SLOTS].rearrange("p (f c) -> p f c", f=2)).then_inc(e_hT_h, 1)

            def result(k):
                act.wait_ge(dn_used, job_piece(STEPS, STEPS, 0, k))
                act.wait_ge(e_scatter, k * NT + 3)
                copy(m_y[:, 0:512], bank[2][0:SLOTS, :]).then_inc(e_y_act, 1)

            def iteration(k, i, last=False):
                for p in range(2):
                    if i < STEPS or not last:
                        up_half(k, i, p)
                    if i == STEPS and p == 0 and not last:
                        gathered(k + 1)
                if i == STEPS + 2:
                    result(k)
                if i >= 1 and (i - 1 < STEPS or not last):
                    silu_step(k, i - 1)
                if i >= DN_LATE and (i - DN_LATE < STEPS or not last):
                    hidden_step(k, i - DN_LATE)
                    dn_step(k, i - DN_LATE)
                if i == 7:
                    act.wait_ge(e_pickT, k + 1)
                    act.wait_ge(e_scatter, k * NT + 3)
                    copy(m_pickT, bank[7][0:SLOTS, 0:TOK]).then_inc(e_pickT_sb, 1)

            def job(k, last=False):
                act.activation(silu_of_one[:, :], ones[0:1, 0:1], ACT.Silu)
                for i in range(FIRST, STEPS + FIRST):
                    iteration(k, i, last)

            up_half(0, 0, 0)
            up_half(0, 0, 1)
            gathered(0)
            for i in range(1, FIRST):
                iteration(0, i)
            with act.Fori(0, NEXP - 1) as k:
                job(k)
            act.wait_ge(jobs_known, 1)
            last_job = act.value_load(n_last_job[0:1, 0:1], min_val=NEXP - 1, max_val=JOBS - 1)
            with act.If(last_job > NEXP - 1):
                with act.Fori(NEXP - 1, JOBS - 1) as k:
                    job(k)
            job(last_job, last=True)

        @block.gpsimd
        def _(pool):
            mask = before.unsqueeze(1).to_broadcast([P, 2, P])

            def diagonal(v):
                return v.rearrange("p (b c) -> p b c", b=3)[:, 0:3:2, :]

            pool.wait_ge(consts_in, 16)
            for i in range(NH + 1):
                if i < NH:
                    pool.wait_ge(keep_raw, i + 1)
                    pool.tensor_tensor(diagonal(lk[i % 2]), diagonal(lk[i % 2]), mask, ALU.mult).then_inc(keep_done, 1)
                if i >= 1:
                    pool.wait_ge(stick_raw, i)
                    pool.tensor_tensor(diagonal(att[:, i - 1, :]), diagonal(att[:, i - 1, :]), mask, ALU.mult)\
                        .then_inc(stick_done, 1)

        @block.vector
        def _(dve):
            marks = [0]

            def mark(ins):
                marks[0] += 1
                ins.then_inc(dve_chain, 1)
                return marks[0]

            def reads(n):
                dve.wait_ge(dve_chain, n)

            def normalise(n):
                dve.wait_ge(sumsq, NT * (n + 1))
                rs = stat[:, 8 + 2 * n:10 + 2 * n]
                dve.tensor_scalar(rs, stat[:, 2 * n:2 * n + 2], 1.0 / DM, EPS, ALU.mult, ALU.add).then_inc(ms_done, 1)
                dve.wait_ge(root_done, n + 1)
                reads(mark(dve.reciprocal(rs, rs)))
                for t in range(NT):
                    dve.tensor_scalar(u[:, t, :], h[:, t, :], rs[:, t:t + 1], None, ALU.mult).then_inc(u_done, 1)

            def up_piece(n):
                cols = piece_cols(n)
                dve.wait_ge(up_h, n + 1)
                dve.tensor_tensor(buffer(up_lo, n, 4 * cols), raw_piece(n, cols), buffer(up_hi, n, 4 * cols).bitcast(f32),
                                  ALU.subtract).then_inc(up_l, 1)

            def dn_piece(n):
                dve.wait_ge(dn_h, n + 1)
                dve.tensor_tensor(buffer(dn_lo, n, DM), ffn_dn((n // 2) % RING)[:, n % 2, :],
                                  buffer(dn_hi, n, DM).bitcast(f32), ALU.subtract).then_inc(dn_l, 1)

            def uT_part(m, norm):
                for b in range(4):
                    dve.wait_ge(uT_h, 4 * m + b + 1)
                    for k in (2 * b, 2 * b + 1):
                        c = 256 * (k % 2)
                        last = dve.scalar_tensor_tensor(uT_lo[:, k, :], bank[4 + b][:, c:c + TOK],
                                                        nw[:, KD * norm + k:KD * norm + k + 1],
                                                        uT_hi[:, k, :].bitcast(f32), ALU.mult, ALU.subtract)
                    last.then_inc(uT_l, 1)

            def output_part(n, ps):
                dve.wait_ge(o_h, n + 1)
                c = slice(4 * (n % 2), 4 * (n % 2) + 4)
                dve.tensor_tensor(uT_lo[:, c, :], pair[ps][:, :].rearrange("p (i t) -> p i t", i=4),
                                  uT_hi[:, c, :].bitcast(f32), ALU.subtract).then_inc(o_l, 1)

            def add_residual(first_bank, tile0, res0):
                for half in range(2):
                    for t in range(NT):
                        if t == 0:
                            dve.wait_ge(res_ps, res0 + half + 1)
                        else:
                            dve.wait_ge(up_used, 2 * (tile0 + half + 1))
                        c = slice(512 * half, 512 * half + 512)
                        dve.tensor_tensor(h[:, t, c], h[:, t, c], bank[first_bank + 2 * t + half], ALU.add).then_inc(h_done, 1)

            def rope(v, half, step):
                n = v.shape[2]
                shape = [P, NT, n, half]
                c = cos[:, :, 0:16:step].unsqueeze(2).to_broadcast(shape)
                s = sin[:, :, 0:16:step].unsqueeze(2).to_broadcast(shape)
                tmp = rope_tmp
                t1, t2, t3, t4 = (tmp[:, 256 * j:256 * j + NT * n * half].rearrange("p (t n f) -> p t n f", t=NT, n=n)
                                  for j in range(4))
                x1, x2 = v[:, :, :, 0:half], v[:, :, :, half:2 * half]
                dve.tensor_tensor(t1, x1, c, ALU.mult)
                dve.tensor_tensor(t2, x2, s, ALU.mult)
                dve.tensor_tensor(t3, x2, c, ALU.mult)
                reads(mark(dve.tensor_tensor(t4, x1, s, ALU.mult)))
                dve.tensor_tensor(x1, t1, t2, ALU.subtract)
                return dve.tensor_tensor(x2, t3, t4, ALU.add)

            dve.wait_ge(nw_ps, 1)
            dve.tensor_copy(nw[:, :], bank[0][:, 0:5 * KD]).then_inc(nw_done, 1)
            normalise(0)
            up_piece(0)
            dve.wait_ge(nw_done, 1)
            uT_part(0, NORM_A)
            for n in range(1, 6):
                up_piece(n)

            dve.wait_ge(proj_sb, 4)
            reads(mark(rope(proj(C_QI, C_WI - C_QI).rearrange("p t (n d) -> p t n d", d=ID), ID // 8, 2)))
            for t in range(NT):
                dve.tensor_copy(ki2[:, t, :].rearrange("p (r d) -> p r d", r=2),
                                proj(C_KI, ID)[:, t, :].unsqueeze(1).to_broadcast([P, 2, ID]))
            dve.tensor_scalar(w_idx[:, :, :], proj(C_WI, IH), IH ** -0.5, None, ALU.mult).then_inc(idx_roped, 1)
            up_piece(6)
            up_piece(7)

            def qk_norm(g):
                c, n = ((C_K, 2), (0, 4), (512, 4))[g]
                v = proj(c, HD * n).rearrange("p t (n d) -> p t n d", d=HD)
                dve.wait_ge(qk_sq, g + 1)
                reads(mark(dve.tensor_reduce(qk_ss[:, g, :, 0:n], sq[:, :, 0:HD * n].rearrange("p t (n d) -> p t n d", d=HD),
                                             AX.X, ALU.add)))
                rs = qk_rs[:, g, :, 0:n]
                dve.tensor_scalar(rs, qk_ss[:, g, :, 0:n], 1.0 / HD, EPS, ALU.mult, ALU.add).then_inc(qk_ms, 1)
                dve.wait_ge(qk_root, g + 1)
                reads(mark(dve.reciprocal(rs, rs)))
                for t in range(NT):
                    for i in range(n):
                        last = dve.scalar_tensor_tensor(v[:, t, i, :], v[:, t, i, :], qk_rs[:, g, t, i:i + 1],
                                                        qk_w[:, int(g == 0), :], ALU.mult, ALU.mult)
                reads(mark(last))
                rope(v, HD // 8, 1).then_inc(qk_roped, 1)

            dve.wait_ge(qkw_in, 32)
            qk_norm(0)
            up_piece(8)
            up_piece(9)

            dve.wait_ge(idx_roped, 1)
            dve.wait_ge(rel_done, 6)
            rel = (rel0, rel1)
            masks = (imask[:, P:2 * P], imask)
            done = [0, 0]
            for i in range(IH):
                for t in range(NT):
                    if i:
                        reads(done[t])
                    done[t] = mark(dve.scalar_tensor_tensor(score[t], rel[t][:, i, :], w_idx[:, t, i:i + 1],
                                                            masks[t] if i == 0 else score[t], ALU.mult, ALU.add))
            for _ in range(TOPK // 8):
                for t in range(NT):
                    reads(done[t])
                    done[t] = mark(dve.max(top8[:, t, :], score[t]))
                for t in range(NT):
                    reads(done[t])
                    done[t] = mark(dve.match_replace(score[t], top8[:, t, :], score[t], TAKEN))
            for t in range(NT):
                reads(done[t])
                done[t] = mark(dve.tensor_scalar(bias[t], score[t], 0.5 * (TAKEN + NOT_CAUSAL), MASKED, ALU.is_ge, ALU.mult))
            for t in range(NT):
                reads(done[t])
                own = bias[t][:, P * t:P * t + P]
                done[t] = mark(dve.tensor_tensor(own, own, imask[:, P:2 * P], ALU.add))
            up_piece(10)
            up_piece(11)
            qk_norm(1)
            qk_norm(2)
            dve.wait_ge(router_h, 1)
            dve.tensor_tensor(router_lo[:, :], router[:, :, :].rearrange("p k e -> p (k e)"),
                              router_hi[:, :].bitcast(f32), ALU.subtract).then_inc(router_l, 1)

            def group(g):
                return (prob0, 0, 8, 0) if g == 0 else (prob1[:, 4 * (g - 1):4 * g, :], 4 + 4 * g, 4, 1)

            for g in range(3):
                prob, r, n, t = group(g)
                dve.wait_ge(logits_ps, g + 1)
                reads(done[t])
                for b in range(2):
                    part = prob[:, b * n // 2:(b + 1) * n // 2, :]
                    last = dve.scalar_tensor_tensor(part, bank[2 * (g + 1) + b].rearrange("p (i s) -> p i s", i=n // 2), SCALE,
                                                    bias[t].unsqueeze(1).to_broadcast([P, n // 2, P * (t + 1)]),
                                                    ALU.mult, ALU.add)
                reads(mark(last))
                dve.tensor_reduce(soft[:, 0, r:r + n], prob, AX.X, ALU.max, negate=True).then_inc(rowmax_done, 1)
            for g in range(3):
                prob, r, n, t = group(g)
                dve.wait_ge(exp_done, g + 1)
                reads(mark(dve.reciprocal(soft[:, 2, r:r + n], soft[:, 1, r:r + n])))
                dve.tensor_tensor(prob, prob, soft[:, 2, r:r + n].unsqueeze(2).to_broadcast([P, n, P * (t + 1)]),
                                  ALU.mult).then_inc(prob_done, 1)
            output_part(0, 3)
            output_part(1, 0)
            up_piece(12)
            up_piece(13)
            add_residual(2, T_OUT, 0)

            dve.wait_ge(h_done, 4)
            normalise(1)
            up_piece(14)
            uT_part(1, NORM_F0)
            up_piece(15)
            for i in range(STEPS):
                if i + 1 < STEPS:
                    for p in range(2):
                        up_piece(2 * (T_DENSE + i + 1) + p)
                dve.wait_ge(silu_done, i + 1)
                if i >= 2:
                    dve.wait_ge(hid_h, i - 1)
                up = pair[i % 2][:, :].rearrange("p (f c) -> p f c", f=2)[:, :, TOK:2 * TOK]
                dve.tensor_tensor(d_raw[:, i % 2], d_silu[:, i % 2], up, ALU.mult).then_inc(hid_raw, 1)
                dn_piece(2 * i)
                dve.wait_ge(hid_raw, i + 1)
                dve.wait_ge(hid_h, i + 1)
                dve.tensor_tensor(d_lo, d_raw[:, i % 2], d_hi.bitcast(f32), ALU.subtract).then_inc(hid_l, 1)
                dn_piece(2 * i + 1)
            dve.wait_ge(dn_used, 2 * STEPS)
            for half in range(2):
                for t in range(NT):
                    c = slice(512 * half, 512 * half + 512)
                    dve.tensor_tensor(h[:, t, c], h[:, t, c], bank[4 + 2 * t + half], ALU.add).then_inc(h_done, 1)

            dve.wait_ge(h_done, 8)
            normalise(2)
            n = 2 * T_BQ
            up_piece(n)
            uT_part(2, NORM_B)
            for m in range(1, 6):
                up_piece(n + m)
            for j in range(2):
                dve.wait_ge(up_used, 2 * (T_BQ + j + 1))
                dve.tensor_copy(q_T[:, 4 * j:4 * j + 4, :], pair[j][:, :].rearrange("p (i t) -> p i t", i=4)).then_inc(bq_sb, 1)
            uT_part(3, NORM_KV)
            for m in range(6, 10):
                up_piece(n + m)

            def log_keep(i):
                z, b = bank[i % 2][:, 0:384], i % 2
                dve.wait_ge(z_ps, i + 1)
                dve.wait_ge(z_log, 3 * i + 3)
                reads(mark(dve.tensor_scalar(lb[b], z, SCALE, 0.0, ALU.mult, ALU.min)))
                reads(mark(dve.tensor_tensor(lb[b], lb[b], absz[b], ALU.subtract)))
                if i >= 2:
                    dve.wait_ge(after_ps, i - 1)
                dve.scalar_tensor_tensor(lk[b], z, -SCALE, lb[b], ALU.mult, ALU.add).then_inc(keep_raw, 1)

            def exponent(i):
                dve.wait_ge(after_ps, i + 1)
                if i >= 2:
                    dve.wait_ge(stick_raw, i - 1)
                dve.tensor_tensor(neg[i % 2], bank[2 + i % 2][:, 0:384], lb[i % 2], ALU.add).then_inc(expo_done, 1)

            log_keep(0)
            for i in range(NH):
                if i + 1 < NH:
                    log_keep(i + 1)
                exponent(i)
                if i % 2 == 0:
                    up_piece(n + 10 + i // 2)
            output_part(2, 0)
            output_part(3, 1)
            up_piece(2 * T_BO + 2)
            up_piece(2 * T_BO + 3)
            add_residual(4, T_BO, 2)

            dve.wait_ge(h_done, 12)
            normalise(3)
            uT_part(4, NORM_F1)
            lg, gt, eq, rank, fits, routed, ex, gate, need = (rt[:, j] for j in range(9))
            misc = rt[:, 9]
            wide = [P, NT, NEXP]
            dve.memset(m_y[:, 0:512], 0.0).then_inc(e_y_act, 1)
            dve.memset(m_y[:, 512:1024], 0.0).then_inc(e_y_dve, 1)
            dve.memset(m_pickT, 0.0).then_inc(e_pickT_sb, 1)
            dve.memset(slot_of[:, :, JOBS:JOBS + 1], NO_SLOT).then_inc(e_scatter, 1)
            dve.memset(gate_of[:, :, 0:1], 0.0).then_inc(e_added, 1)
            dve.wait_ge(route_ps, 1)
            reads(mark(dve.tensor_copy(lg, bank[0][:, 0:NT * NEXP].rearrange("p (t e) -> p t e", t=NT))))
            for t in range(NT):
                last = dve.max(top8[:, t, :], lg[:, t, :])
            reads(mark(last))
            first, second = top8[:, :, 0:1], top8[:, :, 1:2]
            dve.tensor_scalar(misc[:, :, 2:3], first, -1.0, None, ALU.mult).then_inc(route_top, 1)
            dve.tensor_tensor(misc[:, :, 0:1], first, second, ALU.is_gt)
            dve.tensor_tensor(gt, lg, second.to_broadcast(wide), ALU.is_gt)
            reads(mark(dve.tensor_tensor(eq, lg, second.to_broadcast(wide), ALU.is_equal)))
            for t in range(NT):
                dve.tensor_tensor_scan(rank[:, t, :], ones[:, 0:NEXP], eq[:, t, :], 0.0, ALU.mult, ALU.add)
            reads(mark(dve.tensor_scalar(misc[:, :, 1:2], misc[:, :, 0:1], -1.0, 2.0, ALU.mult, ALU.add)))
            reads(mark(dve.tensor_tensor(fits, rank, misc[:, :, 1:2].to_broadcast(wide), ALU.is_le)))
            reads(mark(dve.tensor_tensor(fits, fits, eq, ALU.mult)))
            dve.tensor_tensor(routed, fits, gt, ALU.add).then_inc(sel_done, 1)
            dve.wait_ge(sel_done, 1)
            dve.wait_ge(route_exp, 1)
            reads(mark(dve.tensor_tensor(ex, ex, routed, ALU.mult)))
            reads(mark(dve.tensor_reduce(misc[:, :, 3:4], ex, AX.X, ALU.add)))
            reads(mark(dve.reciprocal(misc[:, :, 4:5], misc[:, :, 3:4])))
            reads(mark(dve.tensor_tensor(gate, ex, misc[:, :, 4:5].to_broadcast(wide), ALU.mult)))
            dve.wait_ge(rank_ps, 1)
            ranks = bank[1][:, 0:NT * NEXP].rearrange("p (t e) -> p t e", t=NT)
            reads(mark(dve.tensor_scalar(rank, ranks, -NO_SLOT, None, ALU.add)))
            reads(mark(dve.tensor_tensor(rank, rank, routed, ALU.mult)))
            for c in range(CHUNKS):
                dve.tensor_copy(gate_of[:, :, 1 + NEXP * c:1 + NEXP * (c + 1)], gate)
                last = dve.tensor_scalar(slot_of[:, :, NEXP * c:NEXP * (c + 1)], rank, NO_SLOT - SLOTS * c, None, ALU.add)
            reads(mark(dve.tensor_reduce(misc[:, 0, 5:6], bank[1][:, 2 * NEXP:3 * NEXP], AX.X, ALU.max)))
            reads(mark(dve.tensor_scalar(misc[:, 0, 6:7], misc[:, 0, 5:6], float(SLOTS), float(JOBS - NEXP), ALU.is_gt, ALU.mult)))
            dve.tensor_scalar(n_last_job[:, :], misc[:, 0, 6:7], float(NEXP - 1), None, ALU.add).then_inc(jobs_known, 1)

            def pick(j):
                for t in range(NT):
                    last = dve.tensor_scalar(m_pick[:, t, :], slot_no, slot_of[:, t, bass.ds(j, 1)], None, ALU.is_equal)
                last.then_inc(e_pick, 1)

            def gathered(k):
                dve.wait_ge(e_gather, k + 1)
                w = nw[:, KD * NORM_F1:KD * (NORM_F1 + 1)].rearrange("p (b j) -> p b j", b=2).unsqueeze(3)\
                    .to_broadcast([P, 2, 4, SLOTS])
                src = pair[2][:, :].rearrange("p (b c) -> p b c", b=2)[:, :, 0:4 * SLOTS].rearrange("p b (j c) -> p b j c", j=4)
                dve.tensor_tensor(m_u.rearrange("p (b j c) -> p b j c", b=2, j=4), src, w, ALU.mult).then_inc(e_u, 1)

            def gathered_lo(k):
                dve.wait_ge(e_u, k + 1)
                dve.wait_ge(e_u_h, k + 1)
                dve.tensor_tensor(m_u_lo, m_u, m_u_hi.bitcast(f32), ALU.subtract).then_inc(e_u_l, 1)

            def add_scattered(k, t):
                dve.wait_ge(e_scatter, k * NT + (t + 2))
                dve.wait_ge(e_added, k * NT + (t + 1))
                dve.scalar_tensor_tensor(h[:, t, :], pair[2][:, :], gate_of[:, t, bass.ds(k, 1)], h[:, t, :],
                                         ALU.mult, ALU.add).then_inc(e_added, 1)

            def up_half(k, i, p):
                dve.wait_ge(up_h, job_piece(T_MOE, i, p + 1, k))
                dve.tensor_tensor(buffer(up_lo, p, 2048), raw_piece(2 * (T_MOE + i % STEPS) + p),
                                  buffer(up_hi, p, 2048).bitcast(f32), ALU.subtract).then_inc(up_l, 1)

            def dn_step(k, i):
                for p in range(2):
                    dve.wait_ge(dn_h, job_piece(STEPS, i, p + 1, k))
                    dve.tensor_tensor(buffer(dn_lo, p, DM), ffn_dn((STEPS + i % STEPS) % RING)[:, p, :],
                                      buffer(dn_hi, p, DM).bitcast(f32), ALU.subtract).then_inc(dn_l, 1)

            def hidden_step(k, i):
                b = step_buffer(i)
                dve.wait_ge(e_silu, k * STEPS + (i + 1))
                dve.tensor_tensor(m_raw[:, b], m_silu[:, b], bank[step_bank[b]][0:SLOTS, FSTEP:2 * FSTEP], ALU.mult)\
                   .then_inc(e_raw, 1)

            def hidden_lo(k, i):
                dve.wait_ge(e_hT_h, k * STEPS + (i + 1))
                dve.tensor_tensor(m_hT_lo[:, i % STEPS % 2], bank[6][:, 0:2 * SLOTS].rearrange("p (f c) -> p f c", f=2),
                                  m_hT_hi[:, i % STEPS % 2].bitcast(f32), ALU.subtract).then_inc(e_hT_l, 1)

            def result(k):
                dve.wait_ge(dn_used, job_piece(STEPS, STEPS, 0, k))
                dve.wait_ge(e_scatter, k * NT + 3)
                dve.tensor_copy(m_y[:, 512:1024], bank[3][0:SLOTS, :]).then_inc(e_y_dve, 1)

            def iteration(k, i, last=False):
                for p in range(2):
                    if i < STEPS or not last:
                        up_half(k, i, p)
                    if i == STEPS and p == 0 and not last:
                        gathered_lo(k + 1)
                if i == STEPS + 2:
                    result(k)
                if i >= 1 and (i - 1 < STEPS or not last):
                    hidden_step(k, i - 1)
                if i >= DN_LATE and (i - DN_LATE < STEPS or not last):
                    hidden_lo(k, i - DN_LATE)
                    dn_step(k, i - DN_LATE)
                if i == 4:
                    add_scattered(k, 0)
                if i == 5:
                    dve.wait_ge(e_gather, k + 1)
                    pick(k)
                if i == 6:
                    add_scattered(k, 1)
                if i == 7 and not last:
                    dve.wait_ge(e_pickT, k + 1)
                    pick(k + 1)
                if i == 9 and not last:
                    gathered(k + 1)

            def job(k, last=False):
                for i in range(FIRST, STEPS + FIRST):
                    iteration(k, i, last)

            up_half(0, 0, 0)
            up_half(0, 0, 1)
            dve.wait_ge(jobs_known, 1)
            pick(0)
            gathered(0)
            gathered_lo(0)
            for i in range(1, FIRST):
                iteration(0, i)
            with dve.Fori(0, NEXP - 1) as k:
                job(k)
            last_job = dve.value_load(n_last_job[0:1, 0:1], min_val=NEXP - 1, max_val=JOBS - 1)
            with dve.If(last_job > NEXP - 1):
                with dve.Fori(NEXP - 1, JOBS - 1) as k:
                    job(k)
            job(last_job, last=True)
            add_scattered(last_job + 1, 0)
            add_scattered(last_job + 1, 1)


def shape_constants():
    import numpy as np
    c = np.zeros((P, K_END), np.float32)
    r = np.arange(P)
    c[:, K_ID:K_ID + P] = np.eye(P)
    c[:, K_BEFORE:K_BEFORE + P] = r[:, None] < r[None, :]
    c[:, K_AFTER:K_AFTER + P] = r[:, None] > r[None, :]
    c[:, K_ONES:K_ONES + P] = 1.0
    c[:, K_IMASK + P:K_IMASK + 2 * P] = np.where(r[None, :] > r[:, None], np.float32(NOT_CAUSAL), np.float32(0))
    c[:, K_SLOT:K_SLOT + SLOTS] = np.arange(SLOTS)
    inv = np.float32(500000.0) ** (-np.arange(16, dtype=np.float32) * np.float32(2.0) / np.float32(32))
    angle = np.arange(TOK, dtype=np.float32)[:, None] * inv.astype(np.float32)[None, :]
    for k, fn in ((K_COS, np.cos), (K_SIN, np.sin)):
        c[:, k:k + 32] = fn(angle).reshape(NT, P, 16).transpose(1, 0, 2).reshape(P, 32)
    return c


_INS = ["x", "a_norm_w", "a_w_in", "a_q_norm_w", "a_k_norm_w", "a_w_out", "kv_norm_w", "kv_w", "b_norm_w",
        "b_w_q", "b_w_out", "ffn_norm_w", "dense_w_gate_up", "dense_w_down", "moe_router_w",
        "moe_w_gate_up", "moe_w_down"]


def kernel(**inputs):
    import numpy as np
    import concourse.bacc as bacc
    from concourse.bass_utils import run_bass_kernel_spmd

    nc = bacc.Bacc("TRN2", target_bir_lowering=False, num_devices=1)
    arrays = {f"in_{name}": np.ascontiguousarray(inputs[name]) for name in _INS}
    arrays["in_consts"] = shape_constants()
    args = [nc.dram_tensor(name, a.shape, mybir.dt.from_np(a.dtype), kind="ExternalInput").ap()
            for name, a in arrays.items()]
    args.append(nc.dram_tensor("out_0", (1, TOK, DM), mybir.dt.float32, kind="ExternalOutput").ap())
    program(nc, *args)
    return run_bass_kernel_spmd(nc, [arrays], core_ids=[0]).results[0]["out_0"]
```

```python
import concourse.bass as bass
from concourse import mybir
from concourse.alu_op_type import AluOpType as ALU
from contextlib import ExitStack

P = 128
TOK = 256
NT = TOK // P
DM = 1024
KD = DM // P
HD = 128
NH = 8
NKV = 2
GROUP = NH // NKV
IH, ID = 8, 64
A_IN = 2120
C_K, C_V, C_QI, C_KI, C_WI = 1024, 1280, 1536, 2048, 2112
TOPK = 64
F = 2816
FSTEP = 256
STEPS = F // FSTEP
NEXP = 8
SLOTS = 96
CHUNKS = -(-TOK // SLOTS)
JOBS = NEXP * CHUNKS
RING = 4
EPS = 1e-6
SCALE = HD ** -0.5
NOT_CAUSAL = -1.0e38
TAKEN = -2.0e38
MASKED = -1.0e30
NO_SLOT = -1.0e4

K_ID, K_BEFORE, K_AFTER, K_ONES, K_IMASK, K_SLOT, K_COS, K_SIN = 0, 128, 256, 384, 512, 768, 864, 896
K_EPS = 928
K_END = 929

NORM_A, NORM_F0, NORM_F1, NORM_KV, NORM_B = range(5)

T_IN, T_OUT, T_DENSE = 0, 5, 7
T_BQ, T_BK, T_BV, T_BO = T_DENSE + STEPS, T_DENSE + STEPS + 2, T_DENSE + STEPS + 4, T_DENSE + STEPS + 6
T_MOE = T_BO + 2
IN_COLS = [(C_QI, 512), (C_KI, 72), (C_K, 512), (0, 512), (512, 512)]


def program(nc, x, a_norm_w, a_w_in, a_q_norm_w, a_k_norm_w, a_w_out, kv_norm_w, kv_w, b_norm_w,
            b_w_q, b_w_out, ffn_norm_w, dense_w_gate_up, dense_w_down, moe_router_w,
            moe_w_gate_up, moe_w_down, consts, out):
    f32, f32r, i32 = mybir.dt.float32, mybir.dt.float32r, mybir.dt.int32
    ACT = mybir.ActivationFunctionType
    AX = mybir.AxisListType
    ctx = ExitStack()
    with ctx:
        def sb(name, shape, dt=f32):
            return ctx.enter_context(nc.sbuf_tensor(name, shape, dt))

        def sem(name):
            return ctx.enter_context(nc.semaphore(name))

        up_ring = sb("up_ring", [P, RING, 4096])
        dn_ring = sb("dn_ring", [P, RING, 2048])
        up_hi = sb("up_hi", [P, 2, 2048], f32r)
        up_lo = sb("up_lo", [P, 2, 2048], f32r)
        dn_hi = sb("dn_hi", [P, 2, DM], f32r)
        dn_lo = sb("dn_lo", [P, 2, DM], f32r)
        cst = sb("cst", [P, K_END])
        h = sb("h", [P, NT, DM])
        u = sb("u", [P, NT, DM])
        uT_hi = sb("uT_hi", [P, KD, TOK], f32r)
        uT_lo = sb("uT_lo", [P, KD, TOK], f32r)
        q_T = sb("q_T", [P, NH, TOK])
        hid_hi = sb("hid_hi", [P, 512], f32r)
        hid_lo = sb("hid_lo", [P, 512], f32r)
        router_hi = sb("router_hi", [P, KD * NEXP], f32r)
        router_lo = sb("router_lo", [P, KD * NEXP], f32r)
        work = sb("work", [P, 6 * 384])
        kT_a = sb("kT_a", [P, NKV, TOK])
        norm_rows = sb("norm_rows", [5 * KD, P])
        nw = sb("nw", [P, 5 * KD])
        qk_w = sb("qk_w", [P, 2, HD])
        router = sb("router", [P, KD, NEXP])
        mean_sq = sb("mean_sq", [P, 4, NT, 2])
        rs = sb("rs", [P, 4, NT])
        one_out = sb("one_out", [1, 1])
        qk_rs = sb("qk_rs", [P, 3, NT, GROUP])
        w_idx = sb("w_idx", [P, NT, IH])
        top8 = sb("top8", [P, NT, 8])
        soft = sb("soft", [P, 3, NT * NH])
        rt = sb("rt", [P, 10, NT, NEXP])
        slot_of = sb("slot_of", [P, NT, JOBS + 1])
        gate_of = sb("gate_of", [P, NT, JOBS + 1])
        n_last_job = sb("n_last_job", [P, 1], i32)

        ident, before, after = cst[:, K_ID:K_ID + P], cst[:, K_BEFORE:K_BEFORE + P], cst[:, K_AFTER:K_AFTER + P]
        ones, imask = cst[:, K_ONES:K_ONES + P], cst[:, K_IMASK:K_IMASK + 2 * P]
        eps = cst[:, K_EPS:K_EPS + 1]
        slot_no = cst[:, K_SLOT:K_SLOT + SLOTS]
        cos = cst[:, K_COS:K_COS + 32].rearrange("p (t f) -> p t f", t=NT)
        sin = cst[:, K_SIN:K_SIN + 32].rearrange("p (t f) -> p t f", t=NT)

        pj_rest = work[:, 0:NT * (A_IN - DM)].rearrange("p (t c) -> p t c", t=NT)

        def proj(c, cols):
            return u[:, :, c:c + cols] if c < DM else pj_rest[:, :, c - DM:c - DM + cols]

        scratch = dn_ring[:, :, :].rearrange("p s c -> p (s c)")
        at = [0]

        def take(n):
            at[0] += n
            assert at[0] <= RING * 2048
            return scratch[:, at[0] - n:at[0]]

        space0, space1, spaceT = take(1024), take(2048), take(3072)
        rel0 = space0.rearrange("p (h s) -> p h s", h=IH)
        rel1 = space1.rearrange("p (h s) -> p h s", h=IH)
        prob0 = space0.rearrange("p (h s) -> p h s", h=NH)
        prob1 = space1.rearrange("p (h s) -> p h s", h=NH)
        probT = spaceT.rearrange("p (h c) -> p h c", h=NH)
        sq = spaceT[:, 0:1024]
        rope_tmp = spaceT[:, 1024:2048]
        qiT = spaceT[:, 2048:3072].rearrange("p (j t) -> p j t", j=IH // 2)
        kiT = take(256)
        ki2 = take(256).rearrange("p (t c) -> p t c", t=NT)
        score = [take(128), take(256)]
        bias = [take(128), take(256)]
        at[0] = 0
        kT_b = take(2048).rearrange("p (h t) -> p h t", h=NH)
        v_b = take(2048).rearrange("p (t c) -> p t c", t=NT)
        att = take(3072).rearrange("p (h c) -> p h c", h=NH)
        u_flat = u[:, :, :].rearrange("p t c -> p (t c)")

        def two_heads(v):
            return v.rearrange("p (h c) -> p h c", h=2)

        absz = [two_heads(work[:, 768 * j:768 * j + 768]) for j in range(2)]
        neg = absz
        lb = [two_heads(u_flat[:, 768 * j:768 * j + 768]) for j in range(2)]
        lk = [two_heads(v) for v in (work[:, 1536:2304], take(768))]
        d_silu = work[:, 0:1024].rearrange("p (b f c) -> p b f c", b=2, f=2)
        d_raw = work[:, 1024:2048].rearrange("p (b f c) -> p b f c", b=2, f=2)
        d_hi = hid_hi[:, :].rearrange("p (f c) -> p f c", f=2)
        d_lo = hid_lo[:, :].rearrange("p (f c) -> p f c", f=2)
        m_silu = work[0:SLOTS, 0:768].rearrange("p (b c) -> p b c", b=3)
        m_raw = work[0:SLOTS, 768:1536].rearrange("p (b c) -> p b c", b=3)
        m_pick = work[:, 1536:1536 + NT * SLOTS].rearrange("p (t c) -> p t c", t=NT)
        m_pickT = work[0:SLOTS, 1792:1792 + TOK]
        q_flat = q_T[:, :, :].rearrange("p h t -> p (h t)")
        route_T = work[0:NEXP, 0:TOK]
        m_y = q_flat[0:SLOTS, 0:DM]
        m_u = q_flat[:, DM:DM + KD * SLOTS]
        m_u_hi = uT_hi[:, :, :].rearrange("p k t -> p (k t)")[:, 0:KD * SLOTS]
        m_u_lo = uT_lo[:, :, :].rearrange("p k t -> p (k t)")[:, 0:KD * SLOTS]
        m_hT_hi = hid_hi[:, 0:4 * SLOTS].rearrange("p (b f c) -> p b f c", b=2, f=2)
        m_hT_lo = hid_lo[:, 0:4 * SLOTS].rearrange("p (b f c) -> p b f c", b=2, f=2)

        pair = [ctx.enter_context(nc.psum_tensor(f"pair{i}", [P, 1024], f32)) for i in range(4)]
        step_bank = (0, 1, 7)
        bank = [pair[i // 2][:, 512 * (i % 2):512 * (i % 2) + 512] for i in range(8)]

        consts_in, x_in, rows_in, qkw_in, router_in = (sem(n) for n in
            ("consts_in", "x_in", "rows_in", "qkw_in", "router_in"))
        first_in = sem("first_in")
        up_in = [sem(f"up_in{s}") for s in range(RING)]
        dn_in = [sem(f"dn_in{s}") for s in range(RING)]
        up_h, up_l, up_used = sem("up_h"), sem("up_l"), sem("up_used")
        dn_h, dn_l, dn_used = sem("dn_h"), sem("dn_l"), sem("dn_used")
        router_h, router_l = sem("router_h"), sem("router_l")
        nw_ps, nw_done = sem("nw_ps"), sem("nw_done")
        h_done = sem("h_done")
        sumsq, ms_done, root_done, rs_done, u_done = (sem(n) for n in ("sumsq", "ms_done", "root_done", "rs_done", "u_done"))
        uT_ps, uT_h, uT_l = sem("uT_ps"), sem("uT_h"), sem("uT_l")
        proj_ps, proj_sb = sem("proj_ps"), sem("proj_sb")
        idx_roped, idx_T, idx_T_sb = sem("idx_roped"), sem("idx_T"), sem("idx_T_sb")
        idx_qk, rel_done = sem("idx_qk"), sem("rel_done")
        qk_ms, qk_root, qk_rstd, qk_scaled, qk_roped = (sem(n) for n in ("qk_ms", "qk_root", "qk_rstd", "qk_scaled", "qk_roped"))
        qk_T, qk_T_sb = sem("qk_T"), sem("qk_T_sb")
        logits_ps, rowmax_done, exp_done, prob_done = sem("logits_ps"), sem("rowmax_done"), sem("exp_done"), sem("prob_done")
        probT_ps, probT_sb = sem("probT_ps"), sem("probT_sb")
        o_ps, o_h, o_l = sem("o_ps"), sem("o_h"), sem("o_l")
        res_ps = sem("res_ps")
        dve_chain = sem("dve_chain")
        silu_done, hid_raw, hid_h, hid_l = sem("silu_done"), sem("hid_raw"), sem("hid_h"), sem("hid_l")
        bk_sb, bq_sb = sem("bk_sb"), sem("bq_sb")
        z_ps, z_log, keep_raw, keep_done = sem("z_ps"), sem("z_log"), sem("keep_raw"), sem("keep_done")
        after_ps, expo_done, stick_raw, stick_done = sem("after_ps"), sem("expo_done"), sem("stick_raw"), sem("stick_done")
        v_ps, v_sb = sem("v_ps"), sem("v_sb")
        routeT_ps, routeT_sb = sem("routeT_ps"), sem("routeT_sb")
        route_ps, route_top, route_exp, sel_done = sem("route_ps"), sem("route_top"), sem("route_exp"), sem("sel_done")
        rank_ps, jobs_known = sem("rank_ps"), sem("jobs_known")
        e_silu, e_raw, e_hT, e_hT_h, e_hT_l = sem("e_silu"), sem("e_raw"), sem("e_hT"), sem("e_hT_h"), sem("e_hT_l")
        e_y_act, e_y_dve = sem("e_y_act"), sem("e_y_dve")
        e_pick, e_pickT, e_pickT_sb = sem("e_pick"), sem("e_pickT"), sem("e_pickT_sb")
        e_gather, e_u, e_u_h, e_u_l = sem("e_gather"), sem("e_u"), sem("e_u_h"), sem("e_u_l")
        e_scatter, e_added, out_done = sem("e_scatter"), sem("e_added"), sem("out_done")

        block = ctx.enter_context(nc.Block())

        def up_tile(n, cols=512):
            return up_ring[:, n % RING, 0:KD * cols].rearrange("p (k c) -> p k c", k=KD)

        def ffn_up(s):
            return up_ring[:, s, :].rearrange("p (k g c) -> p k g c", k=KD, g=2)

        def ffn_dn(s):
            return dn_ring[:, s, :].rearrange("p (b n) -> p b n", b=2)

        def up_arrived(n):
            return 16 * sum(2 if T_DENSE <= m < T_DENSE + STEPS else 1 for m in range(n % RING, n + 1, RING))

        def dn_arrived(n):
            return 16 * (n // RING + 1)

        def job_arrived(first, i, k, before_jobs, transfers):
            slot = [(first + j) % RING for j in range(STEPS)]
            return k * (16 * transfers * slot.count(slot[i])) + (before_jobs + 16 * transfers * slot[:i + 1].count(slot[i]))

        def job_up_arrived(i, k):
            last = max(n for n in range(T_MOE) if n % RING == (T_MOE + i) % RING)
            return job_arrived(T_MOE, i, k, up_arrived(last), 2)

        def job_dn_arrived(i, k):
            last = max(n for n in range(STEPS) if n % RING == (STEPS + i) % RING)
            return job_arrived(STEPS, i, k, dn_arrived(last), 1)

        def job_free(first, i, k):
            last_user = i - RING if i >= RING else max(range(i, STEPS, RING)) - STEPS
            return k * (2 * STEPS) + 2 * (first + last_user + 1)

        FIRST = 3
        DN_LATE = 2

        def step_buffer(i):
            return 2 if i % STEPS == STEPS - 1 else i % STEPS % 2

        def last_step_in_buffer(i):
            return max(j for j in range(-STEPS, i) if step_buffer(j) == step_buffer(i))

        def job_piece(first, i, p, k):
            return k * (2 * STEPS) + (2 * (first + i) + p)

        def buffer(ring, n, cols):
            return ring[:, n % 2, 0:cols]

        def raw_piece(n, cols=512):
            return up_ring[:, (n // 2) % RING, 4 * cols * (n % 2):4 * cols * (n % 2 + 1)]

        def piece_cols(n):
            return IN_COLS[n // 2][1] if n < 2 * T_OUT else 512

        @block.sync
        def _(sp):
            for t in range(NT):
                sp.dma_start(h[:, t, :], x[0, P * t:P * t + P, :]).then_inc(x_in, 16)
            sp.dma_start(cst[:, :], consts).then_inc(consts_in, 16)
            sp.dma_start(norm_rows[KD * NORM_B:KD * NORM_B + KD, :], b_norm_w[0].rearrange("(k c) -> k c", c=P))\
              .then_inc(rows_in, 16)

            def columns(n, w, c0, cols=512):
                if n >= RING:
                    sp.wait_ge(up_l, 2 * (n - RING + 1))
                src = w.rearrange("(k p) c -> p k c", p=P)[:, :, c0:c0 + cols]
                if n == 0:
                    sp.dma_start(up_tile(n, cols)[:, 0:4, :], src[:, 0:4, :]).then_inc(first_in, 16)
                    sp.dma_start(up_tile(n, cols)[:, 4:8, :], src[:, 4:8, :]).then_inc(up_in[n % RING], 16)
                else:
                    sp.dma_start(up_tile(n, cols), src).then_inc(up_in[n % RING], 16)

            for j, (c, cols) in enumerate(IN_COLS):
                columns(T_IN + j, a_w_in[0], c, cols)
            for j in range(2):
                columns(T_OUT + j, a_w_out[0], 512 * j)

            dup = dense_w_gate_up[0].rearrange("(k p) (g c) -> p k g c", p=P, g=2)
            ddn = dense_w_down[0].rearrange("(b p) n -> p b n", p=P)
            for i in range(STEPS + DN_LATE):
                if i < STEPS:
                    n = T_DENSE + i
                    sp.wait_ge(up_l, 2 * (n - RING + 1))
                    for g in range(2):
                        sp.dma_start(ffn_up(n % RING)[:, :, g, :], dup[:, :, g, FSTEP * i:FSTEP * (i + 1)])\
                          .then_inc(up_in[n % RING], 16)
                m = i - DN_LATE
                if m == 0:
                    sp.wait_ge(o_ps, 2)
                if m >= RING:
                    sp.wait_ge(dn_l, 2 * (m - RING + 1))
                if m >= 0:
                    sp.dma_start(ffn_dn(m % RING), ddn[:, 2 * m:2 * m + 2, :]).then_inc(dn_in[m % RING], 16)

            for first, w, c0 in ((T_BQ, b_w_q[0], 0), (T_BK, kv_w, 0), (T_BV, kv_w, DM), (T_BO, b_w_out[0], 0)):
                for j in range(2):
                    columns(first + j, w, c0 + 512 * j)

            eup = moe_w_gate_up[0].rearrange("e (k p) (g c) -> e p k g c", p=P, g=2)
            edn = moe_w_down[0].rearrange("e (b p) n -> e p b n", p=P)

            def expert_up(i, e):
                s = (T_MOE + i) % RING
                for g in range(2):
                    src = eup[bass.ds(e, 1), :, :, g, FSTEP * i:FSTEP * (i + 1)]
                    sp.dma_start(ffn_up(s)[:, :, g, :], src.rearrange("e p k c -> (e p) k c")).then_inc(up_in[s], 16)

            def expert_dn(i, e):
                s = (STEPS + i) % RING
                src = edn[bass.ds(e, 1), :, 2 * i:2 * i + 2, :]
                sp.dma_start(ffn_dn(s), src.rearrange("e p b n -> (e p) b n")).then_inc(dn_in[s], 16)

            for i in range(RING):
                sp.wait_ge(up_l, 2 * (T_MOE + i - RING + 1))
                expert_up(i, 0)
                m = i - DN_LATE
                if m == 0:
                    sp.wait_ge(o_ps, 4)
                if m >= 0:
                    sp.wait_ge(dn_l, 2 * (STEPS + m - RING + 1))
                    expert_dn(m, 0)

            def job(k, e, next_e, last=False):
                for i in range(RING, STEPS + RING):
                    if i < STEPS or not last:
                        sp.wait_ge(up_l, job_free(T_MOE, i % STEPS, k + i // STEPS))
                        expert_up(i % STEPS, e if i < STEPS else next_e)
                    m = i - DN_LATE
                    if m < STEPS or not last:
                        sp.wait_ge(dn_l, job_free(STEPS, m % STEPS, k + m // STEPS))
                        expert_dn(m % STEPS, e if m < STEPS else next_e)

            with sp.Fori(0, NEXP - 1) as k:
                job(k, k, k + 1)
            sp.wait_ge(jobs_known, 1)
            last_job = sp.value_load(n_last_job[0:1, 0:1], min_val=NEXP - 1, max_val=JOBS - 1)
            with sp.If(last_job > NEXP - 1):
                for c in range(1, CHUNKS):
                    job(c * NEXP - 1, NEXP - 1, 0)
                    with sp.Fori(0, NEXP - 1) as e:
                        job(e + c * NEXP, e, e + 1)
            job(last_job, NEXP - 1, None, last=True)
            for t in range(NT):
                sp.wait_ge(e_added, last_job * NT + (NT + t + 2))
                sp.dma_start(out[0, P * t:P * t + P, :], h[:, t, :]).then_inc(out_done, 16)
            sp.wait_ge(out_done, 16 * NT)

        @block.tensor
        def _(pe):
            def uT_blocks(n):
                src = h if n in (0, 3) else u
                for t in range(NT):
                    if n == 0:
                        pe.wait_ge(x_in, 16 * NT)
                    elif n == 3:
                        pe.wait_ge(h_done, 11 + t)
                    else:
                        pe.wait_ge(u_done, NT * (n - 1) + t + 1)
                    for k in range(KD):
                        c = 256 * (k % 2) + P * t
                        mm = pe.transpose(bank[4 + k // 2][:, c:c + P], src[:, t, P * k:P * k + P], ident)
                        if t == NT - 1 and k % 2 == 1:
                            mm.then_inc(uT_ps, 1)

            def product(ps, a_hi, a_lo, b_hi, b_lo, start, stop, shared=False):
                pe.matmul(ps, a_hi, b_hi, start=start, stop=False, skip_group_check=shared)
                pe.matmul(ps, a_hi, b_lo, start=False, stop=False, skip_group_check=shared)
                return pe.matmul(ps, a_lo, b_hi, start=False, stop=stop, skip_group_check=shared)

            def token_columns(n, t, ps, cols=512):
                hi, lo = (buffer(b, n, 4 * cols).rearrange("p (k c) -> p k c", k=4) for b in (up_hi, up_lo))
                for j in range(4):
                    k = 4 * (n % 2) + j
                    mm = product(ps[:, 0:cols], uT_hi[:, k, P * t:P * t + P], uT_lo[:, k, P * t:P * t + P],
                                 hi[:, j, :], lo[:, j, :], k == 0, k == KD - 1)
                return mm

            def residual_product(n0, first_bank):
                for n in range(2 * n0, 2 * n0 + 4):
                    half = n // 2 - n0
                    pe.wait_ge(up_l, n + 1)
                    for t in range(NT):
                        mm = token_columns(n, t, bank[first_bank + 2 * t + half])
                        if t == 0 and n % 2 == 1:
                            mm.then_inc(res_ps, 1)
                    mm.then_inc(up_used, 1)

            pe.wait_ge(consts_in, 16)
            pe.wait_ge(rows_in, 16 * 4)
            pe.transpose(bank[0][:, 0:5 * KD], norm_rows[:, :], ident[0:5 * KD, 0:5 * KD]).then_inc(nw_ps, 1)
            uT_blocks(0)

            def project(j, halves=(0, 1)):
                cols = IN_COLS[j][1]
                for n in (2 * j + half for half in halves):
                    pe.wait_ge(up_l, n + 1)
                    if n < 2:
                        pe.wait_ge(uT_l, 2 * n + 2)
                    if n == 0:
                        pe.wait_ge(nw_done, 1)
                    for t in range(NT):
                        use = NT * j + t
                        if use >= 4 and n % 2 == 0:
                            pe.wait_ge(proj_sb, use - 3)
                        mm = token_columns(n, t, bank[use % 4], cols)
                        if t == 0 and n % 2 == 1:
                            mm.then_inc(proj_ps, 1)
                    mm.then_inc(up_used, 1)

            project(0)
            project(1)
            project(2)
            pe.wait_ge(idx_roped, 1)
            for j in range(IH // 2):
                for t in range(NT):
                    c = 256 * (j % 2) + P * t
                    pe.transpose(bank[4 + j // 2][:, c:c + P], proj(C_QI + P * j, P)[:, t, :], ident)
            for t in range(NT):
                mm = pe.transpose(bank[6][:, P * t:P * t + P], ki2[:, t, :], ident)
            mm.then_inc(idx_T, 1)
            project(3, halves=(0,))

            def index_scores(t, heads, first_bank):
                keys = P * (t + 1)
                for n, i in enumerate(heads):
                    part = slice(ID * (i % 2), ID * (i % 2) + ID)
                    c = (n // 2) * keys
                    mm = pe.matmul(bank[first_bank + i % 2][:, c:c + keys], qiT[part, i // 2, P * t:P * t + P],
                                   kiT[part, 0:keys], start=True, stop=True)
                mm.then_inc(idx_qk, 1)

            pe.wait_ge(idx_T_sb, 3)
            index_scores(0, range(8), 4)
            index_scores(1, range(4), 6)
            pe.wait_ge(proj_sb, 6)
            index_scores(1, range(4, 8), 0)
            project(3, halves=(1,))
            pe.wait_ge(rel_done, 6)
            project(4)

            for n, ps in enumerate((bank[4], bank[5], bank[6], bank[7], bank[0])):
                if n == 0:
                    pe.wait_ge(rel_done, 6)
                if n == 4:
                    pe.wait_ge(proj_sb, 9)
                pe.wait_ge(qk_roped, (1, 2, 2, 3, 3)[n])
                c0 = C_K if n == 0 else 2 * HD * (n - 1)
                for i in range(2):
                    for t in range(NT):
                        mm = pe.transpose(ps[:, 256 * i + P * t:256 * i + P * t + P],
                                          proj(c0 + HD * i, HD)[:, t, :], ident)
                mm.then_inc(qk_T, 1)

            pe.wait_ge(qk_T_sb, 5)
            pe.wait_ge(proj_sb, 10)
            for i in range(NH):
                mm = pe.matmul(pair[1][:, P * i:P * i + P], q_T[:, i, 0:P], kT_a[:, i // GROUP, 0:P],
                               start=True, stop=True)
            mm.then_inc(logits_ps, 1)
            for i in range(NH):
                mm = pe.matmul(pair[2 + i // 4][:, TOK * (i % 4):TOK * (i % 4) + TOK], q_T[:, i, P:TOK],
                               kT_a[:, i // GROUP, :], start=True, stop=True)
                if i % 4 == 3:
                    mm.then_inc(logits_ps, 1)
            for g in range(3):
                pe.wait_ge(prob_done, g + 1)
                for i in range(8):
                    src = prob0[:, i, :] if g == 0 else prob1[:, 4 * (g - 1) + i // 2, P * (i % 2):P * (i % 2) + P]
                    mm = pe.transpose(pair[g][:, P * i:P * i + P], src, ident)
                mm.then_inc(probT_ps, 1)

            def weighted_values(weightsT, value, pairs, two_ready=None):
                for i in range(NH):
                    if two_ready is not None and i % 2 == 0:
                        pe.wait_ge(two_ready, i // 2 + 1)
                    ps = pair[pairs[i // 4]][:, TOK * (i % 4):TOK * (i % 4) + TOK]
                    pe.matmul(ps, value(0, i), weightsT[:, i, 0:TOK], start=True, stop=False)
                    mm = pe.matmul(ps[:, P:TOK], value(1, i), weightsT[:, i, TOK:TOK + P], start=False, stop=True)
                    if i % 4 == 3:
                        mm.then_inc(o_ps, 1)

            pe.wait_ge(probT_sb, 3)
            weighted_values(probT, lambda t, i: proj(C_V + HD * (i // GROUP), HD)[:, t, :], (3, 0))
            pe.wait_ge(o_l, 2)
            residual_product(T_OUT, 2)

            uT_blocks(1)

            def columns_tokens(n, p0, c0s):
                hi, lo = (buffer(b, n, 2048).rearrange("p (k c) -> p k c", k=4) for b in (up_hi, up_lo))
                for b, c0 in enumerate(c0s):
                    for j in range(4):
                        k = 4 * (n % 2) + j
                        mm = product(pair[p0][:, TOK * b:TOK * b + TOK], hi[:, j, c0:c0 + P], lo[:, j, c0:c0 + P],
                                     uT_hi[:, k, :], uT_lo[:, k, :], k == 0 and b % 2 == 0, k == KD - 1, shared=True)
                mm.then_inc(up_used, 1)

            def dense_up(i):
                for n in (2 * (T_DENSE + i), 2 * (T_DENSE + i) + 1):
                    pe.wait_ge(up_l, n + 1)
                    if i == 0:
                        pe.wait_ge(uT_l, 4 + 2 * (n % 2) + 2)
                    if i >= 2 and n % 2 == 0:
                        pe.wait_ge(hid_raw, i - 1)
                    columns_tokens(n, i % 2, (0, FSTEP, P, FSTEP + P))

            def dense_dn(i):
                for f in range(2):
                    n = 2 * i + f
                    pe.wait_ge(dn_l, n + 1)
                    if f == 0:
                        pe.wait_ge(hid_l, i + 1)
                    for t in range(NT):
                        for half in range(2):
                            c = slice(512 * half, 512 * half + 512)
                            mm = product(bank[4 + 2 * t + half], d_hi[:, f, P * t:P * t + P], d_lo[:, f, P * t:P * t + P],
                                         buffer(dn_hi, n, DM)[:, c], buffer(dn_lo, n, DM)[:, c], n == 0, n == 2 * STEPS - 1)
                    mm.then_inc(dn_used, 1)

            for i in range(STEPS):
                dense_up(i)
                if i > 0:
                    dense_dn(i - 1)
            dense_dn(STEPS - 1)

            uT_blocks(2)
            for j in range(4):
                for n in (2 * (T_BQ + j), 2 * (T_BQ + j) + 1):
                    pe.wait_ge(up_l, n + 1)
                    if j == 0:
                        pe.wait_ge(uT_l, 8 + 2 * (n % 2) + 2)
                    if j == 2:
                        pe.wait_ge(uT_l, 12 + 2 * (n % 2) + 2)
                    columns_tokens(n, j, (0, HD, 2 * HD, 3 * HD))

            def sticks_z(j):
                if j >= 2:
                    pe.wait_ge(keep_raw, j - 1)
                for i in (2 * j, 2 * j + 1):
                    ps = bank[2 * (j % 2) + i % 2]
                    pe.matmul(ps[:, 0:TOK], kT_b[:, i, 0:P], q_T[:, i, :], start=True, stop=True)
                    mm = pe.matmul(ps[:, TOK:TOK + P], kT_b[:, i, P:TOK], q_T[:, i, P:TOK], start=True, stop=True)
                mm.then_inc(z_ps, 1)

            def sticks_after(j):
                pe.wait_ge(keep_done, j + 1)
                if j >= 1:
                    pe.wait_ge(expo_done, j)
                for i in range(2):
                    ps, src = bank[4 + i], lk[j % 2][:, i, :]
                    pe.matmul(ps[:, 0:TOK], after, src[:, 0:TOK], start=True, stop=False)
                    pe.matmul(ps[:, P:TOK], ones, src[:, TOK:TOK + P], start=False, stop=True)
                    mm = pe.matmul(ps[:, TOK:TOK + P], after, src[:, TOK:TOK + P], start=True, stop=True)
                mm.then_inc(after_ps, 1)

            def values(m):
                n = 2 * T_BV + m
                pe.wait_ge(up_l, n + 1)
                if m == 2:
                    pe.wait_ge(v_sb, 2)
                for t in range(NT):
                    mm = token_columns(n, t, bank[6 + t])
                    if t == 0 and n % 2 == 1:
                        mm.then_inc(v_ps, 1)
                mm.then_inc(up_used, 1)

            pe.wait_ge(bk_sb, 2)
            pe.wait_ge(bq_sb, 2)
            sticks_z(0)
            sticks_z(1)
            values(0)
            values(1)
            sticks_after(0)
            sticks_z(2)
            values(2)
            sticks_after(1)
            sticks_z(3)
            sticks_after(2)
            values(3)
            sticks_after(3)
            pe.wait_ge(v_sb, 4)
            weighted_values(att, lambda t, i: v_b[:, t, HD * i:HD * i + HD], (0, 1), stick_done)
            pe.wait_ge(o_l, 4)
            residual_product(T_BO, 0)

            uT_blocks(3)
            pe.wait_ge(uT_l, 20)
            pe.wait_ge(router_l, 1)
            for k in range(KD):
                c = slice(NEXP * k, NEXP * k + NEXP)
                mm = product(bank[0][0:NEXP, 0:TOK], router_hi[:, c], router_lo[:, c], uT_hi[:, k, :], uT_lo[:, k, :],
                             k == 0, k == KD - 1)
            mm.then_inc(routeT_ps, 1)
            pe.wait_ge(routeT_sb, 1)
            for t in range(NT):
                mm = pe.transpose(bank[1][:, NEXP * t:NEXP * t + NEXP], route_T[:, P * t:P * t + P], ident[0:NEXP, 0:NEXP])
            mm.then_inc(route_ps, 1)
            pe.wait_ge(sel_done, 1)
            routed = rt[:, 5]
            pe.matmul(bank[0][:, 0:8], before, routed[:, 0, :], start=True, stop=True)
            pe.matmul(bank[0][:, 8:16], ones, routed[:, 0, :], start=True, stop=False)
            pe.matmul(bank[0][:, 8:16], before, routed[:, 1, :], start=False, stop=True)
            pe.matmul(bank[0][:, 16:24], ones, routed[:, 0, :], start=True, stop=False)
            pe.matmul(bank[0][:, 16:24], ones, routed[:, 1, :], start=False, stop=True).then_inc(rank_ps, 1)

            def gather(j):
                pe.wait_ge(e_pick, j * 2 + 1)
                for b in range(KD):
                    for t in range(NT):
                        c = SLOTS * (b % 4)
                        mm = pe.matmul(bank[4 + b // 4][:, c:c + SLOTS], u[:, t, P * b:P * b + P], m_pick[:, t, :],
                                       start=(t == 0), stop=(t == NT - 1))
                mm.then_inc(e_gather, 1)

            def scatter(k, t):
                if t == 0:
                    pe.wait_ge(e_y_act, k + 1)
                    pe.wait_ge(e_y_dve, k + 1)
                    pe.wait_ge(e_pickT_sb, k + 1)
                else:
                    pe.wait_ge(e_added, k * NT + 2)
                for half in range(2):
                    c = slice(512 * half, 512 * half + 512)
                    mm = pe.matmul(pair[2][:, c], m_pickT[:, P * t:P * t + P], m_y[:, c], start=True, stop=True)
                mm.then_inc(e_scatter, 1)

            def expert_up(k, i):
                for p in range(2):
                    pe.wait_ge(up_l, job_piece(T_MOE, i, p + 1, k))
                    if i % STEPS == 0 and p == 0:
                        pe.wait_ge(e_u_l, k + (i // STEPS + 1))
                    if i >= 2 and p == 0:
                        if i == STEPS - 1:
                            pe.wait_ge(e_pickT_sb, k + 2)
                        else:
                            pe.wait_ge(e_raw, k * STEPS + (last_step_in_buffer(i) + 1))
                    hi, lo = (buffer(b, p, 2048).rearrange("p (k c) -> p k c", k=4) for b in (up_hi, up_lo))
                    for j in range(4):
                        c = slice(SLOTS * (4 * p + j), SLOTS * (4 * p + j + 1))
                        mm = product(bank[step_bank[step_buffer(i)]][0:SLOTS, :], m_u_hi[:, c], m_u_lo[:, c],
                                     hi[:, j, :], lo[:, j, :], p == 0 and j == 0, p == 1 and j == 3)
                    mm.then_inc(up_used, 1)

            def hidden_T(k, i):
                pe.wait_ge(e_raw, k * STEPS + (i + 1))
                if i > 0:
                    pe.wait_ge(e_hT_l, k * STEPS + i)
                for f in range(2):
                    mm = pe.transpose(bank[6][:, SLOTS * f:SLOTS * f + SLOTS], m_raw[:, step_buffer(i), P * f:P * f + P],
                                      ident[0:SLOTS, 0:SLOTS])
                mm.then_inc(e_hT, 1)

            def expert_dn(k, i):
                for f in range(2):
                    pe.wait_ge(dn_l, job_piece(STEPS, i, f + 1, k))
                    if f == 0:
                        pe.wait_ge(e_hT_l, k * STEPS + (i + 1))
                    if i % STEPS == 0 and f == 0:
                        pe.wait_ge(e_y_act, k + (i // STEPS + 1))
                        pe.wait_ge(e_y_dve, k + (i // STEPS + 1))
                    for half in range(2):
                        c = slice(512 * half, 512 * half + 512)
                        mm = product(pair[1][0:SLOTS, c], m_hT_hi[:, i % STEPS % 2, f, :], m_hT_lo[:, i % STEPS % 2, f, :],
                                     buffer(dn_hi, f, DM)[:, c], buffer(dn_lo, f, DM)[:, c],
                                     i % STEPS == 0 and f == 0, i % STEPS == STEPS - 1 and f == 1)
                    mm.then_inc(dn_used, 1)

            def iteration(k, i, last=False):
                if i < STEPS or not last:
                    expert_up(k, i)
                if i == 3:
                    scatter(k, 0)
                if i == 5:
                    scatter(k, 1)
                if i == 6:
                    pe.wait_ge(e_pick, k * 2 + 2)
                    for t in range(NT):
                        mm = pe.transpose(bank[7][0:SLOTS, P * t:P * t + P], m_pick[:, t, :], ident)
                    mm.then_inc(e_pickT, 1)
                if i == 8 and not last:
                    pe.wait_ge(e_added, k * NT + 3)
                    gather(k + 1)
                if i >= 1 and (i - 1 < STEPS or not last):
                    hidden_T(k, i - 1)
                if i >= DN_LATE and (i - DN_LATE < STEPS or not last):
                    expert_dn(k, i - DN_LATE)

            def job(k, last=False):
                for i in range(FIRST, STEPS + FIRST):
                    iteration(k, i, last)

            gather(0)
            for i in range(FIRST):
                iteration(0, i)
            with pe.Fori(0, NEXP - 1) as k:
                job(k)
            pe.wait_ge(jobs_known, 1)
            last_job = pe.value_load(n_last_job[0:1, 0:1], min_val=NEXP - 1, max_val=JOBS - 1)
            with pe.If(last_job > NEXP - 1):
                with pe.Fori(NEXP - 1, JOBS - 1) as k:
                    job(k)
            job(last_job, last=True)
            pe.wait_ge(e_added, last_job * NT + (NT + 1))
            scatter(last_job + 1, 0)
            scatter(last_job + 1, 1)

        @block.scalar
        def _(act):
            for r, w in ((NORM_A, a_norm_w), (NORM_F0, ffn_norm_w), (NORM_KV, kv_norm_w.unsqueeze(0))):
                n = KD * w.shape[0]
                act.dma_start(norm_rows[KD * r:KD * r + n, :], w.rearrange("l (k c) -> (l k) c", c=P)).then_inc(rows_in, 16)
            act.dma_start(qk_w[:, 0, :], a_q_norm_w[0].partition_broadcast(P)).then_inc(qkw_in, 16)
            act.dma_start(qk_w[:, 1, :], a_k_norm_w[0].partition_broadcast(P)).then_inc(qkw_in, 16)
            act.dma_start(router[:, :, :], moe_router_w[0].rearrange("(k p) e -> p k e", p=P)).then_inc(router_in, 16)

            def copy(out_, in_, scale=1.0):
                return act.activation(out_, in_, ACT.Copy, scale=scale)

            def up_piece(n):
                if n == 0:
                    act.wait_ge(first_in, 16)
                elif n % 2 == 0 or n == 1:
                    act.wait_ge(up_in[(n // 2) % RING], up_arrived(n // 2))
                if n >= 2:
                    act.wait_ge(up_used, n - 1)
                cols = piece_cols(n)
                copy(buffer(up_hi, n, 4 * cols), raw_piece(n, cols)).then_inc(up_h, 1)

            def dn_piece(n):
                if n % 2 == 0:
                    act.wait_ge(dn_in[(n // 2) % RING], dn_arrived(n // 2))
                if n >= 2:
                    act.wait_ge(dn_used, n - 1)
                copy(buffer(dn_hi, n, DM), ffn_dn((n // 2) % RING)[:, n % 2, :]).then_inc(dn_h, 1)

            def squares(n):
                if n > 0:
                    act.activation(one_out[:, :], ones[0:1, 0:1], ACT.Sqrt)
                for half in range(2):
                    for t in range(NT):
                        if n == 0:
                            act.wait_ge(x_in, 16 * NT)
                        else:
                            act.wait_ge(h_done, 4 * (n - 1) + NT * half + t + 1)
                        c = slice(512 * half, 512 * half + 512)
                        act.activation(u[:, t, c], h[:, t, c], ACT.Square, scale=DM ** -0.5,
                                       accum_out=mean_sq[:, n, t, half:half + 1]).then_inc(sumsq, 1)
                if n > 0:
                    roots(n)

            def roots(n):
                for t in range(NT):
                    act.wait_ge(ms_done, NT * n + t + 1)
                    act.activation(rs[:, n, t:t + 1], rs[:, n, t:t + 1], ACT.Sqrt).then_inc(root_done, 1)

            def uT_part(ready, norm):
                for b in range(4):
                    act.wait_ge(uT_ps, ready + b + 1)
                    for k in (2 * b, 2 * b + 1):
                        c = 256 * (k % 2)
                        e = copy(uT_hi[:, k, :], bank[4 + b][:, c:c + TOK], nw[:, KD * norm + k:KD * norm + k + 1])
                    e.then_inc(uT_h, 1)

            def output_part(n, ps):
                act.wait_ge(o_ps, n + 1)
                copy(uT_hi[:, 4 * (n % 2):4 * (n % 2) + 4, :], pair[ps][:, :].rearrange("p (i t) -> p i t", i=4)).then_inc(o_h, 1)

            squares(0)
            act.wait_ge(nw_done, 1)
            uT_part(0, NORM_A)
            up_piece(0)
            up_piece(1)
            roots(0)

            def proj_copy(j):
                c, cols = IN_COLS[j]
                for t in range(NT):
                    if t == 0:
                        act.wait_ge(proj_ps, j + 1)
                    else:
                        act.wait_ge(up_used, 2 * j + 2)
                    if j == 0:
                        act.wait_ge(rs_done, t + 1)
                    copy(proj(c, cols)[:, t, :], bank[(NT * j + t) % 4][:, 0:cols], rs[:, 0, t:t + 1]).then_inc(proj_sb, 1)

            def heads(g):
                c, n = ((C_K, 2), (0, 4), (512, 4))[g]
                return [(t, i, proj(c, HD * n)[:, t, HD * i:HD * i + HD]) for t in range(NT) for i in range(n)]

            def qk_root_mean(g):
                act.wait_ge(proj_sb, (6, 8, 10)[g])
                for m, (t, i, v) in enumerate(heads(g)):
                    e = act.activation(sq[:, HD * m:HD * m + HD], v, ACT.Square, scale=HD ** -0.5,
                                       accum_out=qk_rs[:, g, t, i:i + 1])
                e.then_inc(qk_ms, 1)
                act.wait_ge(qk_ms, g + 1)
                n = 2 if g == 0 else 4
                act.activation(qk_rs[:, g, :, 0:n], qk_rs[:, g, :, 0:n], ACT.Sqrt, bias=eps).then_inc(qk_root, 1)

            def qk_scale(g):
                act.wait_ge(qk_rstd, g + 1)
                for t, i, v in heads(g):
                    e = copy(v, v, qk_rs[:, g, t, i:i + 1])
                e.then_inc(qk_scaled, 1)

            def relu_scores(n):
                act.wait_ge(idx_qk, n + 1)
                for odd in range(2):
                    ps = bank[(4, 6, 0)[n] + odd]
                    if n == 0:
                        dst, src = rel0[:, odd:8:2, :], ps.rearrange("p (i s) -> p i s", i=4)
                    else:
                        dst, src = rel1[:, 4 * (n - 1) + odd:4 * n:2, :], ps.rearrange("p (i s) -> p i s", i=2)
                    act.activation(dst, src, ACT.Relu, scale=ID ** -0.5).then_inc(rel_done, 1)

            up_piece(2)
            up_piece(3)
            proj_copy(0)
            up_piece(4)
            up_piece(5)
            proj_copy(1)
            up_piece(6)
            up_piece(7)
            proj_copy(2)
            act.wait_ge(idx_T, 1)
            for n in range(2):
                copy(qiT[:, 2 * n:2 * n + 2, :], bank[4 + n].rearrange("p (j t) -> p j t", j=2)).then_inc(idx_T_sb, 1)
            copy(kiT, bank[6][:, 0:TOK]).then_inc(idx_T_sb, 1)
            qk_root_mean(0)
            up_piece(8)
            qk_scale(0)
            relu_scores(0)
            relu_scores(1)
            relu_scores(2)
            up_piece(9)
            proj_copy(3)
            qk_root_mean(1)
            qk_scale(1)
            proj_copy(4)
            qk_root_mean(2)
            act.wait_ge(router_in, 16)
            copy(router_hi[:, :], router[:, :, :].rearrange("p k e -> p (k e)")).then_inc(router_h, 1)
            for n, ps in enumerate((bank[4], bank[5], bank[6], bank[7], bank[0])):
                act.wait_ge(qk_T, n + 1)
                dst = kT_a[:, :, :] if n == 0 else q_T[:, 2 * (n - 1):2 * n, :]
                copy(dst, ps.rearrange("p (i t) -> p i t", i=2)).then_inc(qk_T_sb, 1)
            up_piece(10)
            up_piece(11)
            for g in range(3):
                act.wait_ge(rowmax_done, g + 1)
                for i in range(8 if g == 0 else 4):
                    r = i if g == 0 else 8 + 4 * (g - 1) + i
                    row = prob0[:, i, :] if g == 0 else prob1[:, 4 * (g - 1) + i, :]
                    e = act.activation(row, row, ACT.Exp, bias=soft[:, 0, r:r + 1], accum_out=soft[:, 1, r:r + 1])
                e.then_inc(exp_done, 1)
            for g in range(3):
                act.wait_ge(probT_ps, g + 1)
                if g == 0:
                    copy(probT[:, :, 0:P], pair[0][:, :].rearrange("p (i s) -> p i s", i=8)).then_inc(probT_sb, 1)
                else:
                    copy(probT[:, 4 * (g - 1):4 * g, P:], pair[g][:, :].rearrange("p (i s) -> p i s", i=4)).then_inc(probT_sb, 1)
            output_part(0, 3)
            output_part(1, 0)
            up_piece(12)
            up_piece(13)

            squares(1)
            up_piece(14)
            uT_part(4, NORM_F0)
            up_piece(15)
            for i in range(STEPS):
                if i + 1 < STEPS:
                    for p in range(2):
                        up_piece(2 * (T_DENSE + i + 1) + p)
                act.wait_ge(up_used, 2 * (T_DENSE + i + 1))
                if i >= 2:
                    act.wait_ge(hid_raw, i - 1)
                gate = pair[i % 2][:, :].rearrange("p (f c) -> p f c", f=2)[:, :, 0:TOK]
                act.activation(d_silu[:, i % 2], gate, ACT.Silu).then_inc(silu_done, 1)
                dn_piece(2 * i)
                act.wait_ge(hid_raw, i + 1)
                if i >= 1:
                    act.wait_ge(dn_used, 2 * i)
                copy(d_hi[:, :, :], d_raw[:, i % 2]).then_inc(hid_h, 1)
                dn_piece(2 * i + 1)

            squares(2)
            n = 2 * T_BQ
            up_piece(n)
            uT_part(8, NORM_B)
            for m in range(1, 5):
                up_piece(n + m)
            act.wait_ge(up_used, 2 * T_BK)
            act.wait_ge(uT_l, 12)
            uT_part(8, NORM_KV)
            up_piece(n + 5)
            up_piece(n + 6)
            up_piece(n + 7)
            for j in range(2):
                act.wait_ge(up_used, 2 * (T_BK + j + 1))
                copy(kT_b[:, 4 * j:4 * j + 4, :], pair[2 + j][:, :].rearrange("p (i t) -> p i t", i=4)).then_inc(bk_sb, 1)
                up_piece(n + 8 + j)

            def both_banks(ps):
                return ps[:, :].rearrange("p (h c) -> p h c", h=2)[:, :, 0:384]

            def log1p_exp(j):
                act.wait_ge(z_ps, j + 1)
                if j >= 2:
                    act.wait_ge(stick_raw, j - 1)
                b = absz[j % 2]
                act.activation(b, both_banks(pair[j % 2]), ACT.Abs, scale=SCALE).then_inc(z_log, 1)
                act.wait_ge(z_log, 3 * j + 1)
                act.activation(b, b, ACT.Exp, scale=-1.0).then_inc(z_log, 1)
                act.wait_ge(z_log, 3 * j + 2)
                act.activation(b, b, ACT.Ln, bias=1.0).then_inc(z_log, 1)

            def stick_weights(j):
                act.wait_ge(expo_done, j + 1)
                act.activation(att[:, 2 * j:2 * j + 2, :], neg[j % 2], ACT.Exp).then_inc(stick_raw, 1)

            def values_copy(half):
                for t in range(NT):
                    if t == 0:
                        act.wait_ge(v_ps, half + 1)
                    else:
                        act.wait_ge(up_used, 2 * (T_BV + half + 1))
                    copy(v_b[:, t, 512 * half:512 * half + 512], bank[6 + t]).then_inc(v_sb, 1)

            log1p_exp(0)
            log1p_exp(1)
            up_piece(n + 10)
            up_piece(n + 11)
            values_copy(0)
            stick_weights(0)
            log1p_exp(2)
            stick_weights(1)
            log1p_exp(3)
            stick_weights(2)
            values_copy(1)
            up_piece(n + 12)
            stick_weights(3)
            output_part(2, 0)
            output_part(3, 1)
            up_piece(n + 13)
            up_piece(2 * T_BO + 2)
            up_piece(2 * T_BO + 3)

            def up_half(k, i, p):
                if p == 0:
                    act.wait_ge(up_in[(T_MOE + i % STEPS) % RING], job_up_arrived(i % STEPS, k + i // STEPS))
                act.wait_ge(up_used, job_piece(T_MOE, i, p - 1, k))
                copy(buffer(up_hi, p, 2048), raw_piece(2 * (T_MOE + i % STEPS) + p)).then_inc(up_h, 1)

            uT_part(12, NORM_F1)
            squares(3)
            act.wait_ge(routeT_ps, 1)
            copy(route_T, bank[0][0:NEXP, 0:TOK]).then_inc(routeT_sb, 1)
            up_half(0, 0, 0)
            up_half(0, 0, 1)
            act.wait_ge(route_top, 1)
            for t in range(NT):
                e = act.activation(rt[:, 6, t, :], rt[:, 0, t, :], ACT.Exp, bias=rt[:, 9, t, 2:3])
            e.then_inc(route_exp, 1)

            def gathered(k):
                act.wait_ge(e_u, k + 1)
                act.wait_ge(up_used, job_piece(T_MOE, 0, 0, k))
                copy(m_u_hi, m_u).then_inc(e_u_h, 1)

            def dn_step(k, i):
                for p in range(2):
                    if p == 0:
                        act.wait_ge(dn_in[(STEPS + i % STEPS) % RING], job_dn_arrived(i % STEPS, k + i // STEPS))
                    act.wait_ge(dn_used, job_piece(STEPS, i, p - 1, k))
                    copy(buffer(dn_hi, p, DM), ffn_dn((STEPS + i % STEPS) % RING)[:, p, :]).then_inc(dn_h, 1)

            def silu_step(k, i):
                b = step_buffer(i)
                act.wait_ge(up_used, job_piece(T_MOE, i, 2, k))
                if i >= 2 and b < 2:
                    act.wait_ge(e_raw, k * STEPS + (last_step_in_buffer(i) + 1))
                act.activation(m_silu[:, b], bank[step_bank[b]][0:SLOTS, 0:FSTEP], ACT.Silu).then_inc(e_silu, 1)

            def hidden_step(k, i):
                act.wait_ge(e_hT, k * STEPS + (i + 1))
                if i >= 2:
                    act.wait_ge(dn_used, job_piece(STEPS, i - (1 if i == STEPS else 2), 2, k))
                copy(m_hT_hi[:, i % STEPS % 2], bank[6][:, 0:2 * SLOTS].rearrange("p (f c) -> p f c", f=2)).then_inc(e_hT_h, 1)

            def result(k):
                act.wait_ge(dn_used, job_piece(STEPS, STEPS, 0, k))
                act.wait_ge(e_scatter, k * NT + 3)
                copy(m_y[:, 0:512], bank[2][0:SLOTS, :]).then_inc(e_y_act, 1)

            def iteration(k, i, last=False):
                for p in range(2):
                    if i < STEPS or not last:
                        up_half(k, i, p)
                    if i == STEPS and p == 0 and not last:
                        gathered(k + 1)
                if i == STEPS + 2:
                    result(k)
                if i >= 1 and (i - 1 < STEPS or not last):
                    silu_step(k, i - 1)
                if i >= DN_LATE and (i - DN_LATE < STEPS or not last):
                    hidden_step(k, i - DN_LATE)
                    dn_step(k, i - DN_LATE)
                if i == 7:
                    act.wait_ge(e_pickT, k + 1)
                    act.wait_ge(e_scatter, k * NT + 3)
                    copy(m_pickT, bank[7][0:SLOTS, 0:TOK]).then_inc(e_pickT_sb, 1)

            def job(k, last=False):
                act.activation(one_out[:, :], ones[0:1, 0:1], ACT.Silu)
                for i in range(FIRST, STEPS + FIRST):
                    iteration(k, i, last)

            gathered(0)
            for i in range(1, FIRST):
                iteration(0, i)
            with act.Fori(0, NEXP - 1) as k:
                job(k)
            act.wait_ge(jobs_known, 1)
            last_job = act.value_load(n_last_job[0:1, 0:1], min_val=NEXP - 1, max_val=JOBS - 1)
            with act.If(last_job > NEXP - 1):
                with act.Fori(NEXP - 1, JOBS - 1) as k:
                    job(k)
            job(last_job, last=True)

        @block.gpsimd
        def _(pool):
            mask = before.unsqueeze(1).unsqueeze(1).to_broadcast([P, 2, 2, P])

            def diagonal(v):
                return v.rearrange("p h (b c) -> p h b c", b=3)[:, :, 0:3:2, :]

            def mask_keep(j):
                pool.wait_ge(keep_raw, j + 1)
                pool.tensor_tensor(diagonal(lk[j % 2]), diagonal(lk[j % 2]), mask, ALU.mult).then_inc(keep_done, 1)

            def mask_stick(j):
                pool.wait_ge(stick_raw, j + 1)
                v = diagonal(att[:, 2 * j:2 * j + 2, :])
                pool.tensor_tensor(v, v, mask, ALU.mult).then_inc(stick_done, 1)

            pool.wait_ge(consts_in, 16)
            mask_keep(0)
            mask_keep(1)
            mask_stick(0)
            mask_keep(2)
            mask_stick(1)
            mask_keep(3)
            mask_stick(2)
            mask_stick(3)

        @block.vector
        def _(dve):
            marks = [0]

            def mark(ins):
                marks[0] += 1
                ins.then_inc(dve_chain, 1)
                return marks[0]

            def reads(n):
                dve.wait_ge(dve_chain, n)

            def rstd(n, t):
                dve.wait_ge(sumsq, 4 * n + NT + t + 1)
                dve.scalar_tensor_tensor(rs[:, n, t:t + 1], mean_sq[:, n, t, 0:1], EPS, mean_sq[:, n, t, 1:2], ALU.add, ALU.add)\
                   .then_inc(ms_done, 1)
                dve.wait_ge(root_done, NT * n + t + 1)
                return dve.reciprocal(rs[:, n, t:t + 1], rs[:, n, t:t + 1])

            def normalise(n):
                for t in range(NT):
                    reads(mark(rstd(n, t)))
                    dve.tensor_scalar(u[:, t, :], h[:, t, :], rs[:, n, t:t + 1], None, ALU.mult).then_inc(u_done, 1)

            def up_piece(n):
                cols = piece_cols(n)
                dve.wait_ge(up_h, n + 1)
                dve.tensor_tensor(buffer(up_lo, n, 4 * cols), raw_piece(n, cols), buffer(up_hi, n, 4 * cols).bitcast(f32),
                                  ALU.subtract).then_inc(up_l, 1)

            def dn_piece(n):
                dve.wait_ge(dn_h, n + 1)
                dve.tensor_tensor(buffer(dn_lo, n, DM), ffn_dn((n // 2) % RING)[:, n % 2, :],
                                  buffer(dn_hi, n, DM).bitcast(f32), ALU.subtract).then_inc(dn_l, 1)

            def uT_part(m, norm):
                for b in range(4):
                    dve.wait_ge(uT_h, 4 * m + b + 1)
                    for k in (2 * b, 2 * b + 1):
                        c = 256 * (k % 2)
                        last = dve.scalar_tensor_tensor(uT_lo[:, k, :], bank[4 + b][:, c:c + TOK],
                                                        nw[:, KD * norm + k:KD * norm + k + 1],
                                                        uT_hi[:, k, :].bitcast(f32), ALU.mult, ALU.subtract)
                    last.then_inc(uT_l, 1)

            def output_part(n, ps):
                dve.wait_ge(o_h, n + 1)
                c = slice(4 * (n % 2), 4 * (n % 2) + 4)
                dve.tensor_tensor(uT_lo[:, c, :], pair[ps][:, :].rearrange("p (i t) -> p i t", i=4),
                                  uT_hi[:, c, :].bitcast(f32), ALU.subtract).then_inc(o_l, 1)

            def add_residual(first_bank, tile0, res0):
                for half in range(2):
                    for t in range(NT):
                        if t == 0:
                            dve.wait_ge(res_ps, res0 + half + 1)
                        else:
                            dve.wait_ge(up_used, 2 * (tile0 + half + 1))
                        c = slice(512 * half, 512 * half + 512)
                        dve.tensor_tensor(h[:, t, c], h[:, t, c], bank[first_bank + 2 * t + half], ALU.add).then_inc(h_done, 1)

            def rope(v, half, step):
                n = v.shape[2]
                shape = [P, NT, n, half]
                c = cos[:, :, 0:16:step].unsqueeze(2).to_broadcast(shape)
                s = sin[:, :, 0:16:step].unsqueeze(2).to_broadcast(shape)
                tmp = rope_tmp
                t1, t2, t3, t4 = (tmp[:, 256 * j:256 * j + NT * n * half].rearrange("p (t n f) -> p t n f", t=NT, n=n)
                                  for j in range(4))
                x1, x2 = v[:, :, :, 0:half], v[:, :, :, half:2 * half]
                dve.tensor_tensor(t1, x1, c, ALU.mult)
                dve.tensor_tensor(t2, x2, s, ALU.mult)
                dve.tensor_tensor(t3, x2, c, ALU.mult)
                reads(mark(dve.tensor_tensor(t4, x1, s, ALU.mult)))
                dve.tensor_tensor(x1, t1, t2, ALU.subtract)
                return dve.tensor_tensor(x2, t3, t4, ALU.add)

            dve.wait_ge(nw_ps, 1)
            dve.tensor_copy(nw[:, :], bank[0][:, 0:5 * KD]).then_inc(nw_done, 1)
            dve.wait_ge(nw_done, 1)
            uT_part(0, NORM_A)
            up_piece(0)
            up_piece(1)
            for t in range(NT):
                rstd(0, t).then_inc(rs_done, 1)
            for n in range(2, 6):
                up_piece(n)

            dve.wait_ge(proj_sb, 4)
            reads(mark(rope(proj(C_QI, C_WI - C_QI).rearrange("p t (n d) -> p t n d", d=ID), ID // 8, 2)))
            for t in range(NT):
                dve.tensor_copy(ki2[:, t, :].rearrange("p (r d) -> p r d", r=2),
                                proj(C_KI, ID)[:, t, :].unsqueeze(1).to_broadcast([P, 2, ID]))
            dve.tensor_scalar(w_idx[:, :, :], proj(C_WI, IH), IH ** -0.5, None, ALU.mult).then_inc(idx_roped, 1)
            up_piece(6)
            up_piece(7)

            def qk_reciprocal(g):
                dve.wait_ge(qk_root, g + 1)
                v = qk_rs[:, g, :, 0:(2 if g == 0 else 4)]
                dve.reciprocal(v, v).then_inc(qk_rstd, 1)

            def qk_rotate(g):
                c, n = ((C_K, 2), (0, 4), (512, 4))[g]
                v = proj(c, HD * n).rearrange("p t (n d) -> p t n d", d=HD)
                if g < 2:
                    w = qk_w[:, int(g == 0), :].unsqueeze(1).unsqueeze(1).to_broadcast([P, NT, n, HD])
                    dve.wait_ge(qk_scaled, g + 1)
                    last = dve.tensor_tensor(v, v, w, ALU.mult)
                else:
                    dve.wait_ge(qk_rstd, g + 1)
                    for t in range(NT):
                        for i in range(n):
                            last = dve.scalar_tensor_tensor(v[:, t, i, :], v[:, t, i, :], qk_rs[:, g, t, i:i + 1],
                                                            qk_w[:, 0, :], ALU.mult, ALU.mult)
                reads(mark(last))
                rope(v, HD // 8, 1).then_inc(qk_roped, 1)

            dve.wait_ge(qkw_in, 32)
            qk_reciprocal(0)
            up_piece(8)
            qk_rotate(0)

            dve.wait_ge(idx_roped, 1)
            dve.wait_ge(rel_done, 6)
            rel = (rel0, rel1)
            masks = (imask[:, P:2 * P], imask)
            done = [0, 0]
            for i in range(IH):
                for t in range(NT):
                    if i:
                        reads(done[t])
                    done[t] = mark(dve.scalar_tensor_tensor(score[t], rel[t][:, i, :], w_idx[:, t, i:i + 1],
                                                            masks[t] if i == 0 else score[t], ALU.mult, ALU.add))
            up_piece(9)
            for n in range(TOPK // 8):
                if n == 5:
                    qk_reciprocal(1)
                for t in range(NT):
                    reads(done[t])
                    done[t] = mark(dve.max(top8[:, t, :], score[t]))
                for t in range(NT):
                    reads(done[t])
                    done[t] = mark(dve.match_replace(score[t], top8[:, t, :], score[t], TAKEN))
            for t in range(NT):
                reads(done[t])
                done[t] = mark(dve.tensor_scalar(bias[t], score[t], 0.5 * (TAKEN + NOT_CAUSAL), MASKED, ALU.is_ge, ALU.mult))
            for t in range(NT):
                reads(done[t])
                own = bias[t][:, P * t:P * t + P]
                done[t] = mark(dve.tensor_tensor(own, own, imask[:, P:2 * P], ALU.add))
            qk_rotate(1)
            qk_reciprocal(2)
            qk_rotate(2)
            up_piece(10)
            up_piece(11)
            dve.wait_ge(router_h, 1)
            dve.tensor_tensor(router_lo[:, :], router[:, :, :].rearrange("p k e -> p (k e)"),
                              router_hi[:, :].bitcast(f32), ALU.subtract).then_inc(router_l, 1)

            def group(g):
                return (prob0, 0, 8, 0) if g == 0 else (prob1[:, 4 * (g - 1):4 * g, :], 4 + 4 * g, 4, 1)

            for g in range(3):
                prob, r, n, t = group(g)
                dve.wait_ge(logits_ps, g + 1)
                reads(done[t])
                for b in range(2):
                    part = prob[:, b * n // 2:(b + 1) * n // 2, :]
                    last = dve.scalar_tensor_tensor(part, bank[2 * (g + 1) + b].rearrange("p (i s) -> p i s", i=n // 2), SCALE,
                                                    bias[t].unsqueeze(1).to_broadcast([P, n // 2, P * (t + 1)]),
                                                    ALU.mult, ALU.add)
                reads(mark(last))
                dve.tensor_reduce(soft[:, 0, r:r + n], prob, AX.X, ALU.max, negate=True).then_inc(rowmax_done, 1)
            for g in range(3):
                prob, r, n, t = group(g)
                dve.wait_ge(exp_done, g + 1)
                reads(mark(dve.reciprocal(soft[:, 2, r:r + n], soft[:, 1, r:r + n])))
                dve.tensor_tensor(prob, prob, soft[:, 2, r:r + n].unsqueeze(2).to_broadcast([P, n, P * (t + 1)]),
                                  ALU.mult).then_inc(prob_done, 1)
            output_part(0, 3)
            output_part(1, 0)
            up_piece(12)
            up_piece(13)
            add_residual(2, T_OUT, 0)

            dve.wait_ge(h_done, 4)
            normalise(1)
            up_piece(14)
            uT_part(1, NORM_F0)
            up_piece(15)
            for i in range(STEPS):
                if i + 1 < STEPS:
                    for p in range(2):
                        up_piece(2 * (T_DENSE + i + 1) + p)
                dve.wait_ge(silu_done, i + 1)
                if i >= 2:
                    dve.wait_ge(hid_h, i - 1)
                up = pair[i % 2][:, :].rearrange("p (f c) -> p f c", f=2)[:, :, TOK:2 * TOK]
                dve.tensor_tensor(d_raw[:, i % 2], d_silu[:, i % 2], up, ALU.mult).then_inc(hid_raw, 1)
                dn_piece(2 * i)
                dve.wait_ge(hid_raw, i + 1)
                dve.wait_ge(hid_h, i + 1)
                dve.tensor_tensor(d_lo, d_raw[:, i % 2], d_hi.bitcast(f32), ALU.subtract).then_inc(hid_l, 1)
                dn_piece(2 * i + 1)
            dve.wait_ge(dn_used, 2 * STEPS)
            for half in range(2):
                for t in range(NT):
                    c = slice(512 * half, 512 * half + 512)
                    dve.tensor_tensor(h[:, t, c], h[:, t, c], bank[4 + 2 * t + half], ALU.add).then_inc(h_done, 1)

            dve.wait_ge(h_done, 8)
            normalise(2)
            n = 2 * T_BQ
            up_piece(n)
            uT_part(2, NORM_B)
            for m in range(1, 5):
                up_piece(n + m)
            uT_part(3, NORM_KV)
            up_piece(n + 5)
            for j in range(2):
                dve.wait_ge(up_used, 2 * (T_BQ + j + 1))
                dve.tensor_copy(q_T[:, 4 * j:4 * j + 4, :], pair[j][:, :].rearrange("p (i t) -> p i t", i=4)).then_inc(bq_sb, 1)
            for m in range(6, 10):
                up_piece(n + m)

            def both_banks(ps):
                return ps[:, :].rearrange("p (h c) -> p h c", h=2)[:, :, 0:384]

            def log_keep(j):
                z, b = both_banks(pair[j % 2]), j % 2
                dve.wait_ge(z_ps, j + 1)
                dve.wait_ge(z_log, 3 * j + 3)
                reads(mark(dve.tensor_scalar(lb[b], z, SCALE, 0.0, ALU.mult, ALU.min)))
                reads(mark(dve.tensor_tensor(lb[b], lb[b], absz[b], ALU.subtract)))
                if j >= 2:
                    dve.wait_ge(after_ps, j - 1)
                dve.scalar_tensor_tensor(lk[b], z, -SCALE, lb[b], ALU.mult, ALU.add).then_inc(keep_raw, 1)

            def exponent(j):
                dve.wait_ge(after_ps, j + 1)
                dve.tensor_tensor(neg[j % 2], both_banks(pair[2]), lb[j % 2], ALU.add).then_inc(expo_done, 1)

            log_keep(0)
            log_keep(1)
            up_piece(n + 10)
            up_piece(n + 11)
            exponent(0)
            log_keep(2)
            exponent(1)
            exponent(2)
            log_keep(3)
            exponent(3)
            up_piece(n + 12)
            output_part(2, 0)
            output_part(3, 1)
            up_piece(n + 13)
            up_piece(2 * T_BO + 2)
            up_piece(2 * T_BO + 3)
            add_residual(0, T_BO, 2)

            def up_half(k, i, p):
                dve.wait_ge(up_h, job_piece(T_MOE, i, p + 1, k))
                dve.tensor_tensor(buffer(up_lo, p, 2048), raw_piece(2 * (T_MOE + i % STEPS) + p),
                                  buffer(up_hi, p, 2048).bitcast(f32), ALU.subtract).then_inc(up_l, 1)

            dve.memset(m_y[:, 0:512], 0.0).then_inc(e_y_act, 1)
            dve.memset(m_y[:, 512:1024], 0.0).then_inc(e_y_dve, 1)
            dve.memset(m_pickT, 0.0).then_inc(e_pickT_sb, 1)
            dve.memset(slot_of[:, :, JOBS:JOBS + 1], NO_SLOT).then_inc(e_scatter, 1)
            dve.memset(gate_of[:, :, 0:1], 0.0).then_inc(e_added, 1)
            uT_part(4, NORM_F1)
            lg, gt, eq, rank, fits, routed, ex, gate = (rt[:, j] for j in range(8))
            misc = rt[:, 9]
            wide = [P, NT, NEXP]
            for t in range(NT):
                last = rstd(3, t)
            reads(mark(last))
            for t in range(NT):
                dve.tensor_scalar(u[:, t, :], h[:, t, :], rs[:, 3, t:t + 1], None, ALU.mult)
            dve.wait_ge(route_ps, 1)
            for t in range(NT):
                last = dve.tensor_scalar(lg[:, t, :], bank[1][:, NEXP * t:NEXP * t + NEXP], rs[:, 3, t:t + 1], None, ALU.mult)
            reads(mark(last))
            for t in range(NT):
                last = dve.max(top8[:, t, :], lg[:, t, :])
            reads(mark(last))
            first, second = top8[:, :, 0:1], top8[:, :, 1:2]
            dve.tensor_scalar(misc[:, :, 2:3], first, -1.0, None, ALU.mult).then_inc(route_top, 1)
            dve.tensor_tensor(misc[:, :, 0:1], first, second, ALU.is_gt)
            dve.tensor_tensor(gt, lg, second.to_broadcast(wide), ALU.is_gt)
            reads(mark(dve.tensor_tensor(eq, lg, second.to_broadcast(wide), ALU.is_equal)))
            for t in range(NT):
                dve.tensor_tensor_scan(rank[:, t, :], ones[:, 0:NEXP], eq[:, t, :], 0.0, ALU.mult, ALU.add)
            reads(mark(dve.tensor_scalar(misc[:, :, 1:2], misc[:, :, 0:1], -1.0, 2.0, ALU.mult, ALU.add)))
            reads(mark(dve.tensor_tensor(fits, rank, misc[:, :, 1:2].to_broadcast(wide), ALU.is_le)))
            reads(mark(dve.tensor_tensor(fits, fits, eq, ALU.mult)))
            dve.tensor_tensor(routed, fits, gt, ALU.add).then_inc(sel_done, 1)
            dve.wait_ge(sel_done, 1)
            dve.wait_ge(route_exp, 1)
            reads(mark(dve.tensor_tensor(ex, ex, routed, ALU.mult)))
            reads(mark(dve.tensor_reduce(misc[:, :, 3:4], ex, AX.X, ALU.add)))
            reads(mark(dve.reciprocal(misc[:, :, 4:5], misc[:, :, 3:4])))
            reads(mark(dve.tensor_tensor(gate, ex, misc[:, :, 4:5].to_broadcast(wide), ALU.mult)))
            dve.wait_ge(rank_ps, 1)
            ranks = bank[0][:, 0:NT * NEXP].rearrange("p (t e) -> p t e", t=NT)
            reads(mark(dve.tensor_scalar(rank, ranks, -NO_SLOT, None, ALU.add)))
            reads(mark(dve.tensor_tensor(rank, rank, routed, ALU.mult)))
            def pick(j):
                for t in range(NT):
                    last = dve.tensor_scalar(m_pick[:, t, :], slot_no, slot_of[:, t, bass.ds(j, 1)], None, ALU.is_equal)
                last.then_inc(e_pick, 1)

            slots = [dve.tensor_scalar(slot_of[:, :, NEXP * c:NEXP * (c + 1)], rank, NO_SLOT - SLOTS * c, None, ALU.add)
                     for c in range(CHUNKS)]
            reads(mark(slots[-1]))
            pick(0)
            for c in range(CHUNKS):
                dve.tensor_copy(gate_of[:, :, 1 + NEXP * c:1 + NEXP * (c + 1)], gate)
            reads(mark(dve.tensor_reduce(misc[:, 0, 5:6], bank[0][:, 2 * NEXP:3 * NEXP], AX.X, ALU.max)))
            reads(mark(dve.tensor_scalar(misc[:, 0, 6:7], misc[:, 0, 5:6], float(SLOTS), float(JOBS - NEXP),
                                         ALU.is_gt, ALU.mult)))
            dve.tensor_scalar(n_last_job[:, :], misc[:, 0, 6:7], float(NEXP - 1), None, ALU.add).then_inc(jobs_known, 1)

            def gathered(k):
                dve.wait_ge(e_gather, k + 1)
                w = nw[:, KD * NORM_F1:KD * (NORM_F1 + 1)].rearrange("p (b j) -> p b j", b=2).unsqueeze(3)\
                    .to_broadcast([P, 2, 4, SLOTS])
                src = pair[2][:, :].rearrange("p (b c) -> p b c", b=2)[:, :, 0:4 * SLOTS].rearrange("p b (j c) -> p b j c", j=4)
                dve.tensor_tensor(m_u.rearrange("p (b j c) -> p b j c", b=2, j=4), src, w, ALU.mult).then_inc(e_u, 1)

            def gathered_lo(k):
                dve.wait_ge(e_u, k + 1)
                dve.wait_ge(e_u_h, k + 1)
                dve.tensor_tensor(m_u_lo, m_u, m_u_hi.bitcast(f32), ALU.subtract).then_inc(e_u_l, 1)

            def add_scattered(k, t):
                dve.wait_ge(e_scatter, k * NT + (t + 2))
                dve.wait_ge(e_added, k * NT + (t + 1))
                dve.scalar_tensor_tensor(h[:, t, :], pair[2][:, :], gate_of[:, t, bass.ds(k, 1)], h[:, t, :],
                                         ALU.mult, ALU.add).then_inc(e_added, 1)

            def dn_step(k, i):
                for p in range(2):
                    dve.wait_ge(dn_h, job_piece(STEPS, i, p + 1, k))
                    dve.tensor_tensor(buffer(dn_lo, p, DM), ffn_dn((STEPS + i % STEPS) % RING)[:, p, :],
                                      buffer(dn_hi, p, DM).bitcast(f32), ALU.subtract).then_inc(dn_l, 1)

            def hidden_step(k, i):
                b = step_buffer(i)
                dve.wait_ge(e_silu, k * STEPS + (i + 1))
                dve.tensor_tensor(m_raw[:, b], m_silu[:, b], bank[step_bank[b]][0:SLOTS, FSTEP:2 * FSTEP], ALU.mult)\
                   .then_inc(e_raw, 1)

            def hidden_lo(k, i):
                dve.wait_ge(e_hT_h, k * STEPS + (i + 1))
                dve.tensor_tensor(m_hT_lo[:, i % STEPS % 2], bank[6][:, 0:2 * SLOTS].rearrange("p (f c) -> p f c", f=2),
                                  m_hT_hi[:, i % STEPS % 2].bitcast(f32), ALU.subtract).then_inc(e_hT_l, 1)

            def result(k):
                dve.wait_ge(dn_used, job_piece(STEPS, STEPS, 0, k))
                dve.wait_ge(e_scatter, k * NT + 3)
                dve.tensor_copy(m_y[:, 512:1024], bank[3][0:SLOTS, :]).then_inc(e_y_dve, 1)

            def iteration(k, i, last=False):
                for p in range(2):
                    if i < STEPS or not last:
                        up_half(k, i, p)
                    if i == STEPS and p == 0 and not last:
                        gathered_lo(k + 1)
                if i == STEPS + 2:
                    result(k)
                if i >= 1 and (i - 1 < STEPS or not last):
                    hidden_step(k, i - 1)
                if i >= DN_LATE and (i - DN_LATE < STEPS or not last):
                    hidden_lo(k, i - DN_LATE)
                    dn_step(k, i - DN_LATE)
                if i == 4:
                    add_scattered(k, 0)
                if i == 5:
                    dve.wait_ge(e_gather, k + 1)
                    pick(k)
                if i == 6:
                    add_scattered(k, 1)
                if i == 7 and not last:
                    dve.wait_ge(e_pickT, k + 1)
                    pick(k + 1)
                if i == 9 and not last:
                    gathered(k + 1)

            def job(k, last=False):
                for i in range(FIRST, STEPS + FIRST):
                    iteration(k, i, last)

            dve.wait_ge(jobs_known, 1)
            up_half(0, 0, 0)
            up_half(0, 0, 1)
            gathered(0)
            gathered_lo(0)
            for i in range(1, FIRST):
                iteration(0, i)
            with dve.Fori(0, NEXP - 1) as k:
                job(k)
            last_job = dve.value_load(n_last_job[0:1, 0:1], min_val=NEXP - 1, max_val=JOBS - 1)
            with dve.If(last_job > NEXP - 1):
                with dve.Fori(NEXP - 1, JOBS - 1) as k:
                    job(k)
            job(last_job, last=True)
            add_scattered(last_job + 1, 0)
            add_scattered(last_job + 1, 1)


def shape_constants():
    import numpy as np
    c = np.zeros((P, K_END), np.float32)
    r = np.arange(P)
    c[:, K_ID:K_ID + P] = np.eye(P)
    c[:, K_BEFORE:K_BEFORE + P] = r[:, None] < r[None, :]
    c[:, K_AFTER:K_AFTER + P] = r[:, None] > r[None, :]
    c[:, K_ONES:K_ONES + P] = 1.0
    c[:, K_IMASK + P:K_IMASK + 2 * P] = np.where(r[None, :] > r[:, None], np.float32(NOT_CAUSAL), np.float32(0))
    c[:, K_EPS] = EPS
    c[:, K_SLOT:K_SLOT + SLOTS] = np.arange(SLOTS)
    inv = np.float32(500000.0) ** (-np.arange(16, dtype=np.float32) * np.float32(2.0) / np.float32(32))
    angle = np.arange(TOK, dtype=np.float32)[:, None] * inv.astype(np.float32)[None, :]
    for k, fn in ((K_COS, np.cos), (K_SIN, np.sin)):
        c[:, k:k + 32] = fn(angle).reshape(NT, P, 16).transpose(1, 0, 2).reshape(P, 32)
    return c


_INS = ["x", "a_norm_w", "a_w_in", "a_q_norm_w", "a_k_norm_w", "a_w_out", "kv_norm_w", "kv_w", "b_norm_w",
        "b_w_q", "b_w_out", "ffn_norm_w", "dense_w_gate_up", "dense_w_down", "moe_router_w",
        "moe_w_gate_up", "moe_w_down"]


def kernel(**inputs):
    import numpy as np
    import concourse.bacc as bacc
    from concourse.bass_utils import run_bass_kernel_spmd

    nc = bacc.Bacc("TRN2", target_bir_lowering=False, num_devices=1)
    arrays = {f"in_{name}": np.ascontiguousarray(inputs[name]) for name in _INS}
    arrays["in_consts"] = shape_constants()
    args = [nc.dram_tensor(name, a.shape, mybir.dt.from_np(a.dtype), kind="ExternalInput").ap()
            for name, a in arrays.items()]
    args.append(nc.dram_tensor("out_0", (1, TOK, DM), mybir.dt.float32, kind="ExternalOutput").ap())
    program(nc, *args)
    return run_bass_kernel_spmd(nc, [arrays], core_ids=[0]).results[0]["out_0"]
```
